# Optimizing a Trainium2 kernel written in Bass

```python
import math
import jax, jax.numpy as jnp
from jax import lax
import numpy as np

D_MODEL = 1024
BATCH = 1
SEQ = 256
DEPTH = 1

D_MIX = D_MODEL
HEAD_DIM = 64
SB_HEADS = 8
SB_WIDTH = SB_HEADS * HEAD_DIM
SG_HEADS = 8
SG_WIDTH = SG_HEADS * HEAD_DIM
D_IN = 3 * SB_WIDTH + 2 * SG_WIDTH
CHUNK = 128
Q_BLOCK = 128
N_GROUPS = 4
EXPERTS_PER_GROUP = 8
TOP_K = 2
D_EXPERT = 512
EPS = 1e-6


def rmsnorm(x, g):
    xf = x.astype(jnp.float32)
    y = xf * lax.rsqrt(jnp.mean(xf * xf, axis=-1, keepdims=True) + EPS)
    return (y * g.astype(jnp.float32)).astype(x.dtype)

def stick_breaking_attention(q, k, v):
    B, S, H, Dh = q.shape
    nb = S // Q_BLOCK
    scale = 1.0 / math.sqrt(Dh)
    k = k.transpose(0, 2, 1, 3)
    v = v.transpose(0, 2, 1, 3)
    q_blocks = q.transpose(0, 2, 1, 3).reshape(B, H, nb, Q_BLOCK, Dh).transpose(2, 0, 1, 3, 4)
    key_pos = jnp.arange(S)

    def one_block(args):
        qb, blk = args
        z = jnp.einsum('bhqd,bhkd->bhqk', qb, k).astype(jnp.float32) * scale
        q_pos = blk * Q_BLOCK + jnp.arange(Q_BLOCK)
        mask = key_pos[None, :] < q_pos[:, None]
        log_beta = jax.nn.log_sigmoid(z)
        log_1m_beta = jnp.where(mask, jax.nn.log_sigmoid(-z), 0.0)
        after = lax.cumsum(log_1m_beta, axis=log_1m_beta.ndim - 1, reverse=True) - log_1m_beta
        a = jnp.where(mask, jnp.exp(log_beta + after), 0.0)
        return jnp.einsum('bhqk,bhkd->bhqd', a.astype(v.dtype), v)

    out = lax.map(one_block, (q_blocks, jnp.arange(nb)))
    return out.transpose(1, 0, 3, 2, 4).reshape(B, S, H * Dh)

def chunked_spatial_gating(u, vg, sg_norm_g, w_spatial, b_spatial):
    B, S, _ = u.shape
    nc = S // CHUNK
    u = jax.nn.gelu(u)
    vg = rmsnorm(jax.nn.gelu(vg), sg_norm_g)
    vg = vg.reshape(B, nc, CHUNK, SG_HEADS, HEAD_DIM)
    causal = jnp.tril(jnp.ones((CHUNK, CHUNK), dtype=w_spatial.dtype))
    w_masked = w_spatial * causal[None]
    mixed = jnp.einsum('hts,bcshd->bcthd', w_masked, vg) + b_spatial.T[None, None, :, :, None]
    return u * mixed.reshape(B, S, SG_WIDTH)

def hierarchical_moe(x, w_router_group, b_router_group, w_router_expert, b_router_expert,
                     w_gate, w_up, w_down):
    B, S, D = x.shape
    xt = x.reshape(-1, D)
    n = xt.shape[0]
    g_logits = (xt @ w_router_group).astype(jnp.float32) + b_router_group.astype(jnp.float32)
    g_probs = jax.nn.softmax(g_logits, axis=-1)
    g_idx = jnp.argmax(g_logits, axis=-1)
    g_onehot = jax.nn.one_hot(g_idx, N_GROUPS, dtype=jnp.float32)
    g_weight = jnp.sum(g_probs * g_onehot, axis=-1)
    e_logits_all = jnp.einsum('nd,gde->nge', xt, w_router_expert).astype(jnp.float32) \
        + b_router_expert.astype(jnp.float32)[None]
    e_logits = jnp.sum(e_logits_all * g_onehot[:, :, None], axis=1)
    e_probs = jax.nn.softmax(e_logits, axis=-1)
    top_p, top_i = lax.top_k(e_probs, TOP_K)
    top_p = top_p / jnp.sum(top_p, axis=-1, keepdims=True)
    e_w = jnp.sum(jax.nn.one_hot(top_i, EXPERTS_PER_GROUP, dtype=jnp.float32) * top_p[..., None], axis=1)
    combine = (g_onehot[:, :, None] * (g_weight[:, None] * e_w)[:, None, :]).astype(x.dtype)
    out = jnp.zeros((n, D), dtype=x.dtype)
    for g in range(N_GROUPS):
        h = jax.nn.silu(jnp.einsum('nd,edf->nef', xt, w_gate[g])) * jnp.einsum('nd,edf->nef', xt, w_up[g])
        out = out + jnp.einsum('nef,efd->nd', h * combine[:, g, :, None], w_down[g])
    return out.reshape(B, S, D)

def first_inputs(seed: int = 0) -> dict:
    key = jax.random.key(seed)
    ks = jax.random.split(key, 20)
    f32 = jnp.float32
    nrm = lambda k, shape, s: jax.random.normal(k, shape, f32) * s
    gain = lambda k, shape: 1.0 + 0.02 * jax.random.normal(k, shape, f32)
    L, G, E = DEPTH, N_GROUPS, EXPERTS_PER_GROUP
    return {
        "x": jax.random.normal(ks[0], (BATCH, SEQ, D_MODEL), f32),
        "attn_norm_g": gain(ks[1], (L, D_MODEL)),
        "w_in": nrm(ks[2], (L, D_MODEL, D_IN), D_MODEL ** -0.5),
        "sg_norm_g": gain(ks[3], (L, SG_WIDTH)),
        "w_spatial": nrm(ks[4], (L, SG_HEADS, CHUNK, CHUNK), CHUNK ** -0.5),
        "b_spatial": gain(ks[5], (L, SG_HEADS, CHUNK)),
        "sb_out_norm_g": gain(ks[6], (L, SB_WIDTH)),
        "sg_out_norm_g": gain(ks[7], (L, SG_WIDTH)),
        "w_out": nrm(ks[8], (L, D_MIX, D_MODEL), D_MIX ** -0.5),
        "ffn_norm_g": gain(ks[9], (L, D_MODEL)),
        "w_router_group": nrm(ks[10], (L, D_MODEL, G), D_MODEL ** -0.5),
        "b_router_group": nrm(ks[11], (L, G), 0.01),
        "w_router_expert": nrm(ks[12], (L, G, D_MODEL, E), D_MODEL ** -0.5),
        "b_router_expert": nrm(ks[13], (L, G, E), 0.01),
        "w_gate": nrm(ks[14], (L, G, E, D_MODEL, D_EXPERT), D_MODEL ** -0.5),
        "w_up": nrm(ks[15], (L, G, E, D_MODEL, D_EXPERT), D_MODEL ** -0.5),
        "w_down": nrm(ks[16], (L, G, E, D_EXPERT, D_MODEL), D_EXPERT ** -0.5),
        "final_norm_g": gain(ks[17], (D_MODEL,)),
    }

def first_block(x, attn_norm_g, w_in, sg_norm_g, w_spatial, b_spatial, sb_out_norm_g, sg_out_norm_g,
              w_out, ffn_norm_g, w_router_group, b_router_group, w_router_expert, b_router_expert,
              w_gate, w_up, w_down, final_norm_g):
    B, S, _ = x.shape
    h = x
    for layer in range(DEPTH):
        hn = rmsnorm(h, attn_norm_g[layer])
        proj = hn @ w_in[layer]
        q, k, v, u, vg = jnp.split(proj, [SB_WIDTH, 2 * SB_WIDTH, 3 * SB_WIDTH, 3 * SB_WIDTH + SG_WIDTH], axis=-1)
        shp = (B, S, SB_HEADS, HEAD_DIM)
        sb_out = stick_breaking_attention(q.reshape(shp), k.reshape(shp), v.reshape(shp))
        sg_out = chunked_spatial_gating(u, vg, sg_norm_g[layer], w_spatial[layer], b_spatial[layer])
        mixed = jnp.concatenate([rmsnorm(sb_out, sb_out_norm_g[layer]),
                                 rmsnorm(sg_out, sg_out_norm_g[layer])], axis=-1)
        h = h + mixed @ w_out[layer]
        hn = rmsnorm(h, ffn_norm_g[layer])
        h = h + hierarchical_moe(hn, w_router_group[layer], b_router_group[layer],
                                 w_router_expert[layer], b_router_expert[layer],
                                 w_gate[layer], w_up[layer], w_down[layer])
    return rmsnorm(h, final_norm_g)


D_CONV = D_MODEL
CONV_A_WIDTH = 31
D_RNN = 1536
N_RNN_HEADS = 16
RNN_HEAD_DIM = D_RNN // N_RNN_HEADS
CONV_B_WIDTH = 4
LRU_C = 8.0
D_FF = 4 * D_MODEL

SPLITS = (D_CONV, D_CONV, D_RNN, D_RNN, D_MODEL, D_MODEL)
D_IN_2 = sum(SPLITS)


def rms_norm(x, g):
    xf = x.astype(jnp.float32)
    y = xf * lax.rsqrt(jnp.mean(xf * xf, axis=-1, keepdims=True) + EPS)
    return (y * g.astype(jnp.float32)).astype(x.dtype)

def layer_norm(x, g, b):
    xf = x.astype(jnp.float32)
    mu = jnp.mean(xf, axis=-1, keepdims=True)
    xc = xf - mu
    y = xc * lax.rsqrt(jnp.mean(xc * xc, axis=-1, keepdims=True) + EPS)
    return (y * g.astype(jnp.float32) + b.astype(jnp.float32)).astype(x.dtype)

def causal_depthwise_conv(u, w, b):
    k = w.shape[0]
    y = lax.conv_general_dilated(
        u, w[:, None, :].astype(u.dtype), window_strides=(1,), padding=[(k - 1, 0)],
        dimension_numbers=("NWC", "WIO", "NWC"), feature_group_count=u.shape[-1])
    return y + b

def block_diag_linear(x, w, b):
    bsz, s, c = x.shape
    xh = x.reshape(bsz, s, N_RNN_HEADS, RNN_HEAD_DIM)
    y = jnp.einsum("bshi,hij->bshj", xh, w).reshape(bsz, s, c)
    return y + b

def rg_lru(x, w_a, b_a, w_x, b_x, lam):
    s = x.shape[1]
    r = jax.nn.sigmoid(block_diag_linear(x, w_a, b_a).astype(jnp.float32))
    i = jax.nn.sigmoid(block_diag_linear(x, w_x, b_x).astype(jnp.float32))
    log_a = -LRU_C * r * jax.nn.softplus(-lam.astype(jnp.float32))
    a = jnp.exp(log_a)
    mult = jnp.sqrt(-jnp.expm1(2.0 * log_a))
    is_start = (jnp.arange(s) == 0)[None, :, None]
    mult = jnp.where(is_start, 1.0, mult)
    bterm = mult * i * x.astype(jnp.float32)

    def combine(left, right):
        a_l, b_l = left
        a_r, b_r = right
        return a_r * a_l, a_r * b_l + b_r

    _, h = lax.associative_scan(combine, (a, bterm), axis=1)
    return h.astype(x.dtype)

def second_inputs(seed: int = 0) -> dict:
    key = jax.random.key(seed)
    ks = jax.random.split(key, 32)
    f32 = jnp.float32
    L = DEPTH

    def nrm(k, shape, scale):
        return jax.random.normal(k, shape, f32) * scale

    x = jax.random.normal(ks[0], (BATCH, SEQ, D_MODEL), f32)
    g_mix = 1.0 + nrm(ks[1], (L, D_MODEL), 0.02)
    w_in = nrm(ks[2], (L, D_MODEL, D_IN_2), D_MODEL ** -0.5)
    b_in = nrm(ks[3], (L, D_IN_2), 0.02)
    conv_a_w = nrm(ks[4], (L, CONV_A_WIDTH, D_CONV), CONV_A_WIDTH ** -0.5)
    conv_a_b = nrm(ks[5], (L, D_CONV), 0.02)
    ln_g = 1.0 + nrm(ks[6], (L, D_CONV), 0.02)
    ln_b = nrm(ks[7], (L, D_CONV), 0.02)
    w_a_out = nrm(ks[8], (L, D_CONV, D_MODEL), D_CONV ** -0.5)
    conv_b_w = nrm(ks[9], (L, CONV_B_WIDTH, D_RNN), CONV_B_WIDTH ** -0.5)
    conv_b_b = nrm(ks[10], (L, D_RNN), 0.02)
    w_rg_a = nrm(ks[11], (L, N_RNN_HEADS, RNN_HEAD_DIM, RNN_HEAD_DIM), RNN_HEAD_DIM ** -0.5)
    b_rg_a = nrm(ks[12], (L, D_RNN), 0.02)
    w_rg_x = nrm(ks[13], (L, N_RNN_HEADS, RNN_HEAD_DIM, RNN_HEAD_DIM), RNN_HEAD_DIM ** -0.5)
    b_rg_x = nrm(ks[14], (L, D_RNN), 0.02)
    a0 = jax.random.uniform(ks[15], (L, D_RNN), f32, 0.9, 0.999)
    s0 = a0 ** (1.0 / LRU_C)
    lam = jnp.log(s0) - jnp.log1p(-s0)
    w_b_out = nrm(ks[16], (L, D_RNN, D_MODEL), D_RNN ** -0.5)
    w_o = nrm(ks[17], (L, D_MODEL, D_MODEL), D_MODEL ** -0.5)
    g_mlp = 1.0 + nrm(ks[18], (L, D_MODEL), 0.02)
    w_1 = nrm(ks[19], (L, D_MODEL, D_FF), D_MODEL ** -0.5)
    w_2 = nrm(ks[20], (L, D_FF, D_MODEL), D_FF ** -0.5)
    g_final = 1.0 + nrm(ks[21], (D_MODEL,), 0.02)
    return {"x": x, "g_mix": g_mix, "w_in": w_in, "b_in": b_in,
            "conv_a_w": conv_a_w, "conv_a_b": conv_a_b, "ln_g": ln_g, "ln_b": ln_b,
            "w_a_out": w_a_out, "conv_b_w": conv_b_w, "conv_b_b": conv_b_b,
            "w_rg_a": w_rg_a, "b_rg_a": b_rg_a, "w_rg_x": w_rg_x, "b_rg_x": b_rg_x,
            "lam": lam, "w_b_out": w_b_out, "w_o": w_o, "g_mlp": g_mlp,
            "w_1": w_1, "w_2": w_2, "g_final": g_final}

def second_block(x, g_mix, w_in, b_in, conv_a_w, conv_a_b, ln_g, ln_b, w_a_out,
              conv_b_w, conv_b_b, w_rg_a, b_rg_a, w_rg_x, b_rg_x, lam, w_b_out,
              w_o, g_mlp, w_1, w_2, g_final):
    cuts = np.cumsum(SPLITS)[:-1].tolist()
    for l in range(DEPTH):
        h = rms_norm(x, g_mix[l])
        z = jnp.einsum("bsd,de->bse", h, w_in[l]) + b_in[l]
        va, ga, xb, gb, sa, sb = jnp.split(z, cuts, axis=-1)

        u = va * jax.nn.sigmoid(ga)
        u = causal_depthwise_conv(u, conv_a_w[l], conv_a_b[l])
        u = jax.nn.silu(layer_norm(u, ln_g[l], ln_b[l]))
        y_a = jnp.einsum("bsc,cd->bsd", u, w_a_out[l])

        v = causal_depthwise_conv(xb, conv_b_w[l], conv_b_b[l])
        v = rg_lru(v, w_rg_a[l], b_rg_a[l], w_rg_x[l], b_rg_x[l], lam[l])
        y_b = jnp.einsum("bsc,cd->bsd", v * jax.nn.gelu(gb), w_b_out[l])

        m = jax.nn.sigmoid(sa) * y_a + jax.nn.sigmoid(sb) * y_b
        x = x + jnp.einsum("bsd,de->bse", m, w_o[l])

        h = rms_norm(x, g_mlp[l])
        f = jnp.square(jax.nn.relu(jnp.einsum("bsd,df->bsf", h, w_1[l])))
        x = x + jnp.einsum("bsf,fd->bsd", f, w_2[l])
    return rms_norm(x, g_final)


def setup_inputs(seed=0):
    out = dict(first_inputs(seed))
    for name, value in second_inputs(seed + 1).items():
        if name != "x":
            out[name + "_2"] = value
    return out


def reference(
    x, attn_norm_g, w_in, sg_norm_g, w_spatial, b_spatial, sb_out_norm_g, sg_out_norm_g, w_out,
    ffn_norm_g, w_router_group, b_router_group, w_router_expert, b_router_expert, w_gate, w_up,
    w_down, final_norm_g, g_mix_2, w_in_2, b_in_2, conv_a_w_2, conv_a_b_2, ln_g_2, ln_b_2,
    w_a_out_2, conv_b_w_2, conv_b_b_2, w_rg_a_2, b_rg_a_2, w_rg_x_2, b_rg_x_2, lam_2, w_b_out_2,
    w_o_2, g_mlp_2, w_1_2, w_2_2, g_final_2,
):
    x = first_block(
        x, attn_norm_g, w_in, sg_norm_g, w_spatial, b_spatial, sb_out_norm_g, sg_out_norm_g,
        w_out, ffn_norm_g, w_router_group, b_router_group, w_router_expert, b_router_expert,
        w_gate, w_up, w_down, final_norm_g,
    )
    return second_block(
        x, g_mix_2, w_in_2, b_in_2, conv_a_w_2, conv_a_b_2, ln_g_2, ln_b_2, w_a_out_2,
        conv_b_w_2, conv_b_b_2, w_rg_a_2, b_rg_a_2, w_rg_x_2, b_rg_x_2, lam_2, w_b_out_2, w_o_2,
        g_mlp_2, w_1_2, w_2_2, g_final_2,
    )


_drawn_inputs = setup_inputs


def setup_inputs(seed=0):
    import zlib

    import numpy as np

    out = dict(_drawn_inputs(seed))
    spreads = {}
    factors = {'sg_norm_g': 16.353,
     'b_spatial': 3.195,
     'sb_out_norm_g': 3.114,
     'sg_out_norm_g': 4.006,
     'b_router_group': 16.848,
     'b_router_expert': 22.877,
     'g_mix_2': 4.595,
     'conv_a_b_2': 14.82,
     'ln_g_2': 57.09,
     'ln_b_2': 54.663,
     'b_rg_a_2': 28.069,
     'b_rg_x_2': 51.592,
     'g_mlp_2': 10.375,
     'g_final_2': 23.217,
     'ffn_norm_g': 4.118,
     'b_in_2': 3.745,
     'conv_b_b_2': 3.859}
    for name, (base, spread) in spreads.items():
        noise = np.random.default_rng([zlib.crc32(name.encode()), seed]).standard_normal(out[name].shape)
        drawn = base * np.exp(spread * noise) if base else spread * noise
        out[name] = __import__('jax').numpy.asarray(drawn.astype(out[name].dtype))
    for name, factor in factors.items():
        out[name] = (out[name] * factor).astype(out[name].dtype)
    return out
```

```python
from contextlib import ExitStack

import numpy as np

import concourse.bass as bass
from concourse import mybir

F32 = mybir.dt.float32
I32 = mybir.dt.int32
ALU = mybir.AluOpType
ACT = mybir.ActivationFunctionType
AX_X = mybir.AxisListType.X

P = 128
T = 256
TT = T // P
D = 1024
KC = D // P
EPS = 1e-6
HEADS, HEAD_DIM = 8, 64
SB = HEADS * HEAD_DIM
GROUPS, EXPERTS_PER_GROUP = 4, 8
EXPERTS = GROUPS * EXPERTS_PER_GROUP
D_EXPERT = 512
SLOTS = 32
STRIPS = P // SLOTS
PACK = 4
PACKS = EXPERTS // PACK
F_STRIP = D_EXPERT // STRIPS
D_STRIP = D // STRIPS
EXTRA_MAX = 2 * T // SLOTS - 1
BLOCK = 512
SLOT_FLOATS = KC * BLOCK
RING = 6
IN1_BLOCKS = 5
OUT1_BLOCKS = 2
PRE = IN1_BLOCKS + OUT1_BLOCKS
D_RNN, RNN_HEAD = 1536, 96
RC = D_RNN // P
RG = 4
TAPS_A, TAPS_B = 31, 4
LRU_C = 8.0
D_FF = 4 * D
FC = D_FF // P
IN2_BLOCKS = 14
IN2_ORDER = [2, 3, 0, 1] + list(range(4, IN2_BLOCKS))
ZC = IN2_BLOCKS * 4
Z_GA, Z_VA, Z_XB, Z_GB, Z_SA, Z_SB = 0, 8, 16, 28, 40, 48
MASKED = -1e30
B_COMB, B_GATE, B_DOWN, B_TURN, B_GATHER = 0, 2, 4, 6, 7

V_BIN, V_CAB, V_LNG, V_LNB, V_CBB, V_BRA, V_BRX, V_LAM = 0, 56, 64, 72, 80, 92, 104, 116


def build(nc, A, out):
    ctx = ExitStack()
    with ctx:
        def sb(name, shape, dt=F32):
            return ctx.enter_context(nc.sbuf_tensor(name, shape, dt))

        def sem(name):
            return ctx.enter_context(nc.semaphore(name))

        ARENA = 17408
        mem = sb("mem", [P, RING * SLOT_FLOATS + ARENA])
        slot = [mem[:, s * SLOT_FLOATS:(s + 1) * SLOT_FLOATS] for s in range(RING)]

        def carver(start, end):
            at = [start]

            def carve(*shape):
                n = int(np.prod(shape))
                view = mem[:, at[0]:at[0] + n]
                at[0] += n
                assert at[0] <= end, (at[0], end)
                if len(shape) == 2:
                    view = view.rearrange("p (a b) -> p a b", a=shape[0])
                if len(shape) == 3:
                    view = view.rearrange("p (a b c) -> p a b c", a=shape[0], b=shape[1])
                return view
            return carve

        a0 = RING * SLOT_FLOATS
        aend = a0 + ARENA
        X = sb("X", [P, TT, D])
        HN = sb("HN", [P, TT, KC, P])
        HT = sb("HT", [P, KC, T])
        ident = sb("ident", [P, P])
        tri_neg = sb("tri_neg", [P, P])
        neg_ones = sb("neg_ones", [P, P])
        ones = sb("ones", [P, P])
        mean_ones = sb("mean_ones", [P, P])
        before = sb("before", [P, P])
        upto = sb("upto", [P, P])
        maskbias = sb("maskbias", [P, P])
        eps = sb("eps", [P, 1])
        zeros = sb("zeros", [P, P])
        iota_i = sb("iota_i", [P, SLOTS], I32)
        iota_s = sb("iota_s", [P, SLOTS])
        gains = sb("gains", [P, 5, KC])
        G_ATTN, G_MIX, G_FFN, G_MIX2, G_MLP2 = range(5)
        VEC = sb("VEC", [P, P])
        CAW = sb("CAW", [P, TAPS_A * KC])
        CBW = sb("CBW", [P, TAPS_B * RC])
        wr_group = sb("wr_group", [P, KC, GROUPS])
        wr_expert = sb("wr_expert", [P, GROUPS, KC, EXPERTS_PER_GROUP])
        b_router = sb("b_router", [P, GROUPS + EXPERTS])
        g_first = sb("g_first", [P, D])
        g_last = sb("g_last", [P, D])
        ss = sb("ss", [P, 16])
        rstd = sb("rstd", [P, 16])
        sp8 = sb("sp8", [P, 4, RC])
        extra_row = sb("extra_row", [1, 3, 16])
        extra_i = sb("extra_i", [1, 3, 16], I32)
        first_rank = sb("first_rank", [P, 16])
        rank_iota = sb("rank_iota", [P, SLOTS])
        PS = ctx.enter_context(nc.psum_tensor("PS", [P, 8, 512], F32))

        c = carver(a0, aend)
        square = c(D)
        qT, kT = c(HEADS, T), c(4, T)
        V, U, VG = c(TT, SB), c(TT, SB), c(TT, SB)
        wsp, wspT = c(HEADS, P), c(HEADS, P)
        ao, so = c(TT, SB), c(TT, SB)
        att_e, att_s, att_a = c(2, 3 * P), c(2, 3 * P), c(2, 3 * P)
        sgn_g = c(SB)
        bsp, bspT = c(P), c(HEADS)
        vec_raw, caw_raw, cbw_raw = c(P), c(2, P), c(P)
        c = carver(a0 + D, aend)
        logit = c(TT, GROUPS + EXPERTS)
        r_a, r_b, r_c = c(TT, 16), c(TT, EXPERTS), c(TT, 64)
        routed, combine, rank = c(TT, EXPERTS), c(TT, EXPERTS), c(TT, EXPERTS)
        sel, selw = c(TT, P), c(TT, P)
        XG = c(KC, P)
        CT = c(T)
        silu, hid, hidT = c(2, P), c(2, P), c(2, P)
        Y = c(D)
        extra_f, extra_cmp = c(4, EXPERTS)[0:1], c(16, EXPERTS)[0:1]
        c = carver(4 * SLOT_FLOATS, aend)
        Z = c(ZC, T)
        CU = c(KC, T)
        VB, RB, AB = c(RC, T), c(RC, T), c(RC, T)
        bd_at = 4 * SLOT_FLOATS + (ZC * T + KC * T + 3 * RC * T)
        IB = HN[:, :, :, :].rearrange("p a b c -> p (a b c)")[:, 0:2 * 3 * T].rearrange("p (a b c) -> p a b c", a=2, b=3)
        BDA, BDX = (slot[s][:, 0:RG * 3 * 192].rearrange("p (g r n) -> p g r n", g=RG, r=3) for s in (0, 3))
        c = carver(4 * SLOT_FLOATS, aend)
        FT = c(FC // 2, T)
        fin = c(TT, D)

        x_loaded, small_loaded = sem("x_loaded"), sem("small_loaded")
        router_loaded, table_loaded = sem("router_loaded"), sem("table_loaded")
        bd_loaded = sem("bd_loaded")
        loaded = [sem(f"loaded{s}") for s in range(RING)]
        extra_loaded = [sem(f"extra_loaded{s}") for s in range(3)]
        b2_loaded = [sem(f"b2_loaded{s}") for s in range(4)]
        consts = sem("consts")
        pool_chain, dve_chain, act_chain = sem("pool_chain"), sem("dve_chain"), sem("act_chain")
        qz_ready = sem("qz_ready")
        norms = ["attn", "mix", "ffn", "mix2", "mlp2"]
        rms_ready = {n: sem(f"rms_ready_{n}") for n in norms + ["vg", "first", "last"]}
        rows = {n: sem(f"rows_{n}") for n in norms}
        turned = {n: sem(f"turned_{n}") for n in norms}
        hT_ready = {n: sem(f"hT_ready_{n}") for n in norms}
        wsp_turned, wspT_ready = sem("wsp_turned"), sem("wspT_ready")
        tables_turned, tables_ready = sem("tables_turned"), sem("tables_ready")
        qk_ps, qk_ready = sem("qk_ps"), sem("qk_ready")
        vug_ps, v_ready, gelu_ready = sem("vug_ps"), sem("v_ready"), sem("gelu_ready")
        vg_ready = sem("vg_ready")
        score_ps, att_abs, att_ln, att_sp = sem("score_ps"), sem("att_abs"), sem("att_ln"), sem("att_sp")
        att_ps, att_x, att_exp, av_done = sem("att_ps"), sem("att_x"), sem("att_exp"), sem("av_done")
        ao_ready, sgu_ps, so_ready = sem("ao_ready"), sem("sgu_ps"), sem("so_ready")
        out1_ps, x_ready = sem("out1_ps"), sem("x_ready")
        logits_ps, r_exp_in, r_exp = sem("logits_ps"), sem("r_exp_in"), sem("r_exp")
        routed_ready, rank_ps, count_ps = sem("routed_ready"), sem("rank_ps"), sem("count_ps")
        extra_ready = sem("extra_ready")
        sel_ready, gath_ps, xg_ready = sem("sel_ready"), sem("gath_ps"), sem("xg_ready")
        ct_ps, ct_ready = sem("ct_ps"), sem("ct_ready")
        gu_done, silu_ready, hid_ready = sem("gu_done"), sem("silu_ready"), sem("hid_ready")
        hidT_ps, hidT_ready, down_done = sem("hidT_ps"), sem("hidT_ready"), sem("down_done")
        y_act, y_dve, comb_ps = sem("y_act"), sem("y_dve"), sem("comb_ps")
        moe_done, comb_free = sem("moe_done"), sem("comb_free")
        x2_ready = sem("x2_ready")
        sel_made, first_ps, first_ready, slot_ranks = sem("sel_made"), sem("first_ps"), sem("first_ready"), sem("slot_ranks")
        tap_step, short_step = [sem(f"tap_step{i}") for i in range(2)], [sem(f"short_step{i}") for i in range(2)]
        w2_used = sem("w2_used")
        lru_square, lru_root, var_in, var_root = sem("lru_square"), sem("lru_root"), sem("var_in"), sem("var_root")
        z_ps, z_bank_free, z_ready = sem("z_ps"), sem("z_bank_free"), sem("z_ready")
        ga_ready, conv_ready, v2_ready = sem("ga_ready"), sem("conv_ready"), sem("v2_ready")
        lru_ps, lru_gates, lru_log, lru_exp = sem("lru_ps"), sem("lru_gates"), sem("lru_log"), sem("lru_exp")
        lam_ln, gb_ready, sab_ready, h_ready = sem("lam_ln"), sem("gb_ready"), sem("sab_ready"), sem("h_ready")
        mean_ps, centred, sq_ready, var_ps, scaled, a_ready = (
            sem("mean_ps"), sem("centred"), sem("sq_ready"), sem("var_ps"), sem("scaled"), sem("a_ready"))
        y_ps, y_bank_free, m_ready = sem("y_ps"), sem("y_bank_free"), sem("m_ready")
        o_ps, x3_ready = sem("o_ps"), sem("x3_ready")
        f_ps, f_relu, f_bank_free, f_ready = sem("f_ps"), sem("f_relu"), sem("f_bank_free"), sem("f_ready")
        mlp_ps, x4_ready = sem("mlp_ps"), sem("x4_ready")
        fin_ready, stored = sem("fin_ready"), sem("stored")

        x_d = A["x"][0].rearrange("(a p) d -> p a d", p=P)
        out_d = out[0].rearrange("(a p) d -> p a d", p=P)

        def by_pk(w):
            return w.rearrange("(p k) n -> p k n", k=KC)

        def by_kp(w):
            return w.rearrange("(k p) n -> p k n", p=P)

        w_in1, w_out1 = by_pk(A["w_in"][0]), by_pk(A["w_out"][0])
        wg_d = A["w_gate"][0].rearrange("g e (p k) n -> (g e) p (k n)", k=KC)
        wu_d = A["w_up"][0].rearrange("g e (p k) n -> (g e) p (k n)", k=KC)
        wd_d = A["w_down"][0].rearrange("g e (k p) n -> (g e) p k n", p=P)
        w_in2 = by_pk(A["w_in_2"][0])
        wa_d, wb_d, wo_d = by_kp(A["w_a_out_2"][0]), by_kp(A["w_b_out_2"][0]), by_kp(A["w_o_2"][0])
        w1_d, w2_d = by_pk(A["w_1_2"][0]), by_kp(A["w_2_2"][0])

        def chunked(s, n):
            return slot[s][:, 0:SLOT_FLOATS // n * n].rearrange("p (k n) -> p k n", n=n)

        b2 = [(w_in2[:, :, b * BLOCK:(b + 1) * BLOCK], 1 + n % 2) for n, b in enumerate(IN2_ORDER)]
        L_B, L_A, L_O, L_F = 14, 18, 20, 22
        b2 += [(wb_d[:, :, 256 * n:256 * (n + 1)], (3 + n) % 4) for n in range(4)]
        b2 += [(wa_d[:, :, BLOCK * n:BLOCK * (n + 1)], (3 + n) % 4) for n in range(2)]
        b2 += [(wo_d[:, :, BLOCK * n:BLOCK * (n + 1)], (1 + n) % 4) for n in range(2)]
        for half in range(2):
            b2 += [(w1_d[:, :, BLOCK * n:BLOCK * (n + 1)], (3 + n) % 4) for n in range(4 * half, 4 * half + 4)]
            b2 += [(w2_d[:, 4 * n:4 * n + 4, :], (3 + n) % 4) for n in range(4 * half, 4 * half + 4)]

        def b2_arrivals(n):
            return 16 * sum(b2[m][1] == b2[n][1] for m in range(n + 1))

        def b2_used_up(n):
            if n < L_B:
                return z_ps, 4 * (n + 1)
            if n < L_A:
                return y_ps, 2 * (n - L_B + 1)
            if n < L_O:
                return y_ps, KC + 4 * (n - L_A + 1)
            if n < L_F:
                return o_ps, 2 * (n - L_O + 1)
            half, b = (n - L_F) // 8, (n - L_F) % 8
            return (f_ps, 16 * half + 4 * (b + 1)) if b < 4 else (w2_used, 4 * half + b - 3)

        def pre_count(n):
            return 16 * (n // RING + 1)

        block = ctx.enter_context(nc.Block())

        @block.sync
        def _(sp):
            sp.dma_start(X[:, 0, :], x_d[:, 0, :]).then_inc(x_loaded, 16)
            sp.dma_start(X[:, 1, :], x_d[:, 1, :]).then_inc(x_loaded, 16)
            for n in range(PRE):
                if n >= RING:
                    sp.wait_ge(qk_ps, 4)
                w, b = (w_in1, n) if n < IN1_BLOCKS else (w_out1, n - IN1_BLOCKS)
                sp.dma_start(chunked(n % RING, BLOCK), w[:, :, b * BLOCK:(b + 1) * BLOCK]).then_inc(loaded[n % RING], 16)

            def load_expert(e, i):
                for part, w in enumerate((wg_d, wu_d)):
                    s = (PRE + 3 * i + part) % RING
                    sp.dma_start(slot[s], w[bass.ds(e, 1)].rearrange("e p n -> p (e n)")).then_inc(loaded[s], 16)

            def load_down(e, i):
                s = (PRE + 3 * i + 2) % RING
                sp.dma_start(chunked(s, D), wd_d[bass.ds(e, 1)].rearrange("e p k n -> p (e k) n")).then_inc(loaded[s], 16)

            sp.wait_ge(qk_ps, 8)
            sp.wait_ge(vug_ps, 2)
            load_expert(0, 0)
            sp.wait_ge(vug_ps, 4)
            load_down(0, 0)
            sp.wait_ge(vug_ps, 6)
            sp.wait_ge(out1_ps, 2)
            load_expert(1, 1)
            sp.wait_ge(out1_ps, 4)
            load_down(1, 1)
            with sp.Fori(1, EXPERTS // 2) as pair:
                for i in range(2):
                    sp.wait_ge(gu_done, 2 * pair + (i - 1))
                    load_expert(2 * pair + i, i)
                    sp.wait_ge(down_done, 2 * pair + (i - 1))
                    load_down(2 * pair + i, i)
            sp.wait_ge(extra_ready, 1)
            n_extra = sp.value_load(extra_i[0:1, 0, 0:1], min_val=0, max_val=EXTRA_MAX)
            with sp.Fori(0, EXTRA_MAX) as j:
                with sp.If(j < n_extra):
                    e = sp.value_load(extra_i[0:1, 1, bass.ds(j, 1)], min_val=0, max_val=EXPERTS - 1)
                    sp.wait_ge(down_done, j + (EXPERTS - 1))
                    for part, w in enumerate((wg_d, wu_d)):
                        sp.dma_start(slot[1 + part], w[bass.ds(e, 1)].rearrange("e p n -> p (e n)")).then_inc(extra_loaded[part], 16)
                    sp.dma_start(chunked(3, D), wd_d[bass.ds(e, 1)].rearrange("e p k n -> p (e k) n")).then_inc(extra_loaded[2], 16)
            sp.wait_ge(down_done, n_extra + EXPERTS)
            last = {}
            for n, (src, s) in enumerate(b2):
                if s in last:
                    sp.wait_ge(*b2_used_up(last[s]))
                elif n >= L_B:
                    sp.wait_ge(lru_ps, RG)
                last[s] = n
                width = src.shape[2]
                dst = slot[s][:, 0:src.shape[1] * width].rearrange("p (k n) -> p k n", n=width)
                sp.dma_start(dst, src).then_inc(b2_loaded[s], 16)
            for tt in range(TT):
                sp.wait_ge(fin_ready, tt + 1)
                sp.dma_start(out_d[:, tt, :], fin[:, tt, :]).then_inc(stored, 16)
            sp.wait_ge(stored, 16 * TT)

        @block.gpsimd
        def _(pool):
            done = [0]

            def link(ins):
                done[0] += 1
                ins.then_inc(pool_chain, 1)
                pool.wait_ge(pool_chain, done[0])

            def triangle(m, inside, outside, compare, row, col, base=0):
                link(nc.gpsimd.memset(m[:, :], inside))
                nc.gpsimd.affine_select(out=m[:, :], in_=m[:, :], compare_op=compare, fill=outside, base=base,
                                        pattern=[[col, P]], channel_multiplier=row).then_inc(consts, 1)

            triangle(ident, 0.0, 1.0, ALU.not_equal, 1, -1)
            triangle(upto, 1.0, 0.0, ALU.is_ge, -1, 1)
            triangle(before, 1.0, 0.0, ALU.is_gt, -1, 1)
            triangle(maskbias, 0.0, MASKED, ALU.is_gt, -1, 1)
            triangle(tri_neg, -1.0, 0.0, ALU.is_ge, 1, -1)
            nc.gpsimd.memset(neg_ones[:, :], -1.0).then_inc(consts, 1)
            nc.gpsimd.memset(ones[:, :], 1.0).then_inc(consts, 1)
            nc.gpsimd.memset(mean_ones[:, :], 1.0 / D).then_inc(consts, 1)
            nc.gpsimd.memset(zeros[:, :], 0.0).then_inc(consts, 1)
            nc.gpsimd.memset(eps[:, :], EPS).then_inc(consts, 1)
            nc.gpsimd.memset(qT, 0.0).then_inc(qz_ready, 1)
            link(nc.gpsimd.iota(iota_i[:, :], pattern=[[1, SLOTS]], base=0, channel_multiplier=0))
            nc.gpsimd.tensor_copy(iota_s[:, :], iota_i[:, :]).then_inc(consts, 1)

            pool.wait_ge(moe_done, 1)
            link(nc.gpsimd.memset(BDA[:, :, :, :], 0.0))
            link(nc.gpsimd.memset(BDX[:, :, :, :], 0.0))
            for bd, w in ((BDA, A["w_rg_a_2"]), (BDX, A["w_rg_x_2"])):
                heads = w[0].rearrange("(g h) i j -> h i g j", g=RG)
                for h in range(4):
                    r0 = h * RNN_HEAD
                    while r0 < (h + 1) * RNN_HEAD:
                        chunk = r0 // P
                        r1 = min((chunk + 1) * P, (h + 1) * RNN_HEAD)
                        c0 = h * RNN_HEAD - chunk * RNN_HEAD
                        pool.dma_start(bd[r0 - chunk * P:r1 - chunk * P, :, chunk, c0:c0 + RNN_HEAD],
                                       heads[h, r0 - h * RNN_HEAD:r1 - h * RNN_HEAD]).then_inc(bd_loaded, 16)
                        r0 = r1

        N_BD = 12
        N_CONST = 11
        N_SMALL = 8

        @block.scalar
        def _(act):
            done = [0]

            def link(ins):
                done[0] += 1
                ins.then_inc(act_chain, 1)
                act.wait_ge(act_chain, done[0])

            def vec(v):
                return v.rearrange("(p k) -> p k", k=KC)

            half = P // 2
            act.dma_start(gains[:, G_ATTN, :], vec(A["attn_norm_g"][0])).then_inc(small_loaded, 16)
            act.dma_start(wsp, A["w_spatial"][0].rearrange("h t s -> t h s")).then_inc(small_loaded, 16)
            act.dma_start(bsp[0:HEADS], A["b_spatial"][0]).then_inc(small_loaded, 16)
            act.dma_start(sgn_g, A["sg_norm_g"].partition_broadcast(P).rearrange("p a n -> p (a n)")).then_inc(small_loaded, 16)
            act.dma_start(gains[0:half, G_MIX, :], vec(A["sb_out_norm_g"][0])).then_inc(small_loaded, 16)
            act.dma_start(gains[half:P, G_MIX, :], vec(A["sg_out_norm_g"][0])).then_inc(small_loaded, 16)
            act.dma_start(gains[:, G_MIX2, :], vec(A["g_mix_2"][0])).then_inc(small_loaded, 16)
            act.dma_start(gains[:, G_MLP2, :], vec(A["g_mlp_2"][0])).then_inc(small_loaded, 16)
            act.dma_start(gains[:, G_FFN, :], vec(A["ffn_norm_g"][0])).then_inc(router_loaded, 16)
            act.dma_start(wr_group[:, :, :], by_pk(A["w_router_group"][0])).then_inc(router_loaded, 16)
            act.dma_start(wr_expert[:, :, :, :], A["w_router_expert"][0].rearrange("g (p k) e -> p g k e", k=KC)).then_inc(router_loaded, 16)
            act.dma_start(b_router[:, 0:GROUPS], A["b_router_group"][0].partition_broadcast(P)).then_inc(router_loaded, 16)
            act.dma_start(b_router[:, GROUPS:], A["b_router_expert"][0].rearrange("g e -> (g e)").partition_broadcast(P)).then_inc(router_loaded, 16)
            act.dma_start(g_first[:, :], A["final_norm_g"].partition_broadcast(P)).then_inc(router_loaded, 16)
            act.dma_start(g_last[:, :], A["g_final_2"].partition_broadcast(P)).then_inc(router_loaded, 16)

            def rows128(v):
                return v.rearrange("(c p) -> c p", p=P)

            for to, count, name in ((V_CAB, 8, "conv_a_b_2"), (V_LNG, 8, "ln_g_2"), (V_LNB, 8, "ln_b_2"),
                                    (V_CBB, RC, "conv_b_b_2"), (V_BRA, RC, "b_rg_a_2"), (V_BRX, RC, "b_rg_x_2"),
                                    (V_LAM, RC, "lam_2")):
                act.dma_start(vec_raw[to:to + count], rows128(A[name][0])).then_inc(table_loaded, 16)
            b_in = rows128(A["b_in_2"][0])
            act.dma_start(vec_raw[Z_GA:Z_GA + 8], b_in[8:16]).then_inc(table_loaded, 16)
            act.dma_start(vec_raw[Z_VA:Z_VA + 8], b_in[0:8]).then_inc(table_loaded, 16)
            act.dma_start(vec_raw[Z_XB:ZC], b_in[16:ZC]).then_inc(table_loaded, 16)
            taps = A["conv_a_w_2"][0].rearrange("k (c p) -> (k c) p", p=P)
            act.dma_start(caw_raw[:, 0, :], taps[0:P]).then_inc(table_loaded, 16)
            act.dma_start(caw_raw[0:TAPS_A * KC - P, 1, :], taps[P:]).then_inc(table_loaded, 16)
            act.dma_start(cbw_raw[0:TAPS_B * RC], A["conv_b_w_2"][0].rearrange("k (c p) -> (k c) p", p=P)).then_inc(table_loaded, 16)

            def add_squares(rows_, col, scratch):
                link(nc.scalar.activation(scratch, rows_, ACT.Square, accum_out=ss[:, col:col + 1]))

            def rms(name, col, n, width):
                nc.scalar.activation(rstd[:, col:col + n], ss[:, col:col + n], ACT.Sqrt, scale=1.0 / width,
                                     bias=eps[:, :]).then_inc(rms_ready[name], 1)

            def row_squares(name, col):
                for tt in range(TT):
                    add_squares(X[:, tt, :], col + tt, square)
                rms(name, col, TT, D)

            act.wait_ge(consts, N_CONST)
            act.wait_ge(x_loaded, 16 * TT)
            row_squares("attn", 0)
            act.wait_ge(qz_ready, 1)
            for n in range(8):
                act.wait_ge(qk_ps, n + 1)
                ps = PS[:, n % 4, 0:T]
                if n < 4:
                    nc.scalar.activation(qT[0:64, 2 * n, :], ps[0:64], ACT.Copy, scale=HEAD_DIM ** -0.5)
                    nc.scalar.activation(qT[64:P, 2 * n + 1, :], ps[64:P], ACT.Copy, scale=HEAD_DIM ** -0.5).then_inc(qk_ready, 1)
                else:
                    nc.scalar.activation(kT[:, n - 4, :], ps, ACT.Copy).then_inc(qk_ready, 1)
            for n in range(2, 6):
                act.wait_ge(vug_ps, n + 1)
                dst = (U if n < 4 else VG)[:, n % 2, :]
                nc.scalar.activation(dst, PS[:, 4 + n % 4, :], ACT.Gelu_apprx_tanh).then_inc(gelu_ready, 1)
            act.wait_ge(gelu_ready, 4)
            for tt in range(TT):
                add_squares(VG[:, tt, :], 2 + tt, square[:, 0:SB])
            rms("vg", 2, TT, SB)
            def att_log(h):
                act.wait_ge(score_ps, h + 1)
                if h >= 2:
                    act.wait_ge(att_sp, h - 1)
                e = att_e[:, h % 2, :]
                link(nc.scalar.activation(e, PS[:, h % 2, 0:3 * P], ACT.Abs))
                link(nc.scalar.activation(e, e, ACT.Exp, scale=-1.0))
                nc.scalar.activation(e, e, ACT.Ln, bias=1.0).then_inc(att_ln, 1)

            def att_weights(h):
                act.wait_ge(att_x, h + 1)
                nc.scalar.activation(att_a[:, h % 2, :], att_a[:, h % 2, :], ACT.Exp).then_inc(att_exp, 1)

            act.preload_act_table_set("natural_log_exp_and_others")
            for h in range(HEADS):
                att_log(h)
                if h >= 1:
                    att_weights(h - 1)
            att_weights(HEADS - 1)
            for half_n, (rows_, ready) in enumerate(((ao, ao_ready), (so, so_ready))):
                act.wait_ge(ready, TT)
                for tt in range(TT):
                    add_squares(rows_[:, tt, :], 4 + 2 * half_n + tt, square[:, 0:SB])
            rms("mix", 4, 2 * TT, SB)
            act.wait_ge(tables_turned, 1)
            for dst, at in ((VEC, 0), (CAW, P), (CBW, P + TAPS_A * KC)):
                n = dst.shape[1]
                nc.scalar.activation(dst[:, :], PS[:, 0, at:at + n], ACT.Copy).then_inc(tables_ready, 1)
            act.wait_ge(x_ready, 4)
            row_squares("ffn", 8)
            act.wait_ge(r_exp_in, 1)
            nc.scalar.activation(r_a[:, :, 0:GROUPS + 1], r_a[:, :, 0:GROUPS + 1], ACT.Exp).then_inc(r_exp, 1)

            def turn_combine(pack):
                act.wait_ge(ct_ps, pack + 1)
                act.wait_ge(comb_ps, 4 * pack + 1)
                nc.scalar.activation(CT, PS[:, B_GATHER, 0:T], ACT.Copy).then_inc(ct_ready, 1)

            def gate(e, i):
                act.wait_ge(gu_done, e + 1)
                nc.scalar.activation(silu[:, i % 2, :], PS[:, B_GATE + i % 2, 0:P], ACT.Silu).then_inc(silu_ready, 1)

            def hidden_turned(e, i):
                act.wait_ge(hidT_ps, e + 1)
                nc.scalar.activation(hidT[:, i % 2, :], PS[:, B_TURN, 0:P], ACT.Copy).then_inc(hidT_ready, 1)

            def collect(e, i):
                act.wait_ge(down_done, e + 1)
                for j in range(2):
                    ins = nc.scalar.activation(Y[SLOTS * i:SLOTS * (i + 1), D_STRIP * j:D_STRIP * (j + 1)],
                                               PS[SLOTS * j:SLOTS * (j + 1), B_DOWN + i % 2, 0:D_STRIP], ACT.Copy)
                ins.then_inc(y_act, 1)

            with act.Fori(0, PACKS) as pack:
                e = PACK * pack
                turn_combine(pack)
                gate(e, 0)
                gate(e + 1, 1)
                for i in range(PACK):
                    hidden_turned(e + i, i)
                    collect(e + i, i)
                    if i + 2 < PACK:
                        gate(e + (i + 2), i + 2)
            act.wait_ge(extra_ready, 1)
            n_extra = act.value_load(extra_i[0:1, 0, 0:1], min_val=0, max_val=EXTRA_MAX)
            with act.Fori(0, EXTRA_MAX) as j:
                with act.If(j < n_extra):
                    turn_combine(j + PACKS)
                    gate(j + EXPERTS, 0)
                    hidden_turned(j + EXPERTS, 0)
                    collect(j + EXPERTS, 0)

            act.wait_ge(moe_done, 1)
            row_squares("first", 10)
            act.wait_ge(tables_ready, 3)
            link(nc.scalar.activation(sp8[:, 0, :], VEC[:, V_LAM:V_LAM + RC], ACT.Abs))
            link(nc.scalar.activation(sp8[:, 0, :], sp8[:, 0, :], ACT.Exp, scale=-1.0))
            nc.scalar.activation(sp8[:, 0, :], sp8[:, 0, :], ACT.Ln, bias=1.0).then_inc(lam_ln, 1)
            act.wait_ge(x2_ready, TT)
            row_squares("mix2", 12)

            def z_block_pair(pair):
                for i in range(8):
                    act.wait_ge(z_ps, 8 * pair + (i + 1))
                    nc.scalar.activation(Z[:, bass.ds(8 * pair + i, 1), :].rearrange("p a t -> p (a t)"), PS[:, i % 4, 0:T], ACT.Identity,
                                         bias=VEC[:, bass.ds(8 * pair + i, 1)]).then_inc(z_bank_free, 1)

            act.wait_ge(tables_ready, 3)
            with act.Fori(0, 2) as pair:
                z_block_pair(pair)
            act.wait_ge(z_bank_free, 4 + 16)
            nc.scalar.activation(Z[:, Z_GA:Z_GA + 8, :], Z[:, Z_GA:Z_GA + 8, :], ACT.Sigmoid).then_inc(ga_ready, 1)
            with act.Fori(2, 6) as pair:
                z_block_pair(pair)
            for g in range(RG):
                act.wait_ge(lru_ps, g + 1)
                if g >= 2:
                    act.wait_ge(lru_log, g - 1)
                for k in range(3):
                    n = 3 * g + k
                    nc.scalar.activation(RB[:, n, :], PS[:, 4 + k // 2, (k % 2) * T:(k % 2 + 1) * T], ACT.Sigmoid,
                                         bias=VEC[:, V_BRA + n:V_BRA + n + 1])
                    ins = nc.scalar.activation(IB[:, g % 2, k, :], PS[:, 6 + k // 2, (k % 2) * T:(k % 2 + 1) * T], ACT.Sigmoid,
                                               bias=VEC[:, V_BRX + n:V_BRX + n + 1])
                ins.then_inc(lru_gates, 1)
            z_block_pair(6)
            for g in range(RG):
                act.wait_ge(lru_log, g + 1)
                rows_ = slice(3 * g, 3 * g + 3)
                nc.scalar.activation(AB[:, rows_, :], RB[:, rows_, :], ACT.Exp, scale=-1.0)
                nc.scalar.activation(Z[:, Z_XB + 3 * g:Z_XB + 3 * g + 3, :], RB[:, rows_, :], ACT.Tanh).then_inc(lru_exp, 1)
            act.wait_ge(z_bank_free, 4 + ZC)
            nc.scalar.activation(Z[:, Z_GB:Z_GB + RC, :], Z[:, Z_GB:Z_GB + RC, :], ACT.Gelu_apprx_tanh).then_inc(gb_ready, 1)
            nc.scalar.activation(Z[:, Z_SA:ZC, :], Z[:, Z_SA:ZC, :], ACT.Sigmoid).then_inc(sab_ready, 1)
            act.wait_ge(centred, 1)
            nc.scalar.activation(Z[:, Z_GA:Z_GA + 8, :], CU, ACT.Square).then_inc(sq_ready, 1)
            for g in range(RG):
                act.wait_ge(lru_square, g + 1)
                th = Z[:, Z_XB + 3 * g:Z_XB + 3 * g + 3, :]
                nc.scalar.activation(th, th, ACT.Sqrt).then_inc(lru_root, 1)
            act.wait_ge(var_in, 1)
            nc.scalar.activation(IB[:, 0, 0, :], IB[:, 0, 0, :], ACT.Sqrt).then_inc(var_root, 1)
            act.wait_ge(scaled, 1)
            for k in range(KC):
                nc.scalar.activation(CU[:, k, :], CU[:, k, :], ACT.Silu, bias=VEC[:, V_LNB + k:V_LNB + k + 1],
                                     scale=VEC[:, V_LNG + k:V_LNG + k + 1]).then_inc(a_ready, 1)
            act.wait_ge(x3_ready, 4)
            row_squares("mlp2", 14)
            with act.Fori(0, 2) as half_n:
                for i in range(FC // 2):
                    act.wait_ge(f_ps, (FC // 2) * half_n + (i + 1))
                    nc.scalar.activation(FT[:, i, :], PS[:, 4 + i % 4, 0:T], ACT.Relu).then_inc(f_bank_free, 1)
            for tt in range(TT):
                act.wait_ge(x4_ready, 2 * tt + 2)
                add_squares(X[:, tt, :], tt, fin[:, tt, :])
            rms("last", 0, TT, D)

        @block.vector
        def _(dve):
            done = [0]

            def link(ins):
                done[0] += 1
                ins.then_inc(dve_chain, 1)
                dve.wait_ge(dve_chain, done[0])

            def inverse_rms(name, col, n):
                dve.wait_ge(rms_ready[name], 1)
                link(nc.vector.reciprocal(rstd[:, col:col + n], rstd[:, col:col + n]))

            def permuted(tt):
                return HN[:, tt, :, :].rearrange("p k q -> p q k")

            def plain(v):
                return v.rearrange("p (q k) -> p q k", k=KC)

            def normalise(name, col):
                inverse_rms(name, col, TT)
                for tt in range(TT):
                    nc.vector.tensor_scalar(permuted(tt), plain(X[:, tt, :]), rstd[:, col + tt:col + tt + 1], None,
                                            ALU.mult).then_inc(rows[name], 1)

            def apply_gain(name, g, free=None, credits=0):
                for n in range(4):
                    tt, half = n // 2, n % 2
                    dve.wait_ge(turned[name], n + 1)
                    ks = slice(4 * half, 4 * half + 4)
                    ins = nc.vector.tensor_tensor(HT[:, ks, tt * P:(tt + 1) * P], PS[:, 4 + n, :].rearrange("p (k t) -> p k t", k=4),
                                                  gains[:, g, ks].unsqueeze(2).broadcast_to((P, 4, P)), ALU.mult)
                    ins.then_inc(hT_ready[name], 1)

            dve.wait_ge(consts, N_CONST)
            for n in range(2):
                dve.wait_ge(wsp_turned, n + 1)
                nc.vector.tensor_tensor(wspT[:, 4 * n:4 * n + 4, :], PS[:, n, :].rearrange("p (k t) -> p k t", k=4),
                                        upto[:, :].unsqueeze(1).broadcast_to((P, 4, P)), ALU.mult).then_inc(wspT_ready, 1)
            dve.wait_ge(wsp_turned, 3)
            nc.vector.tensor_copy(bspT, PS[:, 2, 0:HEADS]).then_inc(wspT_ready, 1)
            normalise("attn", 0)
            apply_gain("attn", G_ATTN)
            for n in range(2):
                dve.wait_ge(vug_ps, n + 1)
                nc.vector.tensor_copy(V[:, n, :], PS[:, 4 + n, :]).then_inc(v_ready, 1)
            inverse_rms("vg", 2, TT)
            for tt in range(TT):
                nc.vector.scalar_tensor_tensor(VG[:, tt, :], VG[:, tt, :], rstd[:, 2 + tt:3 + tt], sgn_g, ALU.mult,
                                               ALU.mult).then_inc(vg_ready, 1)

            def att_softplus(h):
                dve.wait_ge(att_ln, h + 1)
                s = att_s[:, h % 2, :]
                link(nc.vector.scalar_tensor_tensor(s, PS[:, h % 2, 0:3 * P], 0.0, att_e[:, h % 2, :], ALU.max, ALU.add))
                diagonal = s.rearrange("p (b q) -> p b q", b=3)[:, 0:3:2, :]
                nc.vector.tensor_tensor(diagonal, diagonal, before[:, :].unsqueeze(1).broadcast_to((P, 2, P)), ALU.mult).then_inc(att_sp, 1)

            def att_masked(h):
                dve.wait_ge(att_ps, h + 1)
                if h >= 2:
                    dve.wait_ge(av_done, h - 1)
                a, ps = att_a[:, h % 2, :], PS[:, h % 2, 0:3 * P]
                a3, ps3 = a.rearrange("p (b q) -> p b q", b=3), ps.rearrange("p (b q) -> p b q", b=3)
                nc.vector.tensor_scalar(a3[:, 1, :], ps3[:, 1, :], 0.0, None, ALU.min)
                nc.vector.scalar_tensor_tensor(a3[:, 0:3:2, :], ps3[:, 0:3:2, :], 0.0, maskbias[:, :].unsqueeze(1).broadcast_to((P, 2, P)),
                                               ALU.min, ALU.add).then_inc(att_x, 1)

            for h in range(HEADS):
                att_softplus(h)
                att_masked(h)
            dve.wait_ge(av_done, HEADS)
            for tt in range(TT):
                nc.vector.tensor_copy(ao[:, tt, :], PS[:, 2 + tt, :]).then_inc(ao_ready, 1)
            for tt in range(TT):
                dve.wait_ge(sgu_ps, tt + 1)
                link(nc.vector.tensor_tensor(so[:, tt, :].rearrange("p (h d) -> p h d", h=HEADS),
                                             PS[:, 4 + tt, :].rearrange("p (h d) -> p h d", h=HEADS),
                                             bspT.unsqueeze(2).broadcast_to((P, HEADS, HEAD_DIM)), ALU.add))
                nc.vector.tensor_tensor(so[:, tt, :], so[:, tt, :], U[:, tt, :], ALU.mult).then_inc(so_ready, 1)
            inverse_rms("mix", 4, 2 * TT)
            for tt in range(TT):
                for half_n, src in enumerate((ao, so)):
                    nc.vector.tensor_scalar(permuted(tt)[:, 64 * half_n:64 * half_n + 64, :], plain(src[:, tt, :]),
                                            rstd[:, 4 + 2 * half_n + tt:5 + 2 * half_n + tt], None, ALU.mult).then_inc(rows["mix"], 1)
            apply_gain("mix", G_MIX)
            for n in range(4):
                dve.wait_ge(out1_ps, n + 1)
                half = slice((n // 2) * BLOCK, (n // 2 + 1) * BLOCK)
                nc.vector.tensor_tensor(X[:, n % 2, half], X[:, n % 2, half], PS[:, n, :], ALU.add).then_inc(x_ready, 1)
            dve.wait_ge(x_ready, 4)
            normalise("ffn", 8)
            apply_gain("ffn", G_FFN)

            dve.wait_ge(router_loaded, 16 * 7)
            dve.wait_ge(logits_ps, 1)
            link(nc.vector.tensor_tensor(logit, PS[:, 0, 0:TT * 36].rearrange("p (a n) -> p a n", a=TT),
                                         b_router[:, :].unsqueeze(1).broadcast_to((P, TT, GROUPS + EXPERTS)), ALU.add))
            g_log = logit[:, :, 0:GROUPS]
            e_log = logit[:, :, GROUPS:].rearrange("p a (g e) -> p a g e", g=GROUPS)

            def over(v, n):
                return v.broadcast_to((P, TT, n))

            def first_max(values, n, top, onehot, tmp, places):
                link(nc.vector.tensor_reduce(top, values, AX_X, ALU.max))
                link(nc.vector.tensor_tensor(tmp, values, over(top, n), ALU.is_lt))
                link(nc.vector.scalar_tensor_tensor(tmp, tmp, 64.0, places, ALU.mult, ALU.add))
                link(nc.vector.tensor_reduce(place, tmp, AX_X, ALU.min))
                link(nc.vector.tensor_tensor(onehot, places, over(place, n), ALU.is_equal))

            places4 = iota_s[:, 0:GROUPS].unsqueeze(1).broadcast_to((P, TT, GROUPS))
            places8 = iota_s[:, 0:EXPERTS_PER_GROUP].unsqueeze(1).broadcast_to((P, TT, EXPERTS_PER_GROUP))
            g_hot, g_top, tmp4 = r_c[:, :, 0:4], r_c[:, :, 4:5], r_c[:, :, 8:12]
            top1, top2, place = r_c[:, :, 5:6], r_c[:, :, 6:7], r_c[:, :, 7:8]
            hot1, hot2, tmp8, e_sel, e_rest = (r_c[:, :, 16 + 8 * k:24 + 8 * k] for k in range(5))
            first_max(g_log, GROUPS, g_top, g_hot, tmp4, places4)
            link(nc.vector.tensor_tensor(r_b.rearrange("p a (g e) -> p a g e", g=GROUPS)[:, 0], e_log[:, 0],
                                         g_hot[:, 0].unsqueeze(2).broadcast_to((P, GROUPS, EXPERTS_PER_GROUP)), ALU.mult))
            link(nc.vector.tensor_tensor(r_b.rearrange("p a (g e) -> p a g e", g=GROUPS)[:, 1], e_log[:, 1],
                                         g_hot[:, 1].unsqueeze(2).broadcast_to((P, GROUPS, EXPERTS_PER_GROUP)), ALU.mult))
            link(nc.vector.tensor_reduce(e_sel, r_b.rearrange("p a (g e) -> p a e g", g=GROUPS), AX_X, ALU.add))
            first_max(e_sel, EXPERTS_PER_GROUP, top1, hot1, tmp8, places8)
            link(nc.vector.scalar_tensor_tensor(e_rest, hot1, -3e38, e_sel, ALU.mult, ALU.add))
            first_max(e_rest, EXPERTS_PER_GROUP, top2, hot2, tmp8, places8)
            link(nc.vector.tensor_tensor(r_a[:, :, 0:GROUPS], g_log, over(g_top, GROUPS), ALU.subtract))
            nc.vector.tensor_tensor(r_a[:, :, GROUPS:GROUPS + 1], top2, top1, ALU.subtract).then_inc(r_exp_in, 1)
            link(nc.vector.tensor_tensor(tmp8, hot1, hot2, ALU.add))
            for tt in range(TT):
                nc.vector.tensor_tensor(routed[:, tt, :].rearrange("p (g e) -> p g e", g=GROUPS),
                                        g_hot[:, tt].unsqueeze(2).broadcast_to((P, GROUPS, EXPERTS_PER_GROUP)),
                                        tmp8[:, tt].unsqueeze(1).broadcast_to((P, GROUPS, EXPERTS_PER_GROUP)), ALU.mult).then_inc(routed_ready, 1)
            dve.wait_ge(r_exp, 1)
            w1c, w2c = r_a[:, :, 8:9], r_a[:, :, 9:10]
            link(nc.vector.tensor_reduce(r_a[:, :, 6:7], r_a[:, :, 0:GROUPS], AX_X, ALU.add))
            link(nc.vector.tensor_scalar(r_a[:, :, 7:8], r_a[:, :, GROUPS:GROUPS + 1], 1.0, None, ALU.add))
            link(nc.vector.tensor_tensor(r_a[:, :, 6:7], r_a[:, :, 6:7], r_a[:, :, 7:8], ALU.mult))
            link(nc.vector.reciprocal(w1c, r_a[:, :, 6:7]))
            link(nc.vector.tensor_tensor(w2c, w1c, r_a[:, :, GROUPS:GROUPS + 1], ALU.mult))
            link(nc.vector.tensor_tensor(hot1, hot1, over(w1c, EXPERTS_PER_GROUP), ALU.mult))
            link(nc.vector.tensor_tensor(hot2, hot2, over(w2c, EXPERTS_PER_GROUP), ALU.mult))
            link(nc.vector.tensor_tensor(tmp8, hot1, hot2, ALU.add))
            for tt in range(TT):
                link(nc.vector.tensor_tensor(combine[:, tt, :].rearrange("p (g e) -> p g e", g=GROUPS),
                                             g_hot[:, tt].unsqueeze(2).broadcast_to((P, GROUPS, EXPERTS_PER_GROUP)),
                                             tmp8[:, tt].unsqueeze(1).broadcast_to((P, GROUPS, EXPERTS_PER_GROUP)), ALU.mult))
            dve.wait_ge(rank_ps, 1)
            ranks = PS[:, 1, 0:TT * EXPERTS].rearrange("p (a e) -> p a e", a=TT)
            link(nc.vector.scalar_tensor_tensor(rank, ranks, 1.0, routed, ALU.add, ALU.mult))
            link(nc.vector.tensor_scalar(rank, rank, -1.0, None, ALU.add))

            def select(first, e0, n_experts, w):
                rk, cb = rank[:, :, e0], combine[:, :, e0]
                for tt in range(TT):
                    one = sel[:, tt, 0:n_experts * SLOTS].rearrange("p (e s) -> p e s", e=n_experts)
                    two = selw[:, tt, 0:n_experts * SLOTS].rearrange("p (e s) -> p e s", e=n_experts)
                    link(nc.vector.tensor_tensor(one, rk[:, tt].unsqueeze(2).broadcast_to((P, n_experts, SLOTS)),
                                                 first.unsqueeze(1).broadcast_to((P, n_experts, SLOTS)), ALU.is_equal))
                    ins = nc.vector.tensor_tensor(two, one, cb[:, tt].unsqueeze(2).broadcast_to((P, n_experts, SLOTS)), ALU.mult)
                return ins

            select(iota_s[:, :], slice(0, PACK), PACK, None).then_inc(sel_ready, 1)

            def take_gathered(pack):
                for r in range(2):
                    dve.wait_ge(gath_ps, 2 * pack + (r + 1))
                    ks = slice(4 * r, 4 * r + 4)
                    nc.vector.tensor_tensor(XG[:, ks, :], PS[:, B_GATHER, :].rearrange("p (k s) -> p k s", k=4),
                                            gains[:, G_FFN, ks].unsqueeze(2).broadcast_to((P, 4, P)), ALU.mult).then_inc(xg_ready, 1)

            take_gathered(0)
            dve.sem_inc(comb_free, 2)
            dve.wait_ge(count_ps, 1)
            link(nc.vector.tensor_copy(extra_f[:, 0, :], PS[0:1, B_DOWN + 1, 0:EXPERTS]))
            link(nc.vector.tensor_scalar(extra_f[:, 1, :], extra_f[:, 0, :], float(SLOTS), None, ALU.is_gt))
            for k in range(2, T // SLOTS):
                link(nc.vector.scalar_tensor_tensor(extra_f[:, 1, :], extra_f[:, 0, :], float(SLOTS * k), extra_f[:, 1, :], ALU.is_gt, ALU.add))
            link(nc.vector.memset(extra_f[:, 2, :], 1.0))
            link(nc.vector.tensor_tensor_scan(extra_f[:, 3, :], extra_f[:, 2, :], extra_f[:, 1, :], 0.0, ALU.mult, ALU.add))
            sums = extra_f[:, 3, :]
            tiles = iota_s[0:1, 0:16]
            link(nc.vector.tensor_tensor(extra_cmp[:, :, :], sums.unsqueeze(1).broadcast_to((1, 16, EXPERTS)),
                                         tiles.unsqueeze(2).broadcast_to((1, 16, EXPERTS)), ALU.is_le))
            link(nc.vector.tensor_reduce(extra_row[:, 1, :], extra_cmp[:, :, :], AX_X, ALU.add))
            link(nc.vector.tensor_tensor(extra_cmp[:, :, :], extra_cmp[:, :, :], sums.unsqueeze(1).broadcast_to((1, 16, EXPERTS)), ALU.mult))
            link(nc.vector.tensor_reduce(extra_row[:, 2, :], extra_cmp[:, :, :], AX_X, ALU.max))
            link(nc.vector.tensor_tensor(extra_row[:, 2, :], tiles, extra_row[:, 2, :], ALU.subtract))
            link(nc.vector.tensor_scalar(extra_row[:, 2, :], extra_row[:, 2, :], 1.0, float(SLOTS), ALU.add, ALU.mult))
            link(nc.vector.tensor_scalar(extra_row[:, 0, :], tiles, 0.0, sums[:, EXPERTS - 1:EXPERTS], ALU.mult, ALU.add))
            nc.vector.tensor_copy(extra_i[:, :, :], extra_row[:, :, :]).then_inc(extra_ready, 1)

            def hidden(e, i):
                dve.wait_ge(silu_ready, e + 1)
                nc.vector.tensor_tensor(hid[:, i % 2, :], silu[:, i % 2, :], PS[:, B_GATE + i % 2, P:2 * P], ALU.mult).then_inc(hid_ready, 1)

            def collect(e, i):
                dve.wait_ge(down_done, e + 1)
                for j in range(2, 4):
                    ins = nc.vector.tensor_copy(Y[SLOTS * i:SLOTS * (i + 1), D_STRIP * j:D_STRIP * (j + 1)],
                                                PS[SLOTS * j:SLOTS * (j + 1), B_DOWN + i % 2, 0:D_STRIP])
                ins.then_inc(y_dve, 1)

            def add_pack(pack):
                for n in range(4):
                    half, tt = slice((n // 2) * BLOCK, (n // 2 + 1) * BLOCK), n % 2
                    dve.wait_ge(comb_ps, 4 * pack + (n + 2))
                    nc.vector.tensor_tensor(X[:, tt, half], X[:, tt, half], PS[:, B_COMB + n % 2, :], ALU.add).then_inc(comb_free, 1)

            def select_loop(base, first, e0, n_experts):
                rk, cb = rank[:, :, e0], combine[:, :, e0]
                for tt in range(TT):
                    one = sel[:, tt, 0:n_experts * SLOTS].rearrange("p (e s) -> p e s", e=n_experts)
                    nc.vector.tensor_tensor(one, rk[:, tt].unsqueeze(2).broadcast_to((P, n_experts, SLOTS)),
                                            first.unsqueeze(1).broadcast_to((P, n_experts, SLOTS)), ALU.is_equal).then_inc(sel_made, 1)
                dve.wait_ge(sel_made, base + TT)
                for tt in range(TT):
                    one = sel[:, tt, 0:n_experts * SLOTS].rearrange("p (e s) -> p e s", e=n_experts)
                    two = selw[:, tt, 0:n_experts * SLOTS].rearrange("p (e s) -> p e s", e=n_experts)
                    ins = nc.vector.tensor_tensor(two, one, cb[:, tt].unsqueeze(2).broadcast_to((P, n_experts, SLOTS)), ALU.mult)
                ins.then_inc(sel_ready, 1)

            with dve.Fori(0, PACKS - 1) as pack:
                e = PACK * pack
                hidden(e, 0)
                dve.wait_ge(gath_ps, 2 * pack + 2)
                dve.wait_ge(ct_ps, pack + 1)
                select_loop(TT * pack, iota_s[:, :], bass.ds(e + PACK, PACK), PACK)
                hidden(e + 1, 1)
                collect(e, 0)
                hidden(e + 2, 2)
                collect(e + 1, 1)
                hidden(e + 3, 3)
                collect(e + 2, 2)
                take_gathered(pack + 1)
                collect(e + 3, 3)
                add_pack(pack)
            for i in range(PACK):
                hidden(EXPERTS - PACK + i, i)
                collect(EXPERTS - PACK + i, i)
            add_pack(PACKS - 1)
            dve.wait_ge(gath_ps, 2 * PACKS)
            dve.wait_ge(ct_ps, PACKS)
            link(nc.vector.memset(sel, 0.0))
            link(nc.vector.memset(selw, 0.0))
            dve.wait_ge(first_ps, 1)
            nc.vector.tensor_copy(first_rank[:, :], PS[:, B_DOWN + 1, 0:16]).then_inc(first_ready, 1)
            dve.wait_ge(first_ready, 1)
            n_extra = dve.value_load(extra_i[0:1, 0, 0:1], min_val=0, max_val=EXTRA_MAX)
            with dve.Fori(0, EXTRA_MAX) as j:
                with dve.If(j < n_extra):
                    e = dve.value_load(extra_i[0:1, 1, bass.ds(j, 1)], min_val=0, max_val=EXPERTS - 1)
                    dve.wait_ge(gath_ps, 2 * j + 2 * PACKS)
                    dve.wait_ge(ct_ps, j + PACKS)
                    nc.vector.tensor_scalar(rank_iota[:, :], iota_s[:, :], first_rank[:, bass.ds(j, 1)], None, ALU.add).then_inc(slot_ranks, 1)
                    dve.wait_ge(slot_ranks, j + 1)
                    select_loop(TT * j + TT * (PACKS - 1), rank_iota[:, :], bass.ds(e, 1), 1)
                    take_gathered(j + PACKS)
                    hidden(j + EXPERTS, 0)
                    collect(j + EXPERTS, 0)
                    add_pack(j + PACKS)
            dve.wait_ge(comb_free, 4 * n_extra + (4 * PACKS + 2))
            dve.sem_inc(moe_done, 1)

            dve.wait_ge(tables_ready, 3)
            lam = VEC[:, V_LAM:V_LAM + RC]
            inverse_rms("first", 10, TT)
            for tt in range(TT):
                nc.vector.scalar_tensor_tensor(X[:, tt, :], X[:, tt, :], rstd[:, 10 + tt:11 + tt], g_first[:, :], ALU.mult, ALU.mult).then_inc(x2_ready, 1)
            dve.wait_ge(lam_ln, 1)
            link(nc.vector.tensor_scalar(sp8[:, 1, :], lam, -1.0, 0.0, ALU.mult, ALU.max))
            link(nc.vector.tensor_tensor(sp8[:, 1, :], sp8[:, 1, :], sp8[:, 0, :], ALU.add))
            link(nc.vector.tensor_scalar(sp8[:, 2, :], sp8[:, 1, :], LRU_C, None, ALU.mult))
            dve.wait_ge(x2_ready, TT)
            normalise("mix2", 12)
            apply_gain("mix2", G_MIX2)
            dve.wait_ge(hT_ready["mix2"], 4)
            dve.sem_inc(z_bank_free, 4)

            dve.wait_ge(ga_ready, 1)
            u = Z[:, Z_VA:Z_VA + 8, :]
            link(nc.vector.tensor_tensor(u, u, Z[:, Z_GA:Z_GA + 8, :], ALU.mult))
            with dve.Fori(0, KC // 2) as pair:
                for k in range(TAPS_A):
                    shift = k
                    tap = (TAPS_A - 1 - k) * KC
                    for i in range(2):
                        ch = 2 * pair + i
                        src = Z[:, bass.ds(ch + Z_VA, 1), 0:T - shift].rearrange("p a t -> p (a t)")
                        dst = CU[:, bass.ds(ch, 1), shift:T].rearrange("p a t -> p (a t)")
                        if k == 0:
                            ins = nc.vector.tensor_scalar(dst, src, CAW[:, bass.ds(ch + tap, 1)], VEC[:, bass.ds(ch + V_CAB, 1)], ALU.mult, ALU.add)
                        else:
                            dve.wait_ge(tap_step[i], TAPS_A * pair + k)
                            ins = nc.vector.scalar_tensor_tensor(dst, src, CAW[:, bass.ds(ch + tap, 1)], dst, ALU.mult, ALU.add)
                        ins.then_inc(tap_step[i], 1)
            dve.wait_ge(z_bank_free, 4 + Z_XB + RC)
            for pair in range(RC // 2):
                for k in range(TAPS_B):
                    for i in range(2):
                        n = 2 * pair + i
                        tap = (TAPS_B - 1 - k) * RC + n
                        src, dst = Z[:, Z_XB + n, 0:T - k], VB[:, n, k:T]
                        if k == 0:
                            ins = nc.vector.tensor_scalar(dst, src, CBW[:, tap:tap + 1], VEC[:, V_CBB + n:V_CBB + n + 1], ALU.mult, ALU.add)
                        else:
                            dve.wait_ge(short_step[i], TAPS_B * pair + k)
                            ins = nc.vector.scalar_tensor_tensor(dst, src, CBW[:, tap:tap + 1], dst, ALU.mult, ALU.add)
                        ins.then_inc(short_step[i], 1)
            for i in range(2):
                dve.wait_ge(short_step[i], TAPS_B * RC // 2)
                dve.wait_ge(tap_step[i], TAPS_A * KC // 2)
            dve.sem_inc(v2_ready, 1)
            for g in range(RG):
                rows_ = slice(3 * g, 3 * g + 3)
                dve.wait_ge(lru_gates, g + 1)
                link(nc.vector.tensor_tensor(VB[:, rows_, :], VB[:, rows_, :], IB[:, g % 2, :, :], ALU.mult))
                nc.vector.tensor_tensor(RB[:, rows_, :], RB[:, rows_, :], sp8[:, 2, rows_].unsqueeze(2).broadcast_to((P, 3, T)), ALU.mult).then_inc(lru_log, 1)
            dve.wait_ge(mean_ps, 1)
            nc.vector.tensor_tensor(CU, CU, PS[:, 4, 0:T].unsqueeze(1).broadcast_to((P, KC, T)), ALU.subtract).then_inc(centred, 1)
            for g in range(RG):
                rows_ = slice(3 * g, 3 * g + 3)
                th = Z[:, Z_XB + 3 * g:Z_XB + 3 * g + 3, :]
                dve.wait_ge(lru_exp, g + 1)
                link(nc.vector.tensor_tensor(RB[:, rows_, :], AB[:, rows_, :], AB[:, rows_, :], ALU.mult))
                nc.vector.scalar_tensor_tensor(th, RB[:, rows_, :], 1.0, th, ALU.add, ALU.mult).then_inc(lru_square, 1)
                dve.wait_ge(lru_root, g + 1)
                link(nc.vector.memset(th[:, :, 0:1], 1.0))
                link(nc.vector.tensor_tensor(VB[:, rows_, :], VB[:, rows_, :], th, ALU.mult))
                for n in range(3 * g, 3 * g + 3):
                    ins = nc.vector.tensor_tensor_scan(RB[:, n, :], AB[:, n, :], VB[:, n, :], 0.0, ALU.mult, ALU.add)
                    link(ins)
                if g == 0:
                    dve.wait_ge(gb_ready, 1)
                nc.vector.tensor_tensor(RB[:, rows_, :], RB[:, rows_, :], Z[:, Z_GB + 3 * g:Z_GB + 3 * g + 3, :], ALU.mult).then_inc(h_ready, 1)
            dve.wait_ge(var_ps, 1)
            inv = IB[:, 0, 0, :]
            nc.vector.tensor_scalar(inv, PS[:, 5, 0:T], EPS, None, ALU.add).then_inc(var_in, 1)
            dve.wait_ge(var_root, 1)
            link(nc.vector.reciprocal(inv, inv))
            nc.vector.tensor_tensor(CU, CU, inv.unsqueeze(1).broadcast_to((P, KC, T)), ALU.mult).then_inc(scaled, 1)
            dve.wait_ge(sab_ready, 1)
            for n in range(KC):
                dve.wait_ge(y_ps, n + 1)
                zb = Z[:, Z_SB + n, :]
                nc.vector.tensor_tensor(zb, zb, PS[:, 6 + n % 2, 0:T], ALU.mult).then_inc(y_bank_free, 1)
            dve.wait_ge(y_bank_free, KC)
            for n in range(KC):
                dve.wait_ge(y_ps, KC + n + 1)
                za = Z[:, Z_SA + n, :]
                nc.vector.tensor_tensor(za, za, PS[:, 6 + n % 2, 0:T], ALU.mult).then_inc(y_bank_free, 1)
                dve.wait_ge(y_bank_free, KC + n + 1)
                nc.vector.tensor_tensor(za, za, Z[:, Z_SB + n, :], ALU.add).then_inc(m_ready, 1)
            for n in range(4):
                dve.wait_ge(o_ps, n + 1)
                half = slice((n // 2) * BLOCK, (n // 2 + 1) * BLOCK)
                nc.vector.tensor_tensor(X[:, n % 2, half], X[:, n % 2, half], PS[:, n, :], ALU.add).then_inc(x3_ready, 1)
            dve.wait_ge(x3_ready, 4)
            normalise("mlp2", 14)
            apply_gain("mlp2", G_MLP2)
            dve.wait_ge(hT_ready["mlp2"], 4)
            dve.sem_inc(f_bank_free, 4)
            with dve.Fori(0, 2) as half_n:
                for b in range(4):
                    dve.wait_ge(f_bank_free, 16 * half_n + (4 * b + 8))
                    f4 = FT[:, 4 * b:4 * b + 4, :]
                    nc.vector.tensor_tensor(f4, f4, f4, ALU.mult).then_inc(f_ready, 1)
            for n in range(4):
                dve.wait_ge(mlp_ps, 1)
                half = slice((n % 2) * BLOCK, (n % 2 + 1) * BLOCK)
                nc.vector.tensor_copy(X[:, n // 2, half], PS[:, 2 * (n % 2) + n // 2, :]).then_inc(x4_ready, 1)
            inverse_rms("last", 0, TT)
            for tt in range(TT):
                nc.vector.scalar_tensor_tensor(fin[:, tt, :], X[:, tt, :], rstd[:, tt:tt + 1], g_last[:, :], ALU.mult, ALU.mult).then_inc(fin_ready, 1)

        @block.tensor
        def _(pe):
            def turn_rows(name):
                for n in range(4):
                    tt, half = n // 2, n % 2
                    if n % 2 == 0:
                        pe.wait_ge(rows[name], (tt + 1) * (2 if name == "mix" else 1))
                    for k in range(4):
                        ins = nc.tensor.transpose(PS[:, 4 + n, k * P:(k + 1) * P], HN[:, tt, 4 * half + k, :], ident[:, :])
                    ins.then_inc(turned[name], 1)

            pe.wait_ge(consts, N_CONST)
            pe.wait_ge(small_loaded, 16 * N_SMALL)
            for n in range(2):
                for k in range(4):
                    ins = nc.tensor.transpose(PS[:, n, k * P:(k + 1) * P], wsp[:, 4 * n + k, :], ident[:, :])
                ins.then_inc(wsp_turned, 1)
            nc.tensor.transpose(PS[:, 2, 0:HEADS], bsp[0:HEADS], ident[0:HEADS, 0:HEADS]).then_inc(wsp_turned, 1)
            turn_rows("attn")
            pe.wait_ge(hT_ready["attn"], 4)
            pe.wait_ge(wspT_ready, 3)
            for n in range(8):
                if n % 4 == 0:
                    pe.wait_ge(loaded[n // 4], pre_count(n // 4))
                if n >= 4:
                    pe.wait_ge(qk_ready, n - 3)
                for k in range(KC):
                    ins = nc.tensor.matmul(PS[:, n % 4, 0:T], chunked(n // 4, BLOCK)[:, k, (n % 4) * P:(n % 4 + 1) * P],
                                           HT[:, k, :], start=k == 0, stop=k == KC - 1)
                ins.then_inc(qk_ps, 1)
            for n in range(6):
                b, tt = 2 + n // 2, n % 2
                pe.wait_ge(loaded[b], pre_count(b))
                if n >= 4:
                    pe.wait_ge(v_ready, n - 3)
                for k in range(KC):
                    ins = nc.tensor.matmul(PS[:, 4 + n % 4, :], HT[:, k, tt * P:(tt + 1) * P], chunked(b, BLOCK)[:, k, :],
                                           start=k == 0, stop=k == KC - 1)
                ins.then_inc(vug_ps, 1)

            def scores(h):
                if h >= 2:
                    pe.wait_ge(att_x, h - 1)
                k, q = kT[:, h // 2, :], qT[:, h, :]
                nc.tensor.matmul(PS[:, h % 2, 0:T], k[:, 0:P], q, start=True, stop=False, skip_group_check=True)
                nc.tensor.matmul(PS[:, h % 2, T:T + P], k[:, P:T], q[:, P:T], start=False, stop=False,
                                 skip_group_check=True).then_inc(score_ps, 1)

            def later_keys(h):
                pe.wait_ge(att_sp, h + 1)
                s = att_s[:, h % 2, :]
                nc.tensor.matmul(PS[:, h % 2, 0:T], tri_neg[:, :], s[:, 0:T], start=False, stop=False, skip_group_check=True)
                nc.tensor.matmul(PS[:, h % 2, P:T], neg_ones[:, :], s[:, T:T + P], start=False, stop=False, skip_group_check=True)
                nc.tensor.matmul(PS[:, h % 2, T:T + P], tri_neg[:, :], s[:, T:T + P], start=False, stop=True,
                                 skip_group_check=True).then_inc(att_ps, 1)

            def weighted_values(h):
                pe.wait_ge(att_exp, h + 1)
                a, cols = att_a[:, h % 2, :], slice(h * HEAD_DIM, (h + 1) * HEAD_DIM)
                nc.tensor.matmul(PS[:, 2, cols], a[:, 0:P], V[:, 0, cols], start=True, stop=True)
                nc.tensor.matmul(PS[:, 3, cols], a[:, P:T], V[:, 0, cols], start=True, stop=False)
                nc.tensor.matmul(PS[:, 3, cols], a[:, T:T + P], V[:, 1, cols], start=False, stop=True).then_inc(av_done, 1)

            pe.wait_ge(qk_ready, 8)
            pe.wait_ge(v_ready, TT)
            scores(0)
            for h in range(HEADS):
                if h + 1 < HEADS:
                    scores(h + 1)
                later_keys(h)
                if h >= 1:
                    weighted_values(h - 1)
            weighted_values(HEADS - 1)
            pe.wait_ge(gelu_ready, 4)
            for tt in range(TT):
                pe.wait_ge(vg_ready, tt + 1)
                for h in range(HEADS):
                    cols = slice(h * HEAD_DIM, (h + 1) * HEAD_DIM)
                    ins = nc.tensor.matmul(PS[:, 4 + tt, cols], wspT[:, h, :], VG[:, tt, cols], start=True, stop=True)
                ins.then_inc(sgu_ps, 1)
            pe.wait_ge(table_loaded, 16 * 13)
            at = 0
            for raw, n in ((vec_raw, P), (caw_raw[:, 0, :], P), (caw_raw[:, 1, :], TAPS_A * KC - P), (cbw_raw, TAPS_B * RC)):
                ins = nc.tensor.transpose(PS[:, 0, at:at + n], raw[0:n], ident[0:n, 0:n])
                at += n
            ins.then_inc(tables_turned, 1)
            turn_rows("mix")
            pe.wait_ge(hT_ready["mix"], 4)
            pe.wait_ge(tables_ready, 3)
            for n in range(4):
                half, tt = n // 2, n % 2
                w = IN1_BLOCKS + half
                pe.wait_ge(loaded[w % RING], pre_count(w))
                for k in range(KC):
                    ins = nc.tensor.matmul(PS[:, n, :], HT[:, k, tt * P:(tt + 1) * P], chunked(w % RING, BLOCK)[:, k, :],
                                           start=k == 0, stop=k == KC - 1)
                ins.then_inc(out1_ps, 1)
            turn_rows("ffn")
            pe.wait_ge(hT_ready["ffn"], 4)
            pe.wait_ge(router_loaded, 16 * 7)
            for tt in range(TT):
                at = tt * (GROUPS + EXPERTS)
                for k in range(KC):
                    nc.tensor.matmul(PS[:, 0, at:at + GROUPS], HT[:, k, tt * P:(tt + 1) * P], wr_group[:, k, :],
                                     start=k == 0, stop=k == KC - 1)
                for k in range(KC):
                    ins = nc.tensor.matmul(PS[:, 0, at + GROUPS:at + GROUPS + EXPERTS].rearrange("p (g e) -> p g e", g=GROUPS),
                                           HT[:, k, tt * P:(tt + 1) * P], wr_expert[:, :, k, :], start=k == 0, stop=k == KC - 1)
            ins.then_inc(logits_ps, 1)
            pe.wait_ge(routed_ready, TT)
            nc.tensor.matmul(PS[:, 1, 0:EXPERTS], before[:, :], routed[:, 0, :], start=True, stop=True)
            nc.tensor.matmul(PS[:, 1, EXPERTS:2 * EXPERTS], ones[:, :], routed[:, 0, :], start=True, stop=False)
            nc.tensor.matmul(PS[:, 1, EXPERTS:2 * EXPERTS], before[:, :], routed[:, 1, :], start=False, stop=True).then_inc(rank_ps, 1)
            nc.tensor.matmul(PS[0:1, B_DOWN + 1, 0:EXPERTS], ones[:, 0:1], routed[:, 0, :], start=True, stop=False)
            nc.tensor.matmul(PS[0:1, B_DOWN + 1, 0:EXPERTS], ones[:, 0:1], routed[:, 1, :], start=False, stop=True).then_inc(count_ps, 1)

            def gather(pack):
                pe.wait_ge(sel_ready, pack + 1)
                pe.wait_ge(ct_ready, pack)
                for r in range(2):
                    pe.wait_ge(xg_ready, 2 * pack + r)
                    for k in range(4):
                        for tt in range(TT):
                            ins = nc.tensor.matmul(PS[:, B_GATHER, k * P:(k + 1) * P], HN[:, tt, 4 * r + k, :], sel[:, tt, :],
                                                   start=tt == 0, stop=tt == TT - 1)
                    ins.then_inc(gath_ps, 1)
                pe.wait_ge(xg_ready, 2 * pack + 2)
                for tt in range(TT):
                    ins = nc.tensor.transpose(PS[:, B_GATHER, tt * P:(tt + 1) * P], selw[:, tt, :], ident[:, :])
                ins.then_inc(ct_ps, 1)

            def gate_up(s, i):
                w = mem[:, s * SLOT_FLOATS:(s + 2) * SLOT_FLOATS].rearrange("p (w k n) -> p w k n", w=2, k=KC)
                for k in range(KC):
                    for j in range(STRIPS):
                        ins = nc.tensor.matmul(PS[SLOTS * j:SLOTS * (j + 1), B_GATE + i % 2, 0:2 * F_STRIP].rearrange("p (w n) -> p w n", w=2),
                                               XG[:, k, SLOTS * i:SLOTS * (i + 1)], w[:, :, k, F_STRIP * j:F_STRIP * (j + 1)],
                                               start=k == 0, stop=k == KC - 1, tile_position=(0, SLOTS * j))
                ins.then_inc(gu_done, 1)

            def turn_hidden(e, i):
                pe.wait_ge(hid_ready, e + 1)
                nc.tensor.transpose(PS[:, B_TURN, 0:P], hid[:, i % 2, :], ident[:, :]).then_inc(hidT_ps, 1)

            def down(e, s, i):
                pe.wait_ge(hidT_ready, e + 1)
                w = chunked(s, D)
                for k in range(STRIPS):
                    for j in range(STRIPS):
                        ins = nc.tensor.matmul(PS[SLOTS * j:SLOTS * (j + 1), B_DOWN + i % 2, 0:D_STRIP],
                                               hidT[:, i % 2, SLOTS * k:SLOTS * (k + 1)], w[:, k, D_STRIP * j:D_STRIP * (j + 1)],
                                               start=k == 0, stop=k == STRIPS - 1, tile_position=(0, SLOTS * j))
                ins.then_inc(down_done, 1)

            def combine_pack(pack, y_count):
                pe.wait_ge(y_act, y_count)
                pe.wait_ge(y_dve, y_count)
                pe.wait_ge(ct_ready, pack + 1)
                for n in range(4):
                    half, tt = n // 2, n % 2
                    pe.wait_ge(comb_free, 4 * pack + (n + 1))
                    nc.tensor.matmul(PS[:, B_COMB + n % 2, :], CT[:, tt * P:(tt + 1) * P], Y[:, half * BLOCK:(half + 1) * BLOCK],
                                     start=True, stop=True).then_inc(comb_ps, 1)

            def expert_slots(i):
                return [(PRE + 3 * i + part) % RING for part in range(3)]

            def expert_gate_up(pack, i):
                s = expert_slots(i)
                if i == 0:
                    pe.wait_ge(xg_ready, 2 * pack + 2)
                for part in range(2):
                    pe.wait_ge(loaded[s[part]], 32 * pack + 16 * ((PRE + 3 * i + part) // RING + 1))
                gate_up(s[0], i)

            def expert_down(pack, i):
                turn_hidden(PACK * pack + i, i)
                s = expert_slots(i)[2]
                pe.wait_ge(loaded[s], 32 * pack + 16 * ((PRE + 3 * i + 2) // RING + 1))
                pe.wait_ge(extra_ready, 1)
                down(PACK * pack + i, s, i)

            def residual_first():
                for n in range(4):
                    half, tt = n // 2, n % 2
                    nc.tensor.matmul(PS[:, n, :], ident[:, :], X[:, tt, half * BLOCK:(half + 1) * BLOCK], start=True, stop=False,
                                     skip_group_check=True)

            gather(0)
            pe.sem_inc(comb_ps, 1)
            with pe.Fori(0, PACKS - 1) as pack:
                expert_gate_up(pack, 0)
                for i in range(PACK):
                    if i + 1 < PACK:
                        expert_gate_up(pack, i + 1)
                    else:
                        gather(pack + 1)
                    expert_down(pack, i)
                combine_pack(pack, PACK * pack + PACK)
            expert_gate_up(PACKS - 1, 0)
            for i in range(PACK):
                if i + 1 < PACK:
                    expert_gate_up(PACKS - 1, i + 1)
                expert_down(PACKS - 1, i)
            combine_pack(PACKS - 1, EXPERTS)
            pe.wait_ge(extra_ready, 1)
            nc.tensor.matmul(PS[:, B_DOWN + 1, 0:16], ones[0:1, :], extra_row[0:1, 2, :], start=True, stop=True).then_inc(first_ps, 1)
            n_extra = pe.value_load(extra_i[0:1, 0, 0:1], min_val=0, max_val=EXTRA_MAX)
            pe.wait_ge(first_ready, 1)
            with pe.Fori(0, EXTRA_MAX) as j:
                with pe.If(j < n_extra):
                    gather(j + PACKS)
                    for part in range(2):
                        pe.wait_ge(extra_loaded[part], 16 * j + 16)
                    pe.wait_ge(xg_ready, 2 * j + (2 * PACKS + 2))
                    gate_up(1, 0)
                    turn_hidden(j + EXPERTS, 0)
                    pe.wait_ge(extra_loaded[2], 16 * j + 16)
                    down(j + EXPERTS, 3, 0)
                    combine_pack(j + PACKS, j + (EXPERTS + 1))

            turn_rows("mix2")
            pe.wait_ge(hT_ready["mix2"], 4)

            def z_block_pair(pair):
                for b in range(2):
                    pe.wait_ge(b2_loaded[1 + b], 16 * pair + 16)
                    for i in range(4):
                        pe.wait_ge(z_bank_free, 8 * pair + (4 * b + i + 1))
                        for k in range(KC):
                            ins = nc.tensor.matmul(PS[:, i, 0:T], chunked(1 + b, BLOCK)[:, k, i * P:(i + 1) * P], HT[:, k, :],
                                                   start=k == 0, stop=k == KC - 1)
                        ins.then_inc(z_ps, 1)

            with pe.Fori(0, 6) as pair:
                z_block_pair(pair)
            pe.wait_ge(bd_loaded, 16 * N_BD)
            pe.wait_ge(v2_ready, 1)
            for g in range(RG):
                if g >= 1:
                    pe.wait_ge(lru_gates, g)
                for bd, bank in ((BDA, 4), (BDX, 6)):
                    for o in range(3):
                        dst = PS[:, bank + o // 2, (o % 2) * T:(o % 2 + 1) * T]
                        parts = [(o, 32 * o, 0, P)]
                        parts += [[(1, 0, 96, 32)], [(0, P, 0, 64), (2, 0, 64, 64)], [(1, 160, 0, 32)]][o]
                        for n, (r, c0, p0, m) in enumerate(parts):
                            ins = nc.tensor.matmul(dst[p0:p0 + m], bd[:, g, r, c0:c0 + m], VB[:, 3 * g + r, :], start=n == 0,
                                                   stop=n == len(parts) - 1, skip_group_check=True)
                ins.then_inc(lru_ps, 1)
            pe.wait_ge(lru_gates, RG)
            for k in range(KC):
                ins = nc.tensor.matmul(PS[:, 4, 0:T], mean_ones[:, :], CU[:, k, :], start=k == 0, stop=k == KC - 1)
            ins.then_inc(mean_ps, 1)
            z_block_pair(6)
            pe.wait_ge(sq_ready, 1)
            for k in range(KC):
                ins = nc.tensor.matmul(PS[:, 5, 0:T], mean_ones[:, :], Z[:, Z_GA + k, :], start=k == 0, stop=k == KC - 1)
            ins.then_inc(var_ps, 1)
            pe.wait_ge(h_ready, RG)
            for n in range(KC):
                if n % 2 == 0:
                    pe.wait_ge(b2_loaded[b2[L_B + n // 2][1]], b2_arrivals(L_B + n // 2))
                if n >= 2:
                    pe.wait_ge(y_bank_free, n - 1)
                w = chunked(b2[L_B + n // 2][1], 256)
                for k in range(RC):
                    ins = nc.tensor.matmul(PS[:, 6 + n % 2, 0:T], w[:, k, (n % 2) * P:(n % 2 + 1) * P], RB[:, k, :],
                                           start=k == 0, stop=k == RC - 1)
                ins.then_inc(y_ps, 1)
            pe.wait_ge(a_ready, KC)
            for n in range(KC):
                if n % 4 == 0:
                    pe.wait_ge(b2_loaded[b2[L_A + n // 4][1]], b2_arrivals(L_A + n // 4))
                pe.wait_ge(y_bank_free, KC + n - 1)
                w = chunked(b2[L_A + n // 4][1], BLOCK)
                for k in range(KC):
                    ins = nc.tensor.matmul(PS[:, 6 + n % 2, 0:T], w[:, k, (n % 4) * P:(n % 4 + 1) * P], CU[:, k, :],
                                           start=k == 0, stop=k == KC - 1)
                ins.then_inc(y_ps, 1)
            pe.wait_ge(m_ready, KC)
            for n in range(4):
                half, tt = n // 2, n % 2
                pe.wait_ge(b2_loaded[b2[L_O + half][1]], b2_arrivals(L_O + half))
                w = chunked(b2[L_O + half][1], BLOCK)
                for k in range(KC):
                    ins = nc.tensor.matmul(PS[:, n, :], Z[:, Z_SA + k, tt * P:(tt + 1) * P], w[:, k, :], start=k == 0, stop=k == KC - 1)
                ins.then_inc(o_ps, 1)
            turn_rows("mlp2")
            pe.wait_ge(hT_ready["mlp2"], 4)
            residual_first()
            with pe.Fori(0, 2) as half:
                for b in range(4):
                    s = b2[L_F + b][1]
                    pe.wait_ge(b2_loaded[s], 32 * half + b2_arrivals(L_F + b))
                    for i in range(4):
                        pe.wait_ge(f_bank_free, 16 * half + (4 * b + i + 1))
                        for k in range(KC):
                            ins = nc.tensor.matmul(PS[:, 4 + i, 0:T], chunked(s, BLOCK)[:, k, i * P:(i + 1) * P], HT[:, k, :],
                                                   start=k == 0, stop=k == KC - 1)
                        ins.then_inc(f_ps, 1)
                for b in range(4):
                    s = b2[L_F + 4 + b][1]
                    pe.wait_ge(b2_loaded[s], 32 * half + b2_arrivals(L_F + 4 + b))
                    pe.wait_ge(f_ready, 4 * half + (b + 1))
                    for k in range(4):
                        for n in range(4):
                            h, tt = n // 2, n % 2
                            ins = nc.tensor.matmul(PS[:, n, :], FT[:, 4 * b + k, tt * P:(tt + 1) * P],
                                                   chunked(s, D)[:, k, h * BLOCK:(h + 1) * BLOCK], start=False, stop=False, skip_group_check=True)
                    ins.then_inc(w2_used, 1)
            nc.tensor.matmul(PS[:, 3, 0:2], zeros[:, :], zeros[:, 0:2], start=False, stop=True, skip_group_check=True).then_inc(mlp_ps, 1)


_INS = [
    "x", "attn_norm_g", "w_in", "sg_norm_g", "w_spatial", "b_spatial", "sb_out_norm_g", "sg_out_norm_g", "w_out",
    "ffn_norm_g", "w_router_group", "b_router_group", "w_router_expert", "b_router_expert", "w_gate", "w_up",
    "w_down", "final_norm_g", "g_mix_2", "w_in_2", "b_in_2", "conv_a_w_2", "conv_a_b_2", "ln_g_2", "ln_b_2",
    "w_a_out_2", "conv_b_w_2", "conv_b_b_2", "w_rg_a_2", "b_rg_a_2", "w_rg_x_2", "b_rg_x_2", "lam_2", "w_b_out_2",
    "w_o_2", "g_mlp_2", "w_1_2", "w_2_2", "g_final_2",
]


def kernel(**inputs):
    import numpy as _np
    import concourse.bacc as _bacc
    from concourse import mybir as _mybir
    from concourse.bass_utils import run_bass_kernel_spmd as _run

    nc = _bacc.Bacc("TRN2", target_bir_lowering=False, num_devices=1)
    arrays, args = {}, {}
    for name in _INS:
        a = _np.ascontiguousarray(inputs[name])
        arrays[f"in_{name}"] = a
        args[name] = nc.dram_tensor(f"in_{name}", a.shape, _mybir.dt.from_np(a.dtype), kind="ExternalInput").ap()
    out = nc.dram_tensor("out", (1, T, D), _mybir.dt.float32, kind="ExternalOutput").ap()
    build(nc, args, out)
    r = _run(nc, [arrays], core_ids=[0])
    return r.results[0]["out"]
```

```python
from contextlib import ExitStack

import numpy as np

import concourse.bass as bass
from concourse import mybir

F32 = mybir.dt.float32
F32R = mybir.dt.float32r
I32 = mybir.dt.int32
ALU = mybir.AluOpType
ACT = mybir.ActivationFunctionType
AX_X = mybir.AxisListType.X

P = 128
T = 256
TT = T // P
D = 1024
KC = D // P
EPS = 1e-6
HEADS, HEAD_DIM = 8, 64
SB = HEADS * HEAD_DIM
GROUPS, EXPERTS_PER_GROUP = 4, 8
EXPERTS = GROUPS * EXPERTS_PER_GROUP
D_EXPERT = 512
SLOTS = 32
STRIPS = P // SLOTS
PACK = 4
PACKS = EXPERTS // PACK
F_STRIP = D_EXPERT // STRIPS
D_STRIP = D // STRIPS
EXTRA_MAX = 2 * T // SLOTS - 1
BLOCK = 512
SLOT_FLOATS = KC * BLOCK
RING = 6
IN1_BLOCKS = 5
OUT1_BLOCKS = 2
PRE = IN1_BLOCKS + OUT1_BLOCKS
D_RNN, RNN_HEAD = 1536, 96
RC = D_RNN // P
RG = 4
TAPS_A, TAPS_B = 31, 4
LRU_C = 8.0
D_FF = 4 * D
FC = D_FF // P
HALF = BLOCK // 2
HALF_FLOATS = KC * HALF
C_VA, C_GA, C_XB, C_GB, C_SA, C_SB, ZC = 0, 8, 16, 28, 40, 48, 56
IN2_ORDER = [4, 0] + list(range(8, 14)) + [5, 1, 6, 2, 7, 3] + list(range(14, 28))
IN2_HALVES = len(IN2_ORDER)
IN2_GROUP = 4
LRU_AFTER = 3
RAW, HI = 4, 2
Z_GA, Z_XB, Z_GB, Z_SA, Z_SB = (c - C_GA for c in (C_GA, C_XB, C_GB, C_SA, C_SB))
PAD = TAPS_A - 1
TAP_ROUND = 6
ACT_EXP, ACT_ROOT = 13, 20
PE_MEAN, PE_VAR = 3, 5
MASKED = -1e30
B_COMB, B_GATE, B_DOWN, B_TURN, B_GATHER = 0, 2, 4, 6, 7

V_BIN, V_CAB, V_LNG, V_LNB, V_CBB, V_BRA, V_BRX, V_LAM = 0, 56, 64, 72, 80, 92, 104, 116


def build(nc, A, out):
    ctx = ExitStack()
    with ctx:
        def sb(name, shape, dt=F32):
            return ctx.enter_context(nc.sbuf_tensor(name, shape, dt))

        def sem(name):
            return ctx.enter_context(nc.semaphore(name))

        ARENA = 17664
        mem = sb("mem", [P, RING * SLOT_FLOATS + ARENA])
        mem_at = nc.sbuf_base - 4 * (RING * SLOT_FLOATS + ARENA)
        slot = [mem[:, s * SLOT_FLOATS:(s + 1) * SLOT_FLOATS] for s in range(RING)]

        def carver(start, end):
            at = [start]

            def carve(*shape):
                n = int(np.prod(shape))
                view = mem[:, at[0]:at[0] + n]
                at[0] += n
                assert at[0] <= end, (at[0], end)
                if len(shape) == 2:
                    view = view.rearrange("p (a b) -> p a b", a=shape[0])
                if len(shape) == 3:
                    view = view.rearrange("p (a b c) -> p a b c", a=shape[0], b=shape[1])
                return view
            return carve

        a0 = RING * SLOT_FLOATS
        aend = a0 + ARENA
        X = sb("X", [P, TT, D])
        HN = sb("HN", [P, TT, KC, P])
        hn_at = nc.sbuf_base - 4 * TT * D
        HT = sb("HT", [P, KC, T])
        ht_at = nc.sbuf_base - 4 * TT * D
        ident = sb("ident", [P, P])
        tri_neg = sb("tri_neg", [P, P])
        neg_ones = sb("neg_ones", [P, P])
        ones = sb("ones", [P, P])
        mean_ones = sb("mean_ones", [P, P])
        before = sb("before", [P, P])
        upto = sb("upto", [P, P])
        maskbias = sb("maskbias", [P, P])
        eps = sb("eps", [P, 1])
        zeros = sb("zeros", [P, P])
        iota_i = sb("iota_i", [P, SLOTS], I32)
        iota_s = sb("iota_s", [P, SLOTS])
        gains = sb("gains", [P, 5, KC])
        G_ATTN, G_MIX, G_FFN, G_MIX2, G_MLP2 = range(5)
        VEC = sb("VEC", [P, P])
        CAW = sb("CAW", [P, TAPS_A * KC])
        CBW = sb("CBW", [P, TAPS_B * RC])
        wr_group = sb("wr_group", [P, KC, GROUPS])
        wr_expert = sb("wr_expert", [P, GROUPS, KC, EXPERTS_PER_GROUP])
        b_router = sb("b_router", [P, GROUPS + EXPERTS])
        g_first = sb("g_first", [P, D])
        g_last = sb("g_last", [P, D])
        ss = sb("ss", [P, 16])
        rstd = sb("rstd", [P, 16])
        sp8 = sb("sp8", [P, 4, RC])
        extra_row = sb("extra_row", [1, 3, 16])
        extra_i = sb("extra_i", [1, 3, 16], I32)
        first_rank = sb("first_rank", [P, 16])
        rank_iota = sb("rank_iota", [P, SLOTS])
        PS = ctx.enter_context(nc.psum_tensor("PS", [P, 8, 512], F32))

        c = carver(a0, aend)
        square = c(D)
        qT, kT = c(HEADS, T), c(4, T)
        V, U, VG = c(TT, SB), c(TT, SB), c(TT, SB)
        wsp, wspT = c(HEADS, P), c(HEADS, P)
        ao, so = c(TT, SB), c(TT, SB)
        att_e, att_s, att_a = c(2, 3 * P), c(2, 3 * P), c(2, 3 * P)
        sgn_g = c(SB)
        bsp, bspT = c(P), c(HEADS)
        vec_raw, caw_raw, cbw_raw = c(P), c(2, P), c(P)
        c = carver(a0 + D, aend)
        logit = c(TT, GROUPS + EXPERTS)
        r_a, r_b, r_c = c(TT, 16), c(TT, EXPERTS), c(TT, 64)
        routed, combine, rank = c(TT, EXPERTS), c(TT, EXPERTS), c(TT, EXPERTS)
        sel, selw = c(TT, P), c(TT, P)
        XG = c(KC, P)
        CT = c(T)
        silu, hid, hidT = c(2, P), c(2, P), c(2, P)
        Y = c(D)
        extra_f, extra_cmp = c(4, EXPERTS)[0:1], c(16, EXPERTS)[0:1]
        b2_at = 4 * SLOT_FLOATS
        c = carver(b2_at, aend)
        Z = c(ZC - KC, T)
        UP = c(KC, PAD + T)
        CU = c(KC, T)
        VB, RB, AB = c(RC, T), c(RC, T), c(RC, T)
        late_end = b2_at + (ZC - KC) * T + KC * (PAD + T) + KC * T + 3 * RC * T
        BD = RG * 3 * 192
        BDA = AB.rearrange("p a t -> p (a t)")[:, 0:BD].rearrange("p (g r n) -> p g r n", g=RG, r=3)
        BDX = slot[0][:, 0:BD].rearrange("p (g r n) -> p g r n", g=RG, r=3)
        inv_ln = AB[:, 0, :]
        IB = slot[0][:, BD:BD + 2 * 3 * T].rearrange("p (a b c) -> p a b c", a=2, b=3)
        c = carver(b2_at, b2_at + 2 * FC // 2 * T)
        FT = c(FC // 2, T)
        fin = FT.rearrange("p a t -> p (a t)")[:, 0:TT * D].rearrange("p (a d) -> p a d", a=TT)

        def parts(name, at, *shape):
            return nc.alloc_sbuf_tensor_at(name, [P] + list(shape), F32R, offset=at)

        ring_rest = [parts(f"ring_rest{s}", mem_at + 4 * s * SLOT_FLOATS, SLOT_FLOATS) for s in range(4)]
        z_hi = parts("z_hi", mem_at + 4 * 3 * SLOT_FLOATS, HI, HALF_FLOATS)
        HT_hi = parts("HT_hi", hn_at, TT, KC, P)
        HT_rest = parts("HT_rest", ht_at, KC, T)
        FT_rest = parts("FT_rest", mem_at + 4 * b2_at, FC // 2, T)
        FT_hi = parts("FT_hi", mem_at + 4 * (b2_at + FC // 2 * T), FC // 2, T)
        mlp_hi_at = [late_end - 2 * SLOT_FLOATS, late_end - SLOT_FLOATS, b2_at + (ZC - KC) * T, b2_at + Z_SA * T]
        mlp_hi = [parts(f"mlp_hi{n}", mem_at + 4 * at, SLOT_FLOATS) for n, at in enumerate(mlp_hi_at)]

        def z_raw(n):
            at = SLOT_FLOATS + (n % RAW) * HALF_FLOATS
            return mem[:, at:at + HALF_FLOATS]

        def z_rest(n):
            at = (n % RAW) * HALF_FLOATS
            return ring_rest[1 + at // SLOT_FLOATS][:, at % SLOT_FLOATS:at % SLOT_FLOATS + HALF_FLOATS]

        x_loaded, gain_loaded, small_loaded = sem("x_loaded"), sem("gain_loaded"), sem("small_loaded")
        router_loaded, table_loaded = sem("router_loaded"), sem("table_loaded")
        bd_loaded = sem("bd_loaded")
        loaded = [sem(f"loaded{s}") for s in range(RING)]
        extra_loaded = [sem(f"extra_loaded{s}") for s in range(3)]
        raw_loaded = [sem(f"raw_loaded{s}") for s in range(RAW)]
        late_loaded = [sem(f"late_loaded{s}") for s in range(4)]
        z_hi_ready, z_rest_ready = sem("z_hi_ready"), sem("z_rest_ready")
        hT_hi_ready = {n: sem(f"hT_hi_ready_{n}") for n in ("mix2", "mlp2")}
        hT_rest_ready = {n: sem(f"hT_rest_ready_{n}") for n in ("mix2", "mlp2")}
        mlp_hi_ready, mlp_rest_ready = sem("mlp_hi_ready"), sem("mlp_rest_ready")
        f_squared, f_hi_ready = sem("f_squared"), sem("f_hi_ready")
        pads_ready = sem("pads_ready")
        consts = sem("consts")
        pool_chain, dve_chain, act_chain = sem("pool_chain"), sem("dve_chain"), sem("act_chain")
        qz_ready = sem("qz_ready")
        norms = ["attn", "mix", "ffn", "mix2", "mlp2"]
        rms_ready = {n: sem(f"rms_ready_{n}") for n in norms + ["vg", "first", "last"]}
        rows = {n: sem(f"rows_{n}") for n in norms}
        turned = {n: sem(f"turned_{n}") for n in norms}
        hT_ready = {n: sem(f"hT_ready_{n}") for n in norms}
        wsp_turned, wspT_ready = sem("wsp_turned"), sem("wspT_ready")
        tables_turned, tables_ready = sem("tables_turned"), sem("tables_ready")
        qk_ps, qk_ready = sem("qk_ps"), sem("qk_ready")
        vug_ps, v_ready, gelu_ready = sem("vug_ps"), sem("v_ready"), sem("gelu_ready")
        vg_ready = sem("vg_ready")
        score_ps, att_abs, att_ln, att_sp = sem("score_ps"), sem("att_abs"), sem("att_ln"), sem("att_sp")
        att_ps, att_x, att_exp, av_done = sem("att_ps"), sem("att_x"), sem("att_exp"), sem("av_done")
        ao_ready, sgu_ps, so_ready = sem("ao_ready"), sem("sgu_ps"), sem("so_ready")
        out1_ps, x_ready = sem("out1_ps"), sem("x_ready")
        logits_ps, r_exp_in, r_exp = sem("logits_ps"), sem("r_exp_in"), sem("r_exp")
        routed_ready, rank_ps, count_ps = sem("routed_ready"), sem("rank_ps"), sem("count_ps")
        extra_ready = sem("extra_ready")
        sel_ready, gath_ps, xg_ready = sem("sel_ready"), sem("gath_ps"), sem("xg_ready")
        ct_ps, ct_ready = sem("ct_ps"), sem("ct_ready")
        gu_done, silu_ready, hid_ready = sem("gu_done"), sem("silu_ready"), sem("hid_ready")
        hidT_ps, hidT_ready, down_done = sem("hidT_ps"), sem("hidT_ready"), sem("down_done")
        y_act, y_dve, comb_ps = sem("y_act"), sem("y_dve"), sem("comb_ps")
        moe_done, comb_free = sem("moe_done"), sem("comb_free")
        x2_ready = sem("x2_ready")
        sel_made, first_ps, first_ready, slot_ranks = sem("sel_made"), sem("first_ps"), sem("first_ready"), sem("slot_ranks")
        tap_step, short_step = [sem(f"tap_step{i}") for i in range(2)], [sem(f"short_step{i}") for i in range(2)]
        w2_used = sem("w2_used")
        lru_square, lru_root, var_in, var_root = sem("lru_square"), sem("lru_root"), sem("var_in"), sem("var_root")
        z_ps, z_bank_free, z_ready = sem("z_ps"), sem("z_bank_free"), sem("z_ready")
        conv_a_ready, v2_ready = sem("conv_a_ready"), sem("v2_ready")
        lru_ps, lru_gates, lru_log, lru_exp = sem("lru_ps"), sem("lru_gates"), sem("lru_log"), sem("lru_exp")
        lam_ln, h_ready = sem("lam_ln"), sem("h_ready")
        mean_ps, centred, sq_ready, var_ps, scaled, a_ready = (
            sem("mean_ps"), sem("centred"), sem("sq_ready"), sem("var_ps"), sem("scaled"), sem("a_ready"))
        y_ps, m_ready = sem("y_ps"), sem("m_ready")
        o_ps, x3_ready = sem("o_ps"), sem("x3_ready")
        f_ps, f_relu, f_bank_free, f_ready = sem("f_ps"), sem("f_relu"), sem("f_bank_free"), sem("f_ready")
        mlp_ps, x4_ready = sem("mlp_ps"), sem("x4_ready")
        fin_ready, stored = sem("fin_ready"), sem("stored")

        x_d = A["x"][0].rearrange("(a p) d -> p a d", p=P)
        out_d = out[0].rearrange("(a p) d -> p a d", p=P)

        def by_pk(w):
            return w.rearrange("(p k) n -> p k n", k=KC)

        def by_kp(w):
            return w.rearrange("(k p) n -> p k n", p=P)

        w_in1, w_out1 = by_pk(A["w_in"][0]), by_pk(A["w_out"][0])
        wg_d = A["w_gate"][0].rearrange("g e (p k) n -> (g e) p (k n)", k=KC)
        wu_d = A["w_up"][0].rearrange("g e (p k) n -> (g e) p (k n)", k=KC)
        wd_d = A["w_down"][0].rearrange("g e (k p) n -> (g e) p k n", p=P)
        w_in2 = by_pk(A["w_in_2"][0])
        wa_d, wb_d, wo_d = by_kp(A["w_a_out_2"][0]), by_kp(A["w_b_out_2"][0]), by_kp(A["w_o_2"][0])
        w1_d, w2_d = by_pk(A["w_1_2"][0]), by_kp(A["w_2_2"][0])

        def chunked(s, n):
            return slot[s][:, 0:SLOT_FLOATS // n * n].rearrange("p (k n) -> p k n", n=n)

        late = [wb_d[:, :, HALF * n:HALF * (n + 1)] for n in range(4)]
        L_A, L_O, L_F = 4, 6, 8
        late += [wa_d[:, :, BLOCK * n:BLOCK * (n + 1)] for n in range(2)]
        late += [wo_d[:, :, BLOCK * n:BLOCK * (n + 1)] for n in range(2)]
        for half in range(2):
            late += [w1_d[:, :, BLOCK * n:BLOCK * (n + 1)] for n in range(4 * half, 4 * half + 4)]
            late += [w2_d[:, 4 * n:4 * n + 4, :] for n in range(4 * half, 4 * half + 4)]

        def late_arrived(n):
            return late_loaded[n % 4], 16 * (n // 4 + 1)

        def late_used(n):
            if n < L_A:
                return y_ps, 2 * (n + 1)
            if n < L_O:
                return y_ps, KC + 4 * (n - L_A + 1)
            if n < L_F:
                return o_ps, 2 * (n - L_O + 1)
            half, b = (n - L_F) // 8, (n - L_F) % 8
            return (f_ps, 16 * half + 4 * (b + 1)) if b < 4 else (w2_used, 4 * half + b - 3)

        def pre_count(n):
            return 16 * (n // RING + 1)

        def vec(v):
            return v.rearrange("(p k) -> p k", k=KC)

        block = ctx.enter_context(nc.Block())

        @block.sync
        def _(sp):
            sp.dma_start(X[:, 0, :], x_d[:, 0, :]).then_inc(x_loaded, 16)
            sp.dma_start(X[:, 1, :], x_d[:, 1, :]).then_inc(x_loaded, 16)
            def small_loads():
                half = P // 2
                sp.dma_start(wsp, A["w_spatial"][0].rearrange("h t s -> t h s")).then_inc(small_loaded, 16)
                sp.dma_start(bsp[0:HEADS], A["b_spatial"][0]).then_inc(small_loaded, 16)
                sp.dma_start(sgn_g, A["sg_norm_g"].partition_broadcast(P).rearrange("p a n -> p (a n)")).then_inc(small_loaded, 16)
                sp.dma_start(gains[0:half, G_MIX, :], vec(A["sb_out_norm_g"][0])).then_inc(small_loaded, 16)
                sp.dma_start(gains[half:P, G_MIX, :], vec(A["sg_out_norm_g"][0])).then_inc(small_loaded, 16)
                sp.dma_start(gains[:, G_MIX2, :], vec(A["g_mix_2"][0])).then_inc(small_loaded, 16)
                sp.dma_start(gains[:, G_MLP2, :], vec(A["g_mlp_2"][0])).then_inc(small_loaded, 16)
                sp.dma_start(gains[:, G_FFN, :], vec(A["ffn_norm_g"][0])).then_inc(router_loaded, 16)
                sp.dma_start(wr_group[:, :, :], by_pk(A["w_router_group"][0])).then_inc(router_loaded, 16)
                sp.dma_start(wr_expert[:, :, :, :], A["w_router_expert"][0].rearrange("g (p k) e -> p g k e", k=KC)).then_inc(router_loaded, 16)
                sp.dma_start(b_router[:, 0:GROUPS], A["b_router_group"][0].partition_broadcast(P)).then_inc(router_loaded, 16)
                sp.dma_start(b_router[:, GROUPS:], A["b_router_expert"][0].rearrange("g e -> (g e)").partition_broadcast(P)).then_inc(router_loaded, 16)
                sp.dma_start(g_first[:, :], A["final_norm_g"].partition_broadcast(P)).then_inc(router_loaded, 16)
                sp.dma_start(g_last[:, :], A["g_final_2"].partition_broadcast(P)).then_inc(router_loaded, 16)

                def rows128(v):
                    return v.rearrange("(c p) -> c p", p=P)

                for to, count, name in ((V_CAB, 8, "conv_a_b_2"), (V_LNG, 8, "ln_g_2"), (V_LNB, 8, "ln_b_2"),
                                        (V_CBB, RC, "conv_b_b_2"), (V_BRA, RC, "b_rg_a_2"), (V_BRX, RC, "b_rg_x_2"),
                                        (V_LAM, RC, "lam_2")):
                    sp.dma_start(vec_raw[to:to + count], rows128(A[name][0])).then_inc(table_loaded, 16)
                sp.dma_start(vec_raw[0:ZC], rows128(A["b_in_2"][0])).then_inc(table_loaded, 16)
                taps = A["conv_a_w_2"][0].rearrange("k (c p) -> (k c) p", p=P)
                sp.dma_start(caw_raw[:, 0, :], taps[0:P]).then_inc(table_loaded, 16)
                sp.dma_start(caw_raw[0:TAPS_A * KC - P, 1, :], taps[P:]).then_inc(table_loaded, 16)
                sp.dma_start(cbw_raw[0:TAPS_B * RC], A["conv_b_w_2"][0].rearrange("k (c p) -> (k c) p", p=P)).then_inc(table_loaded, 16)

            for n in range(PRE):
                if n >= RING:
                    small_loads()
                    sp.wait_ge(qk_ps, 4)
                w, b = (w_in1, n) if n < IN1_BLOCKS else (w_out1, n - IN1_BLOCKS)
                sp.dma_start(chunked(n % RING, BLOCK), w[:, :, b * BLOCK:(b + 1) * BLOCK]).then_inc(loaded[n % RING], 16)

            def load_expert(e, i):
                for part, w in enumerate((wg_d, wu_d)):
                    s = (PRE + 3 * i + part) % RING
                    sp.dma_start(slot[s], w[bass.ds(e, 1)].rearrange("e p n -> p (e n)")).then_inc(loaded[s], 16)

            def load_down(e, i):
                s = (PRE + 3 * i + 2) % RING
                sp.dma_start(chunked(s, D), wd_d[bass.ds(e, 1)].rearrange("e p k n -> p (e k) n")).then_inc(loaded[s], 16)

            sp.wait_ge(qk_ps, 8)
            sp.wait_ge(vug_ps, 2)
            load_expert(0, 0)
            sp.wait_ge(vug_ps, 4)
            load_down(0, 0)
            sp.wait_ge(vug_ps, 6)
            sp.wait_ge(out1_ps, 2)
            load_expert(1, 1)
            sp.wait_ge(out1_ps, 4)
            load_down(1, 1)
            with sp.Fori(1, EXPERTS // 2) as pair:
                for i in range(2):
                    sp.wait_ge(gu_done, 2 * pair + (i - 1))
                    load_expert(2 * pair + i, i)
                    sp.wait_ge(down_done, 2 * pair + (i - 1))
                    load_down(2 * pair + i, i)
            sp.wait_ge(extra_ready, 1)
            n_extra = sp.value_load(extra_i[0:1, 0, 0:1], min_val=0, max_val=EXTRA_MAX)
            with sp.Fori(0, EXTRA_MAX) as j:
                with sp.If(j < n_extra):
                    e = sp.value_load(extra_i[0:1, 1, bass.ds(j, 1)], min_val=0, max_val=EXPERTS - 1)
                    sp.wait_ge(down_done, j + EXPERTS)
                    for part, w in enumerate((wg_d, wu_d)):
                        sp.dma_start(slot[4 + part], w[bass.ds(e, 1)].rearrange("e p n -> p (e n)")).then_inc(extra_loaded[part], 16)
                    sp.dma_start(chunked(0, D), wd_d[bass.ds(e, 1)].rearrange("e p k n -> p (e k) n")).then_inc(extra_loaded[2], 16)
            sp.wait_ge(down_done, EXPERTS - 1)
            for n, h in enumerate(IN2_ORDER):
                if n >= RAW:
                    sp.wait_ge(z_ps, 2 * (n - RAW + 1))
                sp.dma_start(z_raw(n).rearrange("p (k n) -> p k n", n=HALF),
                             w_in2[:, :, h * HALF:(h + 1) * HALF]).then_inc(raw_loaded[n % RAW], 16)
            for n, src in enumerate(late):
                if n == 0:
                    sp.wait_ge(lru_log, RG)
                elif n == 1:
                    sp.wait_ge(z_ps, ZC - 4)
                elif n < 4:
                    sp.wait_ge(z_ps, ZC)
                else:
                    sp.wait_ge(*late_used(n - 4))
                rows_, width = src.shape[1], src.shape[2]
                dst = slot[n % 4][:, 0:rows_ * width].rearrange("p (k n) -> p k n", n=width)
                sp.dma_start(dst, src).then_inc(late_loaded[n % 4], 16)
            for tt in range(TT):
                sp.wait_ge(fin_ready, tt + 1)
                sp.dma_start(out_d[:, tt, :], fin[:, tt, :]).then_inc(stored, 16)
            sp.wait_ge(stored, 16 * TT)

        @block.gpsimd
        def _(pool):
            done = [0]

            def link(ins):
                done[0] += 1
                ins.then_inc(pool_chain, 1)
                pool.wait_ge(pool_chain, done[0])

            def triangle(m, inside, outside, compare, row, col, base=0):
                link(nc.gpsimd.memset(m[:, :], inside))
                nc.gpsimd.affine_select(out=m[:, :], in_=m[:, :], compare_op=compare, fill=outside, base=base,
                                        pattern=[[col, P]], channel_multiplier=row).then_inc(consts, 1)

            triangle(ident, 0.0, 1.0, ALU.not_equal, 1, -1)
            triangle(upto, 1.0, 0.0, ALU.is_ge, -1, 1)
            triangle(before, 1.0, 0.0, ALU.is_gt, -1, 1)
            triangle(maskbias, 0.0, MASKED, ALU.is_gt, -1, 1)
            triangle(tri_neg, -1.0, 0.0, ALU.is_ge, 1, -1)
            nc.gpsimd.memset(neg_ones[:, :], -1.0).then_inc(consts, 1)
            nc.gpsimd.memset(ones[:, :], 1.0).then_inc(consts, 1)
            nc.gpsimd.memset(mean_ones[:, :], 1.0 / D).then_inc(consts, 1)
            nc.gpsimd.memset(zeros[:, :], 0.0).then_inc(consts, 1)
            nc.gpsimd.memset(eps[:, :], EPS).then_inc(consts, 1)
            nc.gpsimd.memset(qT, 0.0).then_inc(qz_ready, 1)
            link(nc.gpsimd.iota(iota_i[:, :], pattern=[[1, SLOTS]], base=0, channel_multiplier=0))
            nc.gpsimd.tensor_copy(iota_s[:, :], iota_i[:, :]).then_inc(consts, 1)

            pool.wait_ge(moe_done, 1)
            link(nc.gpsimd.memset(BDA[:, :, :, :], 0.0))
            link(nc.gpsimd.memset(BDX[:, :, :, :], 0.0))
            nc.gpsimd.memset(UP[:, :, 0:PAD], 0.0).then_inc(pads_ready, 1)
            for bd, w in ((BDA, A["w_rg_a_2"]), (BDX, A["w_rg_x_2"])):
                heads = w[0].rearrange("(g h) i j -> h i g j", g=RG)
                for h in range(4):
                    r0 = h * RNN_HEAD
                    while r0 < (h + 1) * RNN_HEAD:
                        chunk = r0 // P
                        r1 = min((chunk + 1) * P, (h + 1) * RNN_HEAD)
                        c0 = h * RNN_HEAD - chunk * RNN_HEAD
                        pool.dma_start(bd[r0 - chunk * P:r1 - chunk * P, :, chunk, c0:c0 + RNN_HEAD],
                                       heads[h, r0 - h * RNN_HEAD:r1 - h * RNN_HEAD]).then_inc(bd_loaded, 16)
                        r0 = r1

            for n in range(IN2_HALVES):
                pool.wait_ge(z_hi_ready, n + 1)
                nc.gpsimd.tensor_tensor(z_rest(n), z_raw(n), z_hi[:, n % HI, :].bitcast(F32), ALU.subtract).then_inc(z_rest_ready, 1)

        N_TABLE = 11
        N_BD = 12
        N_CONST = 11
        N_ROUTER = 7
        N_SMALL = 7

        @block.scalar
        def _(act):
            done = [0]

            def link(ins):
                done[0] += 1
                ins.then_inc(act_chain, 1)
                act.wait_ge(act_chain, done[0])

            act.dma_start(gains[:, G_ATTN, :], vec(A["attn_norm_g"][0])).then_inc(gain_loaded, 16)

            def add_squares(rows_, col, scratch):
                link(nc.scalar.activation(scratch, rows_, ACT.Square, accum_out=ss[:, col:col + 1]))

            def rms(name, col, n, width):
                nc.scalar.activation(rstd[:, col:col + n], ss[:, col:col + n], ACT.Sqrt, scale=1.0 / width,
                                     bias=eps[:, :]).then_inc(rms_ready[name], 1)

            def row_squares(name, col):
                for tt in range(TT):
                    add_squares(X[:, tt, :], col + tt, square)
                rms(name, col, TT, D)

            act.wait_ge(consts, N_CONST)
            act.wait_ge(x_loaded, 16 * TT)
            row_squares("attn", 0)
            act.wait_ge(qz_ready, 1)
            for n in range(8):
                act.wait_ge(qk_ps, n + 1)
                ps = PS[:, n % 4, 0:T]
                if n < 4:
                    nc.scalar.activation(qT[0:64, 2 * n, :], ps[0:64], ACT.Copy, scale=HEAD_DIM ** -0.5)
                    nc.scalar.activation(qT[64:P, 2 * n + 1, :], ps[64:P], ACT.Copy, scale=HEAD_DIM ** -0.5).then_inc(qk_ready, 1)
                else:
                    nc.scalar.activation(kT[:, n - 4, :], ps, ACT.Copy).then_inc(qk_ready, 1)
            for n in range(2, 6):
                act.wait_ge(vug_ps, n + 1)
                dst = (U if n < 4 else VG)[:, n % 2, :]
                nc.scalar.activation(dst, PS[:, 4 + n % 4, :], ACT.Gelu_apprx_tanh).then_inc(gelu_ready, 1)
            act.wait_ge(gelu_ready, 4)
            for tt in range(TT):
                add_squares(VG[:, tt, :], 2 + tt, square[:, 0:SB])
            rms("vg", 2, TT, SB)
            def att_log(h):
                act.wait_ge(score_ps, h + 1)
                if h >= 2:
                    act.wait_ge(att_sp, h - 1)
                e = att_e[:, h % 2, :]
                link(nc.scalar.activation(e, PS[:, h % 2, 0:3 * P], ACT.Abs))
                link(nc.scalar.activation(e, e, ACT.Exp, scale=-1.0))
                nc.scalar.activation(e, e, ACT.Ln, bias=1.0).then_inc(att_ln, 1)

            def att_weights(h):
                act.wait_ge(att_x, h + 1)
                nc.scalar.activation(att_a[:, h % 2, :], att_a[:, h % 2, :], ACT.Exp).then_inc(att_exp, 1)

            act.preload_act_table_set("natural_log_exp_and_others")
            for h in range(HEADS):
                att_log(h)
                if h >= 1:
                    att_weights(h - 1)
            att_weights(HEADS - 1)
            for half_n, (rows_, ready) in enumerate(((ao, ao_ready), (so, so_ready))):
                act.wait_ge(ready, TT)
                for tt in range(TT):
                    add_squares(rows_[:, tt, :], 4 + 2 * half_n + tt, square[:, 0:SB])
            rms("mix", 4, 2 * TT, SB)
            act.wait_ge(tables_turned, 1)
            for dst, at in ((VEC, 0), (CAW, P), (CBW, P + TAPS_A * KC)):
                n = dst.shape[1]
                nc.scalar.activation(dst[:, :], PS[:, 0, at:at + n], ACT.Copy).then_inc(tables_ready, 1)
            act.wait_ge(x_ready, 4)
            row_squares("ffn", 8)
            act.wait_ge(r_exp_in, 1)
            nc.scalar.activation(r_a[:, :, 0:GROUPS + 1], r_a[:, :, 0:GROUPS + 1], ACT.Exp).then_inc(r_exp, 1)

            def turn_combine(pack):
                act.wait_ge(ct_ps, pack + 1)
                act.wait_ge(comb_ps, 4 * pack + 1)
                nc.scalar.activation(CT, PS[:, B_GATHER, 0:T], ACT.Copy).then_inc(ct_ready, 1)

            def gate(e, i):
                act.wait_ge(gu_done, e + 1)
                nc.scalar.activation(silu[:, i % 2, :], PS[:, B_GATE + i % 2, 0:P], ACT.Silu).then_inc(silu_ready, 1)

            def hidden_turned(e, i):
                act.wait_ge(hidT_ps, e + 1)
                nc.scalar.activation(hidT[:, i % 2, :], PS[:, B_TURN, 0:P], ACT.Copy).then_inc(hidT_ready, 1)

            def collect(e, i):
                act.wait_ge(down_done, e + 1)
                for j in range(2):
                    ins = nc.scalar.activation(Y[SLOTS * i:SLOTS * (i + 1), D_STRIP * j:D_STRIP * (j + 1)],
                                               PS[SLOTS * j:SLOTS * (j + 1), B_DOWN + i % 2, 0:D_STRIP], ACT.Copy)
                ins.then_inc(y_act, 1)

            with act.Fori(0, PACKS) as pack:
                e = PACK * pack
                turn_combine(pack)
                gate(e, 0)
                gate(e + 1, 1)
                for i in range(PACK):
                    hidden_turned(e + i, i)
                    collect(e + i, i)
                    if i + 2 < PACK:
                        gate(e + (i + 2), i + 2)
            act.wait_ge(extra_ready, 1)
            n_extra = act.value_load(extra_i[0:1, 0, 0:1], min_val=0, max_val=EXTRA_MAX)
            with act.Fori(0, EXTRA_MAX) as j:
                with act.If(j < n_extra):
                    turn_combine(j + PACKS)
                    gate(j + EXPERTS, 0)
                    hidden_turned(j + EXPERTS, 0)
                    collect(j + EXPERTS, 0)

            act.wait_ge(moe_done, 1)
            row_squares("first", 10)
            act.wait_ge(tables_ready, 3)
            link(nc.scalar.activation(sp8[:, 0, :], VEC[:, V_LAM:V_LAM + RC], ACT.Abs))
            link(nc.scalar.activation(sp8[:, 0, :], sp8[:, 0, :], ACT.Exp, scale=-1.0))
            nc.scalar.activation(sp8[:, 0, :], sp8[:, 0, :], ACT.Ln, bias=1.0).then_inc(lam_ln, 1)

            def split_half(n):
                act.wait_ge(raw_loaded[n % RAW], 16 * (n // RAW + 1))
                if n >= HI:
                    act.wait_ge(z_ps, 2 * (n - HI + 1))
                nc.scalar.activation(z_hi[:, n % HI, :], z_raw(n), ACT.Copy).then_inc(z_hi_ready, 1)

            def split_hT(name):
                for n in range(4):
                    tt, ks = n // 2, slice(4 * (n % 2), 4 * (n % 2) + 4)
                    act.wait_ge(hT_ready[name], n + 1)
                    nc.scalar.activation(HT_hi[:, tt, ks, :], HT[:, ks, tt * P:(tt + 1) * P], ACT.Copy).then_inc(hT_hi_ready[name], 1)

            split_half(0)
            act.wait_ge(x2_ready, TT)
            row_squares("mix2", 12)
            split_half(1)
            split_hT("mix2")

            def take_z(n):
                for i in range(2):
                    ch = 2 * IN2_ORDER[n] + i
                    dst = UP[:, ch, PAD:] if ch < C_GA else Z[:, ch - C_GA, :]
                    func = (ACT.Identity if ch < C_GA or C_XB <= ch < C_GB else
                            ACT.Gelu_apprx_tanh if C_GB <= ch < C_SA else ACT.Sigmoid)
                    act.wait_ge(z_ps, 2 * n + i + 1)
                    nc.scalar.activation(dst, PS[:, (2 * n + i) % 4, 0:T], func, bias=VEC[:, ch:ch + 1]).then_inc(z_bank_free, 1)

            def lru_sigmoids():
                for g in range(RG):
                    act.wait_ge(lru_ps, g + 1)
                    if g >= 2:
                        act.wait_ge(lru_log, g - 1)
                    for k in range(3):
                        n = 3 * g + k
                        nc.scalar.activation(RB[:, n, :], PS[:, 4 + k // 2, (k % 2) * T:(k % 2 + 1) * T], ACT.Sigmoid,
                                             bias=VEC[:, V_BRA + n:V_BRA + n + 1])
                        ins = nc.scalar.activation(IB[:, g % 2, k, :], PS[:, 6 + k // 2, (k % 2) * T:(k % 2 + 1) * T], ACT.Sigmoid,
                                                   bias=VEC[:, V_BRX + n:V_BRX + n + 1])
                    ins.then_inc(lru_gates, 1)

            def lru_exponentials():
                for g in range(RG):
                    act.wait_ge(lru_log, g + 1)
                    rows_ = slice(3 * g, 3 * g + 3)
                    nc.scalar.activation(AB[:, rows_, :], RB[:, rows_, :], ACT.Exp, scale=-1.0)
                    nc.scalar.activation(Z[:, Z_XB + 3 * g:Z_XB + 3 * g + 3, :], RB[:, rows_, :], ACT.Tanh).then_inc(lru_exp, 1)

            def lru_roots():
                for g in range(RG):
                    act.wait_ge(lru_square, g + 1)
                    th = Z[:, Z_XB + 3 * g:Z_XB + 3 * g + 3, :]
                    nc.scalar.activation(th, th, ACT.Sqrt).then_inc(lru_root, 1)

            for n in range(IN2_HALVES):
                take_z(n)
                if n + HI < IN2_HALVES:
                    split_half(n + HI)
                if n == LRU_AFTER * IN2_GROUP - 1:
                    lru_sigmoids()
                if n == ACT_EXP:
                    lru_exponentials()
                if n == ACT_ROOT:
                    lru_roots()
            act.wait_ge(centred, 1)
            nc.scalar.activation(Z[:, Z_GA:Z_GA + KC, :], CU, ACT.Square).then_inc(sq_ready, 1)
            act.wait_ge(var_in, 1)
            nc.scalar.activation(inv_ln, inv_ln, ACT.Sqrt).then_inc(var_root, 1)
            act.wait_ge(scaled, 1)
            for k in range(KC):
                nc.scalar.activation(CU[:, k, :], CU[:, k, :], ACT.Silu, bias=VEC[:, V_LNB + k:V_LNB + k + 1],
                                     scale=VEC[:, V_LNG + k:V_LNG + k + 1]).then_inc(a_ready, 1)
            def split_mlp(n):
                act.wait_ge(*late_arrived(L_F + n))
                if n < 2:
                    act.wait_ge(y_ps, KC)
                elif n == 2:
                    act.wait_ge(y_ps, 2 * KC)
                elif n == 3:
                    act.wait_ge(o_ps, 4)
                else:
                    act.wait_ge(*late_used(L_F + n - 4))
                nc.scalar.activation(mlp_hi[n % 4][:, :], slot[n % 4], ACT.Copy).then_inc(mlp_hi_ready, 1)

            for n in range(3):
                split_mlp(n)
            act.wait_ge(x3_ready, 4)
            row_squares("mlp2", 14)
            split_mlp(3)
            split_hT("mlp2")
            for half_n in range(2):
                for b in range(4):
                    at = 4 * half_n + b
                    for i in range(4):
                        act.wait_ge(f_ps, 4 * at + i + 1)
                        nc.scalar.activation(FT[:, 4 * b + i, :], PS[:, 4 + i, 0:T], ACT.Relu).then_inc(f_bank_free, 1)
                    split_mlp(8 * half_n + b + 4)
                    act.wait_ge(f_squared, at + 1)
                    nc.scalar.activation(FT_hi[:, 4 * b:4 * b + 4, :], FT[:, 4 * b:4 * b + 4, :], ACT.Copy).then_inc(f_hi_ready, 1)
                if half_n == 0:
                    for b in range(4):
                        split_mlp(8 + b)
            for tt in range(TT):
                act.wait_ge(x4_ready, 2 * tt + 2)
                add_squares(X[:, tt, :], tt, fin[:, tt, :])
            rms("last", 0, TT, D)

        @block.vector
        def _(dve):
            done = [0]

            def link(ins):
                done[0] += 1
                ins.then_inc(dve_chain, 1)
                dve.wait_ge(dve_chain, done[0])

            def inverse_rms(name, col, n):
                dve.wait_ge(rms_ready[name], 1)
                link(nc.vector.reciprocal(rstd[:, col:col + n], rstd[:, col:col + n]))

            def permuted(tt):
                return HN[:, tt, :, :].rearrange("p k q -> p q k")

            def plain(v):
                return v.rearrange("p (q k) -> p q k", k=KC)

            def normalise(name, col):
                inverse_rms(name, col, TT)
                for tt in range(TT):
                    nc.vector.tensor_scalar(permuted(tt), plain(X[:, tt, :]), rstd[:, col + tt:col + tt + 1], None,
                                            ALU.mult).then_inc(rows[name], 1)

            def apply_gain(name, g, free=None, credits=0):
                if name == "attn":
                    dve.wait_ge(gain_loaded, 16)
                if name == "mix":
                    dve.wait_ge(small_loaded, 16 * N_SMALL)
                if name == "ffn":
                    dve.wait_ge(router_loaded, 16 * N_ROUTER)
                for n in range(4):
                    tt, half = n // 2, n % 2
                    dve.wait_ge(turned[name], n + 1)
                    ks = slice(4 * half, 4 * half + 4)
                    ins = nc.vector.tensor_tensor(HT[:, ks, tt * P:(tt + 1) * P], PS[:, 4 + n, :].rearrange("p (k t) -> p k t", k=4),
                                                  gains[:, g, ks].unsqueeze(2).broadcast_to((P, 4, P)), ALU.mult)
                    ins.then_inc(hT_ready[name], 1)

            dve.wait_ge(consts, N_CONST)
            normalise("attn", 0)
            apply_gain("attn", G_ATTN)
            for n in range(2):
                dve.wait_ge(vug_ps, n + 1)
                nc.vector.tensor_copy(V[:, n, :], PS[:, 4 + n, :]).then_inc(v_ready, 1)
            inverse_rms("vg", 2, TT)
            dve.wait_ge(small_loaded, 16 * N_SMALL)
            for tt in range(TT):
                nc.vector.scalar_tensor_tensor(VG[:, tt, :], VG[:, tt, :], rstd[:, 2 + tt:3 + tt], sgn_g, ALU.mult,
                                               ALU.mult).then_inc(vg_ready, 1)

            def att_softplus(h):
                dve.wait_ge(att_ln, h + 1)
                s = att_s[:, h % 2, :]
                link(nc.vector.scalar_tensor_tensor(s, PS[:, h % 2, 0:3 * P], 0.0, att_e[:, h % 2, :], ALU.max, ALU.add))
                diagonal = s.rearrange("p (b q) -> p b q", b=3)[:, 0:3:2, :]
                nc.vector.tensor_tensor(diagonal, diagonal, before[:, :].unsqueeze(1).broadcast_to((P, 2, P)), ALU.mult).then_inc(att_sp, 1)

            def att_masked(h):
                dve.wait_ge(att_ps, h + 1)
                if h >= 2:
                    dve.wait_ge(av_done, h - 1)
                a, ps = att_a[:, h % 2, :], PS[:, h % 2, 0:3 * P]
                a3, ps3 = a.rearrange("p (b q) -> p b q", b=3), ps.rearrange("p (b q) -> p b q", b=3)
                nc.vector.tensor_scalar(a3[:, 1, :], ps3[:, 1, :], 0.0, None, ALU.min)
                nc.vector.scalar_tensor_tensor(a3[:, 0:3:2, :], ps3[:, 0:3:2, :], 0.0, maskbias[:, :].unsqueeze(1).broadcast_to((P, 2, P)),
                                               ALU.min, ALU.add).then_inc(att_x, 1)

            def spatial_weights():
                for n in range(2):
                    dve.wait_ge(wsp_turned, n + 1)
                    nc.vector.tensor_tensor(wspT[:, 4 * n:4 * n + 4, :], PS[:, 6 + n, :].rearrange("p (k t) -> p k t", k=4),
                                            upto[:, :].unsqueeze(1).broadcast_to((P, 4, P)), ALU.mult).then_inc(wspT_ready, 1)
                dve.wait_ge(wsp_turned, 3)
                nc.vector.tensor_copy(bspT, PS[:, 4, 0:HEADS]).then_inc(wspT_ready, 1)

            for h in range(HEADS):
                att_softplus(h)
                att_masked(h)
                if h == 4:
                    spatial_weights()
            dve.wait_ge(av_done, HEADS)
            for tt in range(TT):
                nc.vector.tensor_copy(ao[:, tt, :], PS[:, 2 + tt, :]).then_inc(ao_ready, 1)
            for tt in range(TT):
                dve.wait_ge(sgu_ps, tt + 1)
                link(nc.vector.tensor_tensor(so[:, tt, :].rearrange("p (h d) -> p h d", h=HEADS),
                                             PS[:, 4 + tt, :].rearrange("p (h d) -> p h d", h=HEADS),
                                             bspT.unsqueeze(2).broadcast_to((P, HEADS, HEAD_DIM)), ALU.add))
                nc.vector.tensor_tensor(so[:, tt, :], so[:, tt, :], U[:, tt, :], ALU.mult).then_inc(so_ready, 1)
            inverse_rms("mix", 4, 2 * TT)
            for tt in range(TT):
                for half_n, src in enumerate((ao, so)):
                    nc.vector.tensor_scalar(permuted(tt)[:, 64 * half_n:64 * half_n + 64, :], plain(src[:, tt, :]),
                                            rstd[:, 4 + 2 * half_n + tt:5 + 2 * half_n + tt], None, ALU.mult).then_inc(rows["mix"], 1)
            apply_gain("mix", G_MIX)
            for n in range(4):
                dve.wait_ge(out1_ps, n + 1)
                half = slice((n // 2) * BLOCK, (n // 2 + 1) * BLOCK)
                nc.vector.tensor_tensor(X[:, n % 2, half], X[:, n % 2, half], PS[:, n, :], ALU.add).then_inc(x_ready, 1)
            dve.wait_ge(x_ready, 4)
            normalise("ffn", 8)
            apply_gain("ffn", G_FFN)

            dve.wait_ge(router_loaded, 16 * N_ROUTER)
            dve.wait_ge(logits_ps, 1)
            link(nc.vector.tensor_tensor(logit, PS[:, 0, 0:TT * 36].rearrange("p (a n) -> p a n", a=TT),
                                         b_router[:, :].unsqueeze(1).broadcast_to((P, TT, GROUPS + EXPERTS)), ALU.add))
            g_log = logit[:, :, 0:GROUPS]
            e_log = logit[:, :, GROUPS:].rearrange("p a (g e) -> p a g e", g=GROUPS)

            def over(v, n):
                return v.broadcast_to((P, TT, n))

            def first_max(values, n, top, onehot, tmp, places):
                link(nc.vector.tensor_reduce(top, values, AX_X, ALU.max))
                link(nc.vector.tensor_tensor(tmp, values, over(top, n), ALU.is_lt))
                link(nc.vector.scalar_tensor_tensor(tmp, tmp, 64.0, places, ALU.mult, ALU.add))
                link(nc.vector.tensor_reduce(place, tmp, AX_X, ALU.min))
                link(nc.vector.tensor_tensor(onehot, places, over(place, n), ALU.is_equal))

            places4 = iota_s[:, 0:GROUPS].unsqueeze(1).broadcast_to((P, TT, GROUPS))
            places8 = iota_s[:, 0:EXPERTS_PER_GROUP].unsqueeze(1).broadcast_to((P, TT, EXPERTS_PER_GROUP))
            g_hot, g_top, tmp4 = r_c[:, :, 0:4], r_c[:, :, 4:5], r_c[:, :, 8:12]
            top1, top2, place = r_c[:, :, 5:6], r_c[:, :, 6:7], r_c[:, :, 7:8]
            hot1, hot2, tmp8, e_sel, e_rest = (r_c[:, :, 16 + 8 * k:24 + 8 * k] for k in range(5))
            first_max(g_log, GROUPS, g_top, g_hot, tmp4, places4)
            link(nc.vector.tensor_tensor(r_b.rearrange("p a (g e) -> p a g e", g=GROUPS)[:, 0], e_log[:, 0],
                                         g_hot[:, 0].unsqueeze(2).broadcast_to((P, GROUPS, EXPERTS_PER_GROUP)), ALU.mult))
            link(nc.vector.tensor_tensor(r_b.rearrange("p a (g e) -> p a g e", g=GROUPS)[:, 1], e_log[:, 1],
                                         g_hot[:, 1].unsqueeze(2).broadcast_to((P, GROUPS, EXPERTS_PER_GROUP)), ALU.mult))
            link(nc.vector.tensor_reduce(e_sel, r_b.rearrange("p a (g e) -> p a e g", g=GROUPS), AX_X, ALU.add))
            first_max(e_sel, EXPERTS_PER_GROUP, top1, hot1, tmp8, places8)
            link(nc.vector.scalar_tensor_tensor(e_rest, hot1, -3e38, e_sel, ALU.mult, ALU.add))
            first_max(e_rest, EXPERTS_PER_GROUP, top2, hot2, tmp8, places8)
            link(nc.vector.tensor_tensor(r_a[:, :, 0:GROUPS], g_log, over(g_top, GROUPS), ALU.subtract))
            nc.vector.tensor_tensor(r_a[:, :, GROUPS:GROUPS + 1], top2, top1, ALU.subtract).then_inc(r_exp_in, 1)
            link(nc.vector.tensor_tensor(tmp8, hot1, hot2, ALU.add))
            for tt in range(TT):
                nc.vector.tensor_tensor(routed[:, tt, :].rearrange("p (g e) -> p g e", g=GROUPS),
                                        g_hot[:, tt].unsqueeze(2).broadcast_to((P, GROUPS, EXPERTS_PER_GROUP)),
                                        tmp8[:, tt].unsqueeze(1).broadcast_to((P, GROUPS, EXPERTS_PER_GROUP)), ALU.mult).then_inc(routed_ready, 1)
            dve.wait_ge(r_exp, 1)
            w1c, w2c = r_a[:, :, 8:9], r_a[:, :, 9:10]
            link(nc.vector.tensor_reduce(r_a[:, :, 6:7], r_a[:, :, 0:GROUPS], AX_X, ALU.add))
            link(nc.vector.tensor_scalar(r_a[:, :, 7:8], r_a[:, :, GROUPS:GROUPS + 1], 1.0, None, ALU.add))
            link(nc.vector.tensor_tensor(r_a[:, :, 6:7], r_a[:, :, 6:7], r_a[:, :, 7:8], ALU.mult))
            link(nc.vector.reciprocal(w1c, r_a[:, :, 6:7]))
            link(nc.vector.tensor_tensor(w2c, w1c, r_a[:, :, GROUPS:GROUPS + 1], ALU.mult))
            link(nc.vector.tensor_tensor(hot1, hot1, over(w1c, EXPERTS_PER_GROUP), ALU.mult))
            link(nc.vector.tensor_tensor(hot2, hot2, over(w2c, EXPERTS_PER_GROUP), ALU.mult))
            link(nc.vector.tensor_tensor(tmp8, hot1, hot2, ALU.add))
            for tt in range(TT):
                link(nc.vector.tensor_tensor(combine[:, tt, :].rearrange("p (g e) -> p g e", g=GROUPS),
                                             g_hot[:, tt].unsqueeze(2).broadcast_to((P, GROUPS, EXPERTS_PER_GROUP)),
                                             tmp8[:, tt].unsqueeze(1).broadcast_to((P, GROUPS, EXPERTS_PER_GROUP)), ALU.mult))
            dve.wait_ge(rank_ps, 1)
            ranks = PS[:, 1, 0:TT * EXPERTS].rearrange("p (a e) -> p a e", a=TT)
            link(nc.vector.scalar_tensor_tensor(rank, ranks, 1.0, routed, ALU.add, ALU.mult))
            link(nc.vector.tensor_scalar(rank, rank, -1.0, None, ALU.add))

            def select(first, e0, n_experts, w):
                rk, cb = rank[:, :, e0], combine[:, :, e0]
                for tt in range(TT):
                    one = sel[:, tt, 0:n_experts * SLOTS].rearrange("p (e s) -> p e s", e=n_experts)
                    two = selw[:, tt, 0:n_experts * SLOTS].rearrange("p (e s) -> p e s", e=n_experts)
                    link(nc.vector.tensor_tensor(one, rk[:, tt].unsqueeze(2).broadcast_to((P, n_experts, SLOTS)),
                                                 first.unsqueeze(1).broadcast_to((P, n_experts, SLOTS)), ALU.is_equal))
                    ins = nc.vector.tensor_tensor(two, one, cb[:, tt].unsqueeze(2).broadcast_to((P, n_experts, SLOTS)), ALU.mult)
                return ins

            select(iota_s[:, :], slice(0, PACK), PACK, None).then_inc(sel_ready, 1)

            def take_gathered(pack):
                for r in range(2):
                    dve.wait_ge(gath_ps, 2 * pack + (r + 1))
                    ks = slice(4 * r, 4 * r + 4)
                    nc.vector.tensor_tensor(XG[:, ks, :], PS[:, B_GATHER, :].rearrange("p (k s) -> p k s", k=4),
                                            gains[:, G_FFN, ks].unsqueeze(2).broadcast_to((P, 4, P)), ALU.mult).then_inc(xg_ready, 1)

            take_gathered(0)
            dve.sem_inc(comb_free, 2)
            dve.wait_ge(count_ps, 1)
            link(nc.vector.tensor_copy(extra_f[:, 0, :], PS[0:1, B_DOWN + 1, 0:EXPERTS]))
            link(nc.vector.tensor_scalar(extra_f[:, 1, :], extra_f[:, 0, :], float(SLOTS), None, ALU.is_gt))
            for k in range(2, T // SLOTS):
                link(nc.vector.scalar_tensor_tensor(extra_f[:, 1, :], extra_f[:, 0, :], float(SLOTS * k), extra_f[:, 1, :], ALU.is_gt, ALU.add))
            link(nc.vector.memset(extra_f[:, 2, :], 1.0))
            link(nc.vector.tensor_tensor_scan(extra_f[:, 3, :], extra_f[:, 2, :], extra_f[:, 1, :], 0.0, ALU.mult, ALU.add))
            sums = extra_f[:, 3, :]
            tiles = iota_s[0:1, 0:16]
            link(nc.vector.tensor_tensor(extra_cmp[:, :, :], sums.unsqueeze(1).broadcast_to((1, 16, EXPERTS)),
                                         tiles.unsqueeze(2).broadcast_to((1, 16, EXPERTS)), ALU.is_le))
            link(nc.vector.tensor_reduce(extra_row[:, 1, :], extra_cmp[:, :, :], AX_X, ALU.add))
            link(nc.vector.tensor_tensor(extra_cmp[:, :, :], extra_cmp[:, :, :], sums.unsqueeze(1).broadcast_to((1, 16, EXPERTS)), ALU.mult))
            link(nc.vector.tensor_reduce(extra_row[:, 2, :], extra_cmp[:, :, :], AX_X, ALU.max))
            link(nc.vector.tensor_tensor(extra_row[:, 2, :], tiles, extra_row[:, 2, :], ALU.subtract))
            link(nc.vector.tensor_scalar(extra_row[:, 2, :], extra_row[:, 2, :], 1.0, float(SLOTS), ALU.add, ALU.mult))
            link(nc.vector.tensor_scalar(extra_row[:, 0, :], tiles, 0.0, sums[:, EXPERTS - 1:EXPERTS], ALU.mult, ALU.add))
            nc.vector.tensor_copy(extra_i[:, :, :], extra_row[:, :, :]).then_inc(extra_ready, 1)

            def hidden(e, i):
                dve.wait_ge(silu_ready, e + 1)
                nc.vector.tensor_tensor(hid[:, i % 2, :], silu[:, i % 2, :], PS[:, B_GATE + i % 2, P:2 * P], ALU.mult).then_inc(hid_ready, 1)

            def collect(e, i):
                dve.wait_ge(down_done, e + 1)
                for j in range(2, 4):
                    ins = nc.vector.tensor_copy(Y[SLOTS * i:SLOTS * (i + 1), D_STRIP * j:D_STRIP * (j + 1)],
                                                PS[SLOTS * j:SLOTS * (j + 1), B_DOWN + i % 2, 0:D_STRIP])
                ins.then_inc(y_dve, 1)

            def add_pack(pack):
                for n in range(4):
                    half, tt = slice((n // 2) * BLOCK, (n // 2 + 1) * BLOCK), n % 2
                    dve.wait_ge(comb_ps, 4 * pack + (n + 2))
                    nc.vector.tensor_tensor(X[:, tt, half], X[:, tt, half], PS[:, B_COMB + n % 2, :], ALU.add).then_inc(comb_free, 1)

            def select_loop(base, first, e0, n_experts):
                rk, cb = rank[:, :, e0], combine[:, :, e0]
                for tt in range(TT):
                    one = sel[:, tt, 0:n_experts * SLOTS].rearrange("p (e s) -> p e s", e=n_experts)
                    nc.vector.tensor_tensor(one, rk[:, tt].unsqueeze(2).broadcast_to((P, n_experts, SLOTS)),
                                            first.unsqueeze(1).broadcast_to((P, n_experts, SLOTS)), ALU.is_equal).then_inc(sel_made, 1)
                dve.wait_ge(sel_made, base + TT)
                for tt in range(TT):
                    one = sel[:, tt, 0:n_experts * SLOTS].rearrange("p (e s) -> p e s", e=n_experts)
                    two = selw[:, tt, 0:n_experts * SLOTS].rearrange("p (e s) -> p e s", e=n_experts)
                    ins = nc.vector.tensor_tensor(two, one, cb[:, tt].unsqueeze(2).broadcast_to((P, n_experts, SLOTS)), ALU.mult)
                ins.then_inc(sel_ready, 1)

            with dve.Fori(0, PACKS - 1) as pack:
                e = PACK * pack
                hidden(e, 0)
                dve.wait_ge(gath_ps, 2 * pack + 2)
                dve.wait_ge(ct_ps, pack + 1)
                select_loop(TT * pack, iota_s[:, :], bass.ds(e + PACK, PACK), PACK)
                hidden(e + 1, 1)
                collect(e, 0)
                hidden(e + 2, 2)
                collect(e + 1, 1)
                hidden(e + 3, 3)
                collect(e + 2, 2)
                take_gathered(pack + 1)
                collect(e + 3, 3)
                add_pack(pack)
            for i in range(PACK):
                hidden(EXPERTS - PACK + i, i)
                collect(EXPERTS - PACK + i, i)
            add_pack(PACKS - 1)
            dve.wait_ge(gath_ps, 2 * PACKS)
            dve.wait_ge(ct_ps, PACKS)
            link(nc.vector.memset(sel, 0.0))
            link(nc.vector.memset(selw, 0.0))
            dve.wait_ge(first_ps, 1)
            nc.vector.tensor_copy(first_rank[:, :], PS[:, B_DOWN + 1, 0:16]).then_inc(first_ready, 1)
            dve.wait_ge(first_ready, 1)
            n_extra = dve.value_load(extra_i[0:1, 0, 0:1], min_val=0, max_val=EXTRA_MAX)
            with dve.Fori(0, EXTRA_MAX) as j:
                with dve.If(j < n_extra):
                    e = dve.value_load(extra_i[0:1, 1, bass.ds(j, 1)], min_val=0, max_val=EXPERTS - 1)
                    dve.wait_ge(gath_ps, 2 * j + 2 * PACKS)
                    dve.wait_ge(ct_ps, j + PACKS)
                    nc.vector.tensor_scalar(rank_iota[:, :], iota_s[:, :], first_rank[:, bass.ds(j, 1)], None, ALU.add).then_inc(slot_ranks, 1)
                    dve.wait_ge(slot_ranks, j + 1)
                    select_loop(TT * j + TT * (PACKS - 1), rank_iota[:, :], bass.ds(e, 1), 1)
                    take_gathered(j + PACKS)
                    hidden(j + EXPERTS, 0)
                    collect(j + EXPERTS, 0)
                    add_pack(j + PACKS)
            dve.wait_ge(comb_free, 4 * n_extra + (4 * PACKS + 2))
            dve.sem_inc(moe_done, 1)

            dve.wait_ge(tables_ready, 3)
            lam = VEC[:, V_LAM:V_LAM + RC]
            inverse_rms("first", 10, TT)
            for tt in range(TT):
                nc.vector.scalar_tensor_tensor(X[:, tt, :], X[:, tt, :], rstd[:, 10 + tt:11 + tt], g_first[:, :], ALU.mult, ALU.mult).then_inc(x2_ready, 1)
            dve.wait_ge(lam_ln, 1)
            link(nc.vector.tensor_scalar(sp8[:, 1, :], lam, -1.0, 0.0, ALU.mult, ALU.max))
            link(nc.vector.tensor_tensor(sp8[:, 1, :], sp8[:, 1, :], sp8[:, 0, :], ALU.add))
            link(nc.vector.tensor_scalar(sp8[:, 2, :], sp8[:, 1, :], LRU_C, None, ALU.mult))
            dve.wait_ge(x2_ready, TT)
            normalise("mix2", 12)
            apply_gain("mix2", G_MIX2)

            def rest_hT(name):
                for n in range(4):
                    tt, ks = n // 2, slice(4 * (n % 2), 4 * (n % 2) + 4)
                    dve.wait_ge(hT_hi_ready[name], n + 1)
                    at = slice(tt * P, (tt + 1) * P)
                    nc.vector.tensor_tensor(HT_rest[:, ks, at], HT[:, ks, at], HT_hi[:, tt, ks, :].bitcast(F32),
                                            ALU.subtract).then_inc(hT_rest_ready[name], 1)

            dve.sem_inc(z_bank_free, 4)
            rest_hT("mix2")

            def conv_a(pair):
                if pair == 0:
                    dve.wait_ge(pads_ready, 1)
                dve.wait_ge(z_bank_free, 4 + 2 * (IN2_ORDER.index(pair) + 1))
                chs = slice(2 * pair, 2 * pair + 2)
                link(nc.vector.tensor_tensor(UP[:, chs, PAD:], UP[:, chs, PAD:], Z[:, Z_GA + 2 * pair:Z_GA + 2 * pair + 2, :], ALU.mult))
                for ch in range(2 * pair, 2 * pair + 2):
                    nc.vector.tensor_scalar(CU[:, ch, :], UP[:, ch, 0:T], CAW[:, ch:ch + 1], VEC[:, V_CAB + ch:V_CAB + ch + 1],
                                            ALU.mult, ALU.add).then_inc(tap_step[ch % 2], 1)
                with dve.Fori(0, PAD // TAP_ROUND) as r:
                    for j in range(TAP_ROUND):
                        for ch in range(2 * pair, 2 * pair + 2):
                            dve.wait_ge(tap_step[ch % 2], TAP_ROUND * r + (TAPS_A * pair + j + 1))
                            src = UP[:, ch, bass.ds(TAP_ROUND * r + (j + 1), T)]
                            nc.vector.scalar_tensor_tensor(CU[:, ch, :], src, CAW[:, bass.ds(TAP_ROUND * KC * r + ((j + 1) * KC + ch), 1)],
                                                           CU[:, ch, :], ALU.mult, ALU.add).then_inc(tap_step[ch % 2], 1)

            conv_a(0)
            dve.wait_ge(z_bank_free, 4 + 2 * (IN2_ORDER.index((C_XB + RC) // 2 - 1) + 1))
            for pair in range(RC // 2):
                for k in range(TAPS_B):
                    for i in range(2):
                        n = 2 * pair + i
                        tap = (TAPS_B - 1 - k) * RC + n
                        src, dst = Z[:, Z_XB + n, 0:T - k], VB[:, n, k:T]
                        if k == 0:
                            ins = nc.vector.tensor_scalar(dst, src, CBW[:, tap:tap + 1], VEC[:, V_CBB + n:V_CBB + n + 1], ALU.mult, ALU.add)
                        else:
                            dve.wait_ge(short_step[i], TAPS_B * pair + k)
                            ins = nc.vector.scalar_tensor_tensor(dst, src, CBW[:, tap:tap + 1], dst, ALU.mult, ALU.add)
                        ins.then_inc(short_step[i], 1)
            for i in range(2):
                dve.wait_ge(short_step[i], TAPS_B * RC // 2)
            dve.sem_inc(v2_ready, 1)
            conv_a(1)
            for g in range(RG):
                rows_ = slice(3 * g, 3 * g + 3)
                dve.wait_ge(lru_gates, g + 1)
                link(nc.vector.tensor_tensor(VB[:, rows_, :], VB[:, rows_, :], IB[:, g % 2, :, :], ALU.mult))
                nc.vector.tensor_tensor(RB[:, rows_, :], RB[:, rows_, :], sp8[:, 2, rows_].unsqueeze(2).broadcast_to((P, 3, T)), ALU.mult).then_inc(lru_log, 1)
            conv_a(2)
            for g in range(RG):
                rows_ = slice(3 * g, 3 * g + 3)
                th = Z[:, Z_XB + 3 * g:Z_XB + 3 * g + 3, :]
                dve.wait_ge(lru_exp, g + 1)
                link(nc.vector.tensor_tensor(RB[:, rows_, :], AB[:, rows_, :], AB[:, rows_, :], ALU.mult))
                nc.vector.scalar_tensor_tensor(th, RB[:, rows_, :], 1.0, th, ALU.add, ALU.mult).then_inc(lru_square, 1)
            for g in range(RG):
                rows_ = slice(3 * g, 3 * g + 3)
                th = Z[:, Z_XB + 3 * g:Z_XB + 3 * g + 3, :]
                dve.wait_ge(lru_root, g + 1)
                link(nc.vector.memset(th[:, :, 0:1], 1.0))
                link(nc.vector.tensor_tensor(VB[:, rows_, :], VB[:, rows_, :], th, ALU.mult))
                for n in range(3 * g, 3 * g + 3):
                    ins = nc.vector.tensor_tensor_scan(RB[:, n, :], AB[:, n, :], VB[:, n, :], 0.0, ALU.mult, ALU.add)
                link(ins)
                if g == 0:
                    dve.wait_ge(z_bank_free, 4 + 2 * (IN2_ORDER.index((C_GB + RC) // 2 - 1) + 1))
                nc.vector.tensor_tensor(RB[:, rows_, :], RB[:, rows_, :], Z[:, Z_GB + 3 * g:Z_GB + 3 * g + 3, :], ALU.mult).then_inc(h_ready, 1)
            conv_a(3)
            for i in range(2):
                dve.wait_ge(tap_step[i], TAPS_A * KC // 2)
            dve.sem_inc(conv_a_ready, 1)
            dve.wait_ge(mean_ps, 1)
            nc.vector.tensor_tensor(CU, CU, PS[:, 4, 0:T].unsqueeze(1).broadcast_to((P, KC, T)), ALU.subtract).then_inc(centred, 1)
            dve.wait_ge(var_ps, 1)
            nc.vector.tensor_scalar(inv_ln, PS[:, 5, 0:T], EPS, None, ALU.add).then_inc(var_in, 1)
            dve.wait_ge(var_root, 1)
            link(nc.vector.reciprocal(inv_ln, inv_ln))
            nc.vector.tensor_tensor(CU, CU, inv_ln.unsqueeze(1).broadcast_to((P, KC, T)), ALU.mult).then_inc(scaled, 1)
            dve.wait_ge(z_bank_free, 4 + ZC)

            def bank_pair(n):
                return PS[:, n, :].rearrange("p (c t) -> p c t", c=2)

            for n in range(KC // 2):
                dve.wait_ge(y_ps, 2 * n + 2)
                zb = Z[:, Z_SB + 2 * n:Z_SB + 2 * n + 2, :]
                link(nc.vector.tensor_tensor(zb, zb, bank_pair(n), ALU.mult))
            for n in range(KC // 2):
                dve.wait_ge(y_ps, KC + 2 * n + 2)
                za = Z[:, Z_SA + 2 * n:Z_SA + 2 * n + 2, :]
                link(nc.vector.tensor_tensor(za, za, bank_pair(4 + n), ALU.mult))
                nc.vector.tensor_tensor(za, za, Z[:, Z_SB + 2 * n:Z_SB + 2 * n + 2, :], ALU.add).then_inc(m_ready, 1)

            def rest_mlp(n):
                dve.wait_ge(mlp_hi_ready, n + 1)
                nc.vector.tensor_tensor(ring_rest[n % 4][:, :], slot[n % 4], mlp_hi[n % 4][:, :].bitcast(F32),
                                        ALU.subtract).then_inc(mlp_rest_ready, 1)

            for n in range(3):
                rest_mlp(n)
            for n in range(4):
                dve.wait_ge(o_ps, n + 1)
                half = slice((n // 2) * BLOCK, (n // 2 + 1) * BLOCK)
                nc.vector.tensor_tensor(X[:, n % 2, half], X[:, n % 2, half], PS[:, n, :], ALU.add).then_inc(x3_ready, 1)
            dve.wait_ge(x3_ready, 4)
            normalise("mlp2", 14)
            apply_gain("mlp2", G_MLP2)
            dve.wait_ge(hT_ready["mlp2"], 4)
            dve.sem_inc(f_bank_free, 4)
            rest_hT("mlp2")
            rest_mlp(3)
            for half_n in range(2):
                for b in range(4):
                    at = 4 * half_n + b
                    dve.wait_ge(f_bank_free, 4 * at + 8)
                    f4 = FT[:, 4 * b:4 * b + 4, :]
                    nc.vector.tensor_tensor(f4, f4, f4, ALU.mult).then_inc(f_squared, 1)
                    rest_mlp(8 * half_n + b + 4)
                    dve.wait_ge(f_hi_ready, at + 1)
                    nc.vector.tensor_tensor(FT_rest[:, 4 * b:4 * b + 4, :], f4, FT_hi[:, 4 * b:4 * b + 4, :].bitcast(F32),
                                            ALU.subtract).then_inc(f_ready, 1)
                if half_n == 0:
                    for b in range(4):
                        rest_mlp(8 + b)
            for n in range(4):
                dve.wait_ge(mlp_ps, 1)
                half = slice((n % 2) * BLOCK, (n % 2 + 1) * BLOCK)
                nc.vector.tensor_copy(X[:, n // 2, half], PS[:, 2 * (n % 2) + n // 2, :]).then_inc(x4_ready, 1)
            inverse_rms("last", 0, TT)
            for tt in range(TT):
                nc.vector.scalar_tensor_tensor(fin[:, tt, :], X[:, tt, :], rstd[:, tt:tt + 1], g_last[:, :], ALU.mult, ALU.mult).then_inc(fin_ready, 1)

        @block.tensor
        def _(pe):
            def turn_rows(name):
                for n in range(4):
                    tt, half = n // 2, n % 2
                    if n % 2 == 0:
                        pe.wait_ge(rows[name], (tt + 1) * (2 if name == "mix" else 1))
                    for k in range(4):
                        ins = nc.tensor.transpose(PS[:, 4 + n, k * P:(k + 1) * P], HN[:, tt, 4 * half + k, :], ident[:, :])
                    ins.then_inc(turned[name], 1)

            pe.wait_ge(consts, N_CONST)
            turn_rows("attn")
            pe.wait_ge(hT_ready["attn"], 4)
            for n in range(8):
                if n % 4 == 0:
                    pe.wait_ge(loaded[n // 4], pre_count(n // 4))
                if n >= 4:
                    pe.wait_ge(qk_ready, n - 3)
                for k in range(KC):
                    ins = nc.tensor.matmul(PS[:, n % 4, 0:T], chunked(n // 4, BLOCK)[:, k, (n % 4) * P:(n % 4 + 1) * P],
                                           HT[:, k, :], start=k == 0, stop=k == KC - 1)
                ins.then_inc(qk_ps, 1)
            for n in range(6):
                b, tt = 2 + n // 2, n % 2
                pe.wait_ge(loaded[b], pre_count(b))
                if n >= 4:
                    pe.wait_ge(v_ready, n - 3)
                for k in range(KC):
                    ins = nc.tensor.matmul(PS[:, 4 + n % 4, :], HT[:, k, tt * P:(tt + 1) * P], chunked(b, BLOCK)[:, k, :],
                                           start=k == 0, stop=k == KC - 1)
                ins.then_inc(vug_ps, 1)

            def scores(h):
                if h >= 2:
                    pe.wait_ge(att_x, h - 1)
                k, q = kT[:, h // 2, :], qT[:, h, :]
                nc.tensor.matmul(PS[:, h % 2, 0:T], k[:, 0:P], q, start=True, stop=False, skip_group_check=True)
                nc.tensor.matmul(PS[:, h % 2, T:T + P], k[:, P:T], q[:, P:T], start=False, stop=False,
                                 skip_group_check=True).then_inc(score_ps, 1)

            def later_keys(h):
                pe.wait_ge(att_sp, h + 1)
                s = att_s[:, h % 2, :]
                nc.tensor.matmul(PS[:, h % 2, 0:T], tri_neg[:, :], s[:, 0:T], start=False, stop=False, skip_group_check=True)
                nc.tensor.matmul(PS[:, h % 2, P:T], neg_ones[:, :], s[:, T:T + P], start=False, stop=False, skip_group_check=True)
                nc.tensor.matmul(PS[:, h % 2, T:T + P], tri_neg[:, :], s[:, T:T + P], start=False, stop=True,
                                 skip_group_check=True).then_inc(att_ps, 1)

            def weighted_values(h):
                pe.wait_ge(att_exp, h + 1)
                a, cols = att_a[:, h % 2, :], slice(h * HEAD_DIM, (h + 1) * HEAD_DIM)
                nc.tensor.matmul(PS[:, 2, cols], a[:, 0:P], V[:, 0, cols], start=True, stop=True)
                nc.tensor.matmul(PS[:, 3, cols], a[:, P:T], V[:, 0, cols], start=True, stop=False)
                nc.tensor.matmul(PS[:, 3, cols], a[:, T:T + P], V[:, 1, cols], start=False, stop=True).then_inc(av_done, 1)

            pe.wait_ge(qk_ready, 8)
            pe.wait_ge(v_ready, TT)
            def spatial_weights():
                pe.wait_ge(small_loaded, 16 * N_SMALL)
                pe.wait_ge(gelu_ready, 4)
                for n in range(2):
                    for k in range(4):
                        ins = nc.tensor.transpose(PS[:, 6 + n, k * P:(k + 1) * P], wsp[:, 4 * n + k, :], ident[:, :])
                    ins.then_inc(wsp_turned, 1)
                nc.tensor.transpose(PS[:, 4, 0:HEADS], bsp[0:HEADS], ident[0:HEADS, 0:HEADS]).then_inc(wsp_turned, 1)

            scores(0)
            for h in range(HEADS):
                if h + 1 < HEADS:
                    scores(h + 1)
                later_keys(h)
                if h == 3:
                    spatial_weights()
                if h >= 1:
                    weighted_values(h - 1)
            weighted_values(HEADS - 1)
            pe.wait_ge(wspT_ready, 3)
            for tt in range(TT):
                pe.wait_ge(vg_ready, tt + 1)
                for h in range(HEADS):
                    cols = slice(h * HEAD_DIM, (h + 1) * HEAD_DIM)
                    ins = nc.tensor.matmul(PS[:, 4 + tt, cols], wspT[:, h, :], VG[:, tt, cols], start=True, stop=True)
                ins.then_inc(sgu_ps, 1)
            pe.wait_ge(table_loaded, 16 * N_TABLE)
            at = 0
            for raw, n in ((vec_raw, P), (caw_raw[:, 0, :], P), (caw_raw[:, 1, :], TAPS_A * KC - P), (cbw_raw, TAPS_B * RC)):
                ins = nc.tensor.transpose(PS[:, 0, at:at + n], raw[0:n], ident[0:n, 0:n])
                at += n
            ins.then_inc(tables_turned, 1)
            turn_rows("mix")
            pe.wait_ge(hT_ready["mix"], 4)
            pe.wait_ge(tables_ready, 3)
            for n in range(4):
                half, tt = n // 2, n % 2
                w = IN1_BLOCKS + half
                pe.wait_ge(loaded[w % RING], pre_count(w))
                for k in range(KC):
                    ins = nc.tensor.matmul(PS[:, n, :], HT[:, k, tt * P:(tt + 1) * P], chunked(w % RING, BLOCK)[:, k, :],
                                           start=k == 0, stop=k == KC - 1)
                ins.then_inc(out1_ps, 1)
            turn_rows("ffn")
            pe.wait_ge(hT_ready["ffn"], 4)
            pe.wait_ge(router_loaded, 16 * N_ROUTER)
            for tt in range(TT):
                at = tt * (GROUPS + EXPERTS)
                for k in range(KC):
                    nc.tensor.matmul(PS[:, 0, at:at + GROUPS], HT[:, k, tt * P:(tt + 1) * P], wr_group[:, k, :],
                                     start=k == 0, stop=k == KC - 1)
                for k in range(KC):
                    ins = nc.tensor.matmul(PS[:, 0, at + GROUPS:at + GROUPS + EXPERTS].rearrange("p (g e) -> p g e", g=GROUPS),
                                           HT[:, k, tt * P:(tt + 1) * P], wr_expert[:, :, k, :], start=k == 0, stop=k == KC - 1)
            ins.then_inc(logits_ps, 1)
            pe.wait_ge(routed_ready, TT)
            nc.tensor.matmul(PS[:, 1, 0:EXPERTS], before[:, :], routed[:, 0, :], start=True, stop=True)
            nc.tensor.matmul(PS[:, 1, EXPERTS:2 * EXPERTS], ones[:, :], routed[:, 0, :], start=True, stop=False)
            nc.tensor.matmul(PS[:, 1, EXPERTS:2 * EXPERTS], before[:, :], routed[:, 1, :], start=False, stop=True).then_inc(rank_ps, 1)
            nc.tensor.matmul(PS[0:1, B_DOWN + 1, 0:EXPERTS], ones[:, 0:1], routed[:, 0, :], start=True, stop=False)
            nc.tensor.matmul(PS[0:1, B_DOWN + 1, 0:EXPERTS], ones[:, 0:1], routed[:, 1, :], start=False, stop=True).then_inc(count_ps, 1)

            def gather(pack):
                pe.wait_ge(sel_ready, pack + 1)
                pe.wait_ge(ct_ready, pack)
                for r in range(2):
                    pe.wait_ge(xg_ready, 2 * pack + r)
                    for k in range(4):
                        for tt in range(TT):
                            ins = nc.tensor.matmul(PS[:, B_GATHER, k * P:(k + 1) * P], HN[:, tt, 4 * r + k, :], sel[:, tt, :],
                                                   start=tt == 0, stop=tt == TT - 1)
                    ins.then_inc(gath_ps, 1)
                pe.wait_ge(xg_ready, 2 * pack + 2)
                for tt in range(TT):
                    ins = nc.tensor.transpose(PS[:, B_GATHER, tt * P:(tt + 1) * P], selw[:, tt, :], ident[:, :])
                ins.then_inc(ct_ps, 1)

            def gate_up(s, i):
                w = mem[:, s * SLOT_FLOATS:(s + 2) * SLOT_FLOATS].rearrange("p (w k n) -> p w k n", w=2, k=KC)
                for k in range(KC):
                    for j in range(STRIPS):
                        ins = nc.tensor.matmul(PS[SLOTS * j:SLOTS * (j + 1), B_GATE + i % 2, 0:2 * F_STRIP].rearrange("p (w n) -> p w n", w=2),
                                               XG[:, k, SLOTS * i:SLOTS * (i + 1)], w[:, :, k, F_STRIP * j:F_STRIP * (j + 1)],
                                               start=k == 0, stop=k == KC - 1, tile_position=(0, SLOTS * j))
                ins.then_inc(gu_done, 1)

            def turn_hidden(e, i):
                pe.wait_ge(hid_ready, e + 1)
                nc.tensor.transpose(PS[:, B_TURN, 0:P], hid[:, i % 2, :], ident[:, :]).then_inc(hidT_ps, 1)

            def down(e, s, i):
                pe.wait_ge(hidT_ready, e + 1)
                w = chunked(s, D)
                for k in range(STRIPS):
                    for j in range(STRIPS):
                        ins = nc.tensor.matmul(PS[SLOTS * j:SLOTS * (j + 1), B_DOWN + i % 2, 0:D_STRIP],
                                               hidT[:, i % 2, SLOTS * k:SLOTS * (k + 1)], w[:, k, D_STRIP * j:D_STRIP * (j + 1)],
                                               start=k == 0, stop=k == STRIPS - 1, tile_position=(0, SLOTS * j))
                ins.then_inc(down_done, 1)

            def combine_pack(pack, y_count):
                pe.wait_ge(y_act, y_count)
                pe.wait_ge(y_dve, y_count)
                pe.wait_ge(ct_ready, pack + 1)
                for n in range(4):
                    half, tt = n // 2, n % 2
                    pe.wait_ge(comb_free, 4 * pack + (n + 1))
                    nc.tensor.matmul(PS[:, B_COMB + n % 2, :], CT[:, tt * P:(tt + 1) * P], Y[:, half * BLOCK:(half + 1) * BLOCK],
                                     start=True, stop=True).then_inc(comb_ps, 1)

            def expert_slots(i):
                return [(PRE + 3 * i + part) % RING for part in range(3)]

            def expert_gate_up(pack, i):
                s = expert_slots(i)
                if i == 0:
                    pe.wait_ge(xg_ready, 2 * pack + 2)
                for part in range(2):
                    pe.wait_ge(loaded[s[part]], 32 * pack + 16 * ((PRE + 3 * i + part) // RING + 1))
                gate_up(s[0], i)

            def expert_down(pack, i):
                turn_hidden(PACK * pack + i, i)
                s = expert_slots(i)[2]
                pe.wait_ge(loaded[s], 32 * pack + 16 * ((PRE + 3 * i + 2) // RING + 1))
                pe.wait_ge(extra_ready, 1)
                down(PACK * pack + i, s, i)

            def residual_first():
                for n in range(4):
                    half, tt = n // 2, n % 2
                    nc.tensor.matmul(PS[:, n, :], ident[:, :], X[:, tt, half * BLOCK:(half + 1) * BLOCK], start=True, stop=False,
                                     skip_group_check=True)

            gather(0)
            pe.sem_inc(comb_ps, 1)
            with pe.Fori(0, PACKS - 1) as pack:
                expert_gate_up(pack, 0)
                for i in range(PACK):
                    if i + 1 < PACK:
                        expert_gate_up(pack, i + 1)
                    else:
                        gather(pack + 1)
                    expert_down(pack, i)
                combine_pack(pack, PACK * pack + PACK)
            expert_gate_up(PACKS - 1, 0)
            for i in range(PACK):
                if i + 1 < PACK:
                    expert_gate_up(PACKS - 1, i + 1)
                expert_down(PACKS - 1, i)
            combine_pack(PACKS - 1, EXPERTS)
            pe.wait_ge(extra_ready, 1)
            nc.tensor.matmul(PS[:, B_DOWN + 1, 0:16], ones[0:1, :], extra_row[0:1, 2, :], start=True, stop=True).then_inc(first_ps, 1)
            n_extra = pe.value_load(extra_i[0:1, 0, 0:1], min_val=0, max_val=EXTRA_MAX)
            pe.wait_ge(first_ready, 1)
            with pe.Fori(0, EXTRA_MAX) as j:
                with pe.If(j < n_extra):
                    gather(j + PACKS)
                    for part in range(2):
                        pe.wait_ge(extra_loaded[part], 16 * j + 16)
                    pe.wait_ge(xg_ready, 2 * j + (2 * PACKS + 2))
                    gate_up(4, 0)
                    turn_hidden(j + EXPERTS, 0)
                    pe.wait_ge(extra_loaded[2], 16 * j + 16)
                    down(j + EXPERTS, 0, 0)
                    combine_pack(j + PACKS, j + (EXPERTS + 1))

            turn_rows("mix2")
            pe.wait_ge(hT_rest_ready["mix2"], 4)

            def three_passes(dst, terms, start, stop):
                for n, (s_hi, s_rest, m_hi, m_rest) in enumerate(terms):
                    nc.tensor.matmul(dst, s_hi, m_hi, start=start and n == 0, stop=False, skip_group_check=True)
                    nc.tensor.matmul(dst, s_hi, m_rest, start=False, stop=False, skip_group_check=True)
                    ins = nc.tensor.matmul(dst, s_rest, m_hi, start=False, stop=stop and n == len(terms) - 1, skip_group_check=True)
                return ins

            def by_token_tile(v):
                return v.rearrange("p (a t) -> p a t", a=TT)

            def times_hT(dst, hi, rest, cols):
                return three_passes(by_token_tile(dst), [(hi[:, k, cols], rest[:, k, cols], HT_hi[:, :, k, :], by_token_tile(HT_rest[:, k, :]))
                                                         for k in range(KC)], True, True)

            def z_round(r):
                for h in range(IN2_GROUP):
                    pe.wait_ge(z_rest_ready, IN2_GROUP * r + (h + 1))
                    hi, rest = (v.rearrange("p (k n) -> p k n", n=HALF) for v in (z_hi[:, h % HI, :], z_rest(h)))
                    for i in range(2):
                        pe.wait_ge(z_bank_free, 2 * IN2_GROUP * r + (2 * h + i + 1))
                        times_hT(PS[:, (2 * h + i) % 4, 0:T], hi, rest, slice(i * P, (i + 1) * P)).then_inc(z_ps, 1)

            with pe.Fori(0, LRU_AFTER) as r:
                z_round(r)
            pe.wait_ge(bd_loaded, 16 * N_BD)
            pe.wait_ge(v2_ready, 1)
            for g in range(RG):
                if g >= 1:
                    pe.wait_ge(lru_gates, g)
                for bd, bank in ((BDA, 4), (BDX, 6)):
                    for o in range(3):
                        dst = PS[:, bank + o // 2, (o % 2) * T:(o % 2 + 1) * T]
                        pieces = [(o, 32 * o, 0, P)]
                        pieces += [[(1, 0, 96, 32)], [(0, P, 0, 64), (2, 0, 64, 64)], [(1, 160, 0, 32)]][o]
                        for n, (r, c0, p0, m) in enumerate(pieces):
                            ins = nc.tensor.matmul(dst[p0:p0 + m], bd[:, g, r, c0:c0 + m], VB[:, 3 * g + r, :], start=n == 0,
                                                   stop=n == len(pieces) - 1, skip_group_check=True)
                ins.then_inc(lru_ps, 1)
            with pe.Fori(LRU_AFTER, IN2_HALVES // IN2_GROUP) as r:
                z_round(r)
            pe.wait_ge(z_bank_free, 4 + ZC)
            for n in range(KC):
                if n % 2 == 0:
                    pe.wait_ge(*late_arrived(n // 2))
                if n == 0:
                    pe.wait_ge(h_ready, RG)
                w = slot[n // 2][:, 0:RC * HALF].rearrange("p (k n) -> p k n", n=HALF)
                for k in range(RC):
                    ins = nc.tensor.matmul(PS[:, n // 2, (n % 2) * T:(n % 2 + 1) * T], w[:, k, (n % 2) * P:(n % 2 + 1) * P], RB[:, k, :],
                                           start=k == 0, stop=k == RC - 1)
                ins.then_inc(y_ps, 1)
                if n == PE_MEAN:
                    pe.wait_ge(conv_a_ready, 1)
                    pe.wait_ge(lru_gates, RG)
                    for k in range(KC):
                        ins = nc.tensor.matmul(PS[:, 4, 0:T], mean_ones[:, :], CU[:, k, :], start=k == 0, stop=k == KC - 1)
                    ins.then_inc(mean_ps, 1)
                if n == PE_VAR:
                    pe.wait_ge(sq_ready, 1)
                    for k in range(KC):
                        ins = nc.tensor.matmul(PS[:, 5, 0:T], mean_ones[:, :], Z[:, Z_GA + k, :], start=k == 0, stop=k == KC - 1)
                    ins.then_inc(var_ps, 1)
            for n in range(KC):
                if n % 4 == 0:
                    pe.wait_ge(*late_arrived(L_A + n // 4))
                w = chunked((L_A + n // 4) % 4, BLOCK)
                for k in range(KC):
                    if n == 0:
                        pe.wait_ge(a_ready, k + 1)
                    ins = nc.tensor.matmul(PS[:, 4 + n // 2, (n % 2) * T:(n % 2 + 1) * T], w[:, k, (n % 4) * P:(n % 4 + 1) * P], CU[:, k, :],
                                           start=k == 0, stop=k == KC - 1)
                ins.then_inc(y_ps, 1)
            pe.wait_ge(m_ready, KC // 2)
            for n in range(4):
                half, tt = n // 2, n % 2
                pe.wait_ge(*late_arrived(L_O + half))
                w = chunked((L_O + half) % 4, BLOCK)
                for k in range(KC):
                    ins = nc.tensor.matmul(PS[:, n, :], Z[:, Z_SA + k, tt * P:(tt + 1) * P], w[:, k, :], start=k == 0, stop=k == KC - 1)
                ins.then_inc(o_ps, 1)
            turn_rows("mlp2")
            residual_first()
            pe.wait_ge(hT_rest_ready["mlp2"], 4)
            with pe.Fori(0, 2) as half:
                for b in range(4):
                    pe.wait_ge(mlp_rest_ready, 8 * half + (b + 1))
                    hi, rest = (v.rearrange("p (k n) -> p k n", n=BLOCK) for v in (mlp_hi[b][:, :], ring_rest[b][:, :]))
                    for i in range(4):
                        pe.wait_ge(f_bank_free, 16 * half + (4 * b + i + 1))
                        times_hT(PS[:, 4 + i, 0:T], hi, rest, slice(i * P, (i + 1) * P)).then_inc(f_ps, 1)
                for b in range(4):
                    pe.wait_ge(mlp_rest_ready, 8 * half + (b + 5))
                    pe.wait_ge(f_ready, 4 * half + (b + 1))
                    hi, rest = (v.rearrange("p (k n) -> p k n", n=D) for v in (mlp_hi[b][:, :], ring_rest[b][:, :]))
                    for k in range(4):
                        for n in range(4):
                            h, at = slice((n // 2) * BLOCK, (n // 2 + 1) * BLOCK), slice((n % 2) * P, (n % 2 + 1) * P)
                            ins = three_passes(PS[:, n, :], [(FT_hi[:, 4 * b + k, at], FT_rest[:, 4 * b + k, at], hi[:, k, h], rest[:, k, h])],
                                               False, False)
                    ins.then_inc(w2_used, 1)
            nc.tensor.matmul(PS[:, 3, 0:2], zeros[:, :], zeros[:, 0:2], start=False, stop=True, skip_group_check=True).then_inc(mlp_ps, 1)


_INS = [
    "x", "attn_norm_g", "w_in", "sg_norm_g", "w_spatial", "b_spatial", "sb_out_norm_g", "sg_out_norm_g", "w_out",
    "ffn_norm_g", "w_router_group", "b_router_group", "w_router_expert", "b_router_expert", "w_gate", "w_up",
    "w_down", "final_norm_g", "g_mix_2", "w_in_2", "b_in_2", "conv_a_w_2", "conv_a_b_2", "ln_g_2", "ln_b_2",
    "w_a_out_2", "conv_b_w_2", "conv_b_b_2", "w_rg_a_2", "b_rg_a_2", "w_rg_x_2", "b_rg_x_2", "lam_2", "w_b_out_2",
    "w_o_2", "g_mlp_2", "w_1_2", "w_2_2", "g_final_2",
]


def kernel(**inputs):
    import numpy as _np
    import concourse.bacc as _bacc
    from concourse import mybir as _mybir
    from concourse.bass_utils import run_bass_kernel_spmd as _run

    nc = _bacc.Bacc("TRN2", target_bir_lowering=False, num_devices=1)
    arrays, args = {}, {}
    for name in _INS:
        a = _np.ascontiguousarray(inputs[name])
        arrays[f"in_{name}"] = a
        args[name] = nc.dram_tensor(f"in_{name}", a.shape, _mybir.dt.from_np(a.dtype), kind="ExternalInput").ap()
    out = nc.dram_tensor("out", (1, T, D), _mybir.dt.float32, kind="ExternalOutput").ap()
    build(nc, args, out)
    r = _run(nc, [arrays], core_ids=[0])
    return r.results[0]["out"]
```

```python
from contextlib import ExitStack

import numpy as np

import concourse.bass as bass
from concourse import mybir

F32 = mybir.dt.float32
F32R = mybir.dt.float32r
I32 = mybir.dt.int32
ALU = mybir.AluOpType
ACT = mybir.ActivationFunctionType
AX_X = mybir.AxisListType.X

P = 128
T = 256
TT = T // P
D = 1024
KC = D // P
EPS = 1e-6
HEADS, HEAD_DIM = 8, 64
SB = HEADS * HEAD_DIM
GROUPS, EXPERTS_PER_GROUP = 4, 8
EXPERTS = GROUPS * EXPERTS_PER_GROUP
D_EXPERT = 512
SLOTS = 32
EVEN, ODD = (1, 2, 3), (4, 5, 0)
STRIPS = P // SLOTS
PACK = 4
PACKS = EXPERTS // PACK
F_STRIP = D_EXPERT // STRIPS
D_STRIP = D // STRIPS
EXTRA_MAX = 2 * T // SLOTS - 1
BLOCK = 512
SLOT_FLOATS = KC * BLOCK
RING = 6
IN1_BLOCKS = 5
IN1_ORDER = [3, 4, 2, 0, 1]
IN1_HALVES, IN1_HI = 2 * IN1_BLOCKS, 3
VUG_HALVES = 6
PAIRS = HEADS // 2
OUT1_BLOCKS = 2
PRE = IN1_BLOCKS + OUT1_BLOCKS
D_RNN, RNN_HEAD = 1536, 96
RC = D_RNN // P
RG = 4
TAPS_A, TAPS_B = 31, 4
LRU_C = 8.0
D_FF = 4 * D
FC = D_FF // P
HALF = BLOCK // 2
HALF_FLOATS = KC * HALF
C_VA, C_GA, C_XB, C_GB, C_SA, C_SB, ZC = 0, 8, 16, 28, 40, 48, 56
IN2_ORDER = [4, 0] + list(range(8, 14)) + [5, 1, 6, 2, 7, 3] + list(range(14, 28))
IN2_HALVES = len(IN2_ORDER)
IN2_GROUP = 4
Z_BANKS = 2 * IN2_GROUP
LRU_AFTER = 3
RAW, HI = 4, 4
Z_GA, Z_XB, Z_GB, Z_SA, Z_SB = (c - C_GA for c in (C_GA, C_XB, C_GB, C_SA, C_SB))
PAD = TAPS_A - 1
TAP_ROUND = 6
ACT_ROOT, ACT_H = 17, 23
PE_VAR = 2
MLP_W2 = D_FF // BLOCK
MASKED = -1e30
B_COMB, B_GATE, B_DOWN, B_TURN, B_GATHER = 0, 2, 4, 6, 7

V_BIN, V_CAB, V_LNG, V_LNB, V_CBB, V_BRA, V_BRX, V_LAM = 0, 56, 64, 72, 80, 92, 104, 116


def build(nc, A, out):
    ctx = ExitStack()
    with ctx:
        def sb(name, shape, dt=F32):
            return ctx.enter_context(nc.sbuf_tensor(name, shape, dt))

        def sem(name):
            return ctx.enter_context(nc.semaphore(name))

        ARENA = 17664
        mem = sb("mem", [P, RING * SLOT_FLOATS + ARENA])
        mem_at = nc.sbuf_base - 4 * (RING * SLOT_FLOATS + ARENA)
        slot = [mem[:, s * SLOT_FLOATS:(s + 1) * SLOT_FLOATS] for s in range(RING)]

        def carver(start, end):
            at = [start]

            def carve(*shape):
                n = int(np.prod(shape))
                view = mem[:, at[0]:at[0] + n]
                at[0] += n
                assert at[0] <= end, (at[0], end)
                if len(shape) == 2:
                    view = view.rearrange("p (a b) -> p a b", a=shape[0])
                if len(shape) == 3:
                    view = view.rearrange("p (a b c) -> p a b c", a=shape[0], b=shape[1])
                return view
            return carve

        a0 = RING * SLOT_FLOATS
        aend = a0 + ARENA
        X = sb("X", [P, TT, D])
        HN = sb("HN", [P, TT, KC, P])
        hn_at = nc.sbuf_base - 4 * TT * D
        HT = sb("HT", [P, KC, T])
        ht_at = nc.sbuf_base - 4 * TT * D
        ident = sb("ident", [P, P])
        mean_ones = sb("mean_ones", [P, P])
        masks = sb("masks", [P, 6, P])
        tri_neg = masks[:, 0, :]
        neg_ones = masks[:, 1, :]
        ones = masks[:, 2, :]
        before = masks[:, 3, :]
        upto = masks[:, 4, :]
        maskbias = masks[:, 5, :]
        eps = sb("eps", [P, 1])
        iota_i = sb("iota_i", [P, SLOTS], I32)
        iota_s = sb("iota_s", [P, SLOTS])
        gains = sb("gains", [P, 5, KC])
        G_ATTN, G_MIX, G_FFN, G_MIX2, G_MLP2 = range(5)
        VEC = sb("VEC", [P, P])
        CAW = sb("CAW", [P, TAPS_A * KC])
        CBW = sb("CBW", [P, TAPS_B * RC])
        w_router = sb("w_router", [P, KC, GROUPS + EXPERTS])
        b_router = sb("b_router", [P, GROUPS + EXPERTS])
        g_first = sb("g_first", [P, D])
        g_last = sb("g_last", [P, D])
        ss = sb("ss", [P, 16])
        rstd = sb("rstd", [P, 16])
        sp8 = sb("sp8", [P, 4, RC])
        extra_row = sb("extra_row", [1, 5, 16])
        extra_i = sb("extra_i", [1, 5, 16], I32)
        order_i = sb("order_i", [1, EXPERTS + 1], I32)
        first_rank = sb("first_rank", [P, 16])
        rank_iota = sb("rank_iota", [P, SLOTS])
        PS = ctx.enter_context(nc.psum_tensor("PS", [P, 8, 512], F32))

        c = carver(a0, aend)
        square = c(D)
        qT, kT = c(HEADS, T), c(4, T)
        V, U, VG = c(TT, SB), c(TT, SB), c(TT, SB)
        wsp, wspT = c(HEADS, P), c(HEADS, P)
        sgn_g = c(SB)
        bsp, bspT = c(P), c(HEADS)
        vec_raw, caw_raw, cbw_raw = c(P), c(2, P), c(P)
        att_at = aend - 3 * 4 * 3 * P - 2 * TT * SB
        c = carver(att_at, aend)
        att_e, att_s, att_a = ([c(2, 3 * P) for _ in range(2)] for _ in range(3))
        ao, so = c(TT, SB), c(TT, SB)
        HG = mem[:, a0 + D:a0 + 3 * D].rearrange("p (a d) -> p a d", a=TT)
        third_at = aend - 3 * SLOT_FLOATS
        Y = square
        c = carver(a0 + D, third_at)
        logit = c(TT, GROUPS + EXPERTS)
        r_a, r_b, r_c = c(TT, 16), c(TT, EXPERTS), c(TT, 64)
        routed, combine, rank = c(TT, EXPERTS), c(TT, EXPERTS), c(TT, EXPERTS)
        sel, selw = c(TT, P), c(TT, P)
        XG = c(KC, P)
        CT = c(T)
        silu, hid, hidT = c(2, P), c(2, P), c(2, P)
        extra_f, extra_cmp = c(8, EXPERTS)[0:1], c(16, EXPERTS)[0:1]
        swap = c(4, TT, 1)
        b2_at = 4 * SLOT_FLOATS
        c = carver(b2_at, aend)
        Z = c(ZC - KC, T)
        UP = c(KC, PAD + T)
        CU = c(KC, T)
        VB, RB, AB = c(RC, T), c(RC, T), c(RC, T)
        late_end = b2_at + (ZC - KC) * T + KC * (PAD + T) + KC * T + 3 * RC * T
        BD = RG * 3 * 192
        BDA = AB.rearrange("p a t -> p (a t)")[:, 0:BD].rearrange("p (g r n) -> p g r n", g=RG, r=3)
        BDX = RB.rearrange("p a t -> p (a t)")[:, RC * T - BD:].rearrange("p (g r n) -> p g r n", g=RG, r=3)
        inv_ln = masks[:, 0:2, :].rearrange("p a b -> p (a b)")
        sb_place = Z[:, Z_SB:Z_SB + 6, :].rearrange("p a t -> p (a t)")
        IB = [v[:, 0:3 * T].rearrange("p (a t) -> p a t", a=3)
              for v in (masks[:, :, :].rearrange("p a b -> p (a b)"), g_first, sb_place[:, 0:3 * T], sb_place[:, 3 * T:])]
        c = carver(b2_at, b2_at + 2 * FC // 2 * T)
        FT = c(FC // 2, T)
        fin = FT.rearrange("p a t -> p (a t)")[:, 0:TT * D].rearrange("p (a d) -> p a d", a=TT)

        def parts(name, at, *shape):
            return nc.alloc_sbuf_tensor_at(name, [P] + list(shape), F32R, offset=at)

        ring_rest = [parts(f"ring_rest{s}", mem_at + 4 * s * SLOT_FLOATS, SLOT_FLOATS) for s in range(RING)]
        in1_hi = [parts(f"in1_hi{n}", mem_at + 4 * (att_at + n * HALF_FLOATS), KC, HALF) for n in range(IN1_HI)]
        out1_hi = [parts(f"out1_hi{n}", mem_at + 4 * at, KC, HALF)
                   for n, at in enumerate((4 * SLOT_FLOATS, 4 * SLOT_FLOATS + HALF_FLOATS, a0 + D, a0 + D + HALF_FLOATS))]
        z_hi_part = [parts(f"z_hi{n}", mem_at + 4 * s * SLOT_FLOATS, 2, HALF_FLOATS) for n, s in enumerate((3, 0))]
        HT_hi = parts("HT_hi", hn_at, TT, KC, P)
        HT_rest = parts("HT_rest", ht_at, KC, T)
        FT_rest = parts("FT_rest", mem_at + 4 * b2_at, FC // 2, T)
        FT_hi = parts("FT_hi", mem_at + 4 * (b2_at + FC // 2 * T), FC // 2, T)
        mlp_hi_at = [late_end - 2 * SLOT_FLOATS, late_end - SLOT_FLOATS, b2_at + (ZC - KC) * T, b2_at + Z_SA * T]
        mlp_hi = [parts(f"mlp_hi{n}", mem_at + 4 * at, SLOT_FLOATS) for n, at in enumerate(mlp_hi_at)]

        def at_chunk(ch):
            return mem_at + 4 * (b2_at + ch * T)

        at_up, at_cu, at_vb, at_rb, at_ab = (mem_at + 4 * (late_end - n) for n in (
            3 * RC * T + KC * T + KC * (PAD + T), 3 * RC * T + KC * T, 3 * RC * T, 2 * RC * T, RC * T))
        h_hi, h_rest = parts("h_hi", at_chunk(Z_XB), RC, T), parts("h_rest", at_rb, RC, T)
        a_hi, a_rest = parts("a_hi", at_chunk(Z_GA), KC, T), parts("a_rest", at_cu, KC, T)
        m_hi, m_rest = parts("m_hi", at_chunk(Z_SB), KC, T), parts("m_rest", at_chunk(Z_SA), KC, T)
        wb_hi = [parts(f"wb_hi{n}", at, RC, HALF) for n, at in enumerate((at_vb, at_ab, at_chunk(Z_GB)))]
        wa_hi = [parts(f"wa_hi{n}", at, KC, HALF) for n, at in enumerate((at_up, at_ab, at_chunk(Z_GB + 4), at_vb))]
        wo_hi = [parts(f"wo_hi{n}", at, KC, HALF) for n, at in enumerate((at_chunk(Z_XB), at_chunk(Z_XB + KC), at_chunk(Z_GB + 4), at_chunk(Z_GA)))]

        def half_block(v, n):
            return v.rearrange("p (k n) -> p k n", n=BLOCK)[:, :, (n % 2) * HALF:(n % 2 + 1) * HALF]

        def in1_half(n):
            return half_block(slot[n // 2], n), half_block(ring_rest[n // 2][:, :], n)

        def out1_half(n):
            s = (IN1_BLOCKS + n // 2) % RING
            return half_block(slot[s], n), half_block(ring_rest[s][:, :], n)

        def z_raw(n):
            at = SLOT_FLOATS + (n % RAW) * HALF_FLOATS
            return mem[:, at:at + HALF_FLOATS]

        def z_hi(n):
            return z_hi_part[n % HI // 2][:, n % 2, :]

        def z_rest(n):
            at = (n % RAW) * HALF_FLOATS
            return ring_rest[1 + at // SLOT_FLOATS][:, at % SLOT_FLOATS:at % SLOT_FLOATS + HALF_FLOATS]

        x_loaded, gain_loaded, small_loaded = sem("x_loaded"), sem("gain_loaded"), sem("small_loaded")
        router_loaded, table_loaded = sem("router_loaded"), sem("table_loaded")
        bd_loaded = sem("bd_loaded")
        loaded = [sem(f"loaded{s}") for s in range(RING)]
        third_loaded = sem("third_loaded")
        gained, gained_squares, mix2_in = sem("gained"), sem("gained_squares"), sem("mix2_in")
        swapped = sem("swapped")
        extra_loaded = [sem(f"extra_loaded{s}") for s in range(3)]
        raw_loaded = [sem(f"raw_loaded{s}") for s in range(RAW)]
        late_loaded = [sem(f"late_loaded{s}") for s in range(4)]
        z_hi_ready, z_rest_ready = sem("z_hi_ready"), sem("z_rest_ready")
        split_norms = ("attn", "mix", "mix2", "mlp2")
        hT_hi_ready, hT_rest_ready = sem("hT_hi_ready"), sem("hT_rest_ready")
        late_hi_ready, late_rest_dve, late_rest_pool = sem("late_hi_ready"), sem("late_rest_dve"), sem("late_rest_pool")
        out_hi_ready, out_rest_ready, h_rest_ready = sem("out_hi_ready"), sem("out_rest_ready"), sem("h_rest_ready")
        in1_hi_ready, in1_rest_ready, out1_rest_ready = sem("in1_hi_ready"), sem("in1_rest_ready"), sem("out1_rest_ready")
        mlp_hi_ready, mlp_rest_ready = sem("mlp_hi_ready"), sem("mlp_rest_ready")
        f_squared, f_hi_ready = sem("f_squared"), sem("f_hi_ready")
        pads_ready = sem("pads_ready")
        consts = sem("consts")
        pool_chain, dve_chain, act_chain = sem("pool_chain"), sem("dve_chain"), sem("act_chain")
        qz_ready = sem("qz_ready")
        norms = ["attn", "mix", "ffn", "mix2", "mlp2"]
        rms_ready = {n: sem(f"rms_ready_{n}") for n in norms + ["vg", "first", "last"]}
        rows = {n: sem(f"rows_{n}") for n in norms}
        turned = sem("turned")
        hT_ready = sem("hT_ready")
        wsp_turned, wspT_ready = sem("wsp_turned"), sem("wspT_ready")
        tables_turned, tables_ready = sem("tables_turned"), sem("tables_ready")
        qk_ps, qk_ready = sem("qk_ps"), sem("qk_ready")
        vug_ps, v_ready, gelu_ready = sem("vug_ps"), sem("v_ready"), sem("gelu_ready")
        vg_ready = sem("vg_ready")
        score_ps, att_ln, att_sp = sem("score_ps"), sem("att_ln"), sem("att_sp")
        att_ps, att_x, att_exp, av_done = sem("att_ps"), sem("att_x"), sem("att_exp"), sem("av_done")
        ao_ready, sgu_ps, so_ready = sem("ao_ready"), sem("sgu_ps"), sem("so_ready")
        out1_ps, x_ready = sem("out1_ps"), sem("x_ready")
        logits_ps, r_exp_in, r_exp = sem("logits_ps"), sem("r_exp_in"), sem("r_exp")
        routed_ready, rank_ps, count_ps = sem("routed_ready"), sem("rank_ps"), sem("count_ps")
        extra_ready = sem("extra_ready")
        sel_ready, gath_ps, xg_ready = sem("sel_ready"), sem("gath_ps"), sem("xg_ready")
        ct_ps, ct_ready = sem("ct_ps"), sem("ct_ready")
        gu_done, silu_ready, hid_ready = sem("gu_done"), sem("silu_ready"), sem("hid_ready")
        hidT_ps, hidT_ready, down_done = sem("hidT_ps"), sem("hidT_ready"), sem("down_done")
        y_act, y_dve, comb_ps = sem("y_act"), sem("y_dve"), sem("comb_ps")
        moe_done, comb_free = sem("moe_done"), sem("comb_free")
        x2_ready = sem("x2_ready")
        sel_made, first_ps, first_ready, slot_ranks = sem("sel_made"), sem("first_ps"), sem("first_ready"), sem("slot_ranks")
        tap_step, short_step = [sem(f"tap_step{i}") for i in range(2)], [sem(f"short_step{i}") for i in range(2)]
        w2_used = sem("w2_used")
        lru_square, lru_root, var_in, var_root = sem("lru_square"), sem("lru_root"), sem("var_in"), sem("var_root")
        z_ps, z_bank_free = sem("z_ps"), sem("z_bank_free")
        conv_a_ready, v2_ready = sem("conv_a_ready"), sem("v2_ready")
        lru_ps, lru_gates, lru_input, lru_exp = sem("lru_ps"), sem("lru_gates"), sem("lru_input"), sem("lru_exp")
        lam_ln, lam_ready, h_ready = sem("lam_ln"), sem("lam_ready"), sem("h_ready")
        short_first = sem("short_first")
        mean_ps, centred, sq_ready, var_ps, scaled, a_ready = (
            sem("mean_ps"), sem("centred"), sem("sq_ready"), sem("var_ps"), sem("scaled"), sem("a_ready"))
        y_ps, m_ready = sem("y_ps"), sem("m_ready")
        o_ps, x3_ready = sem("o_ps"), sem("x3_ready")
        f_ps, f_bank_free, f_ready = sem("f_ps"), sem("f_bank_free"), sem("f_ready")
        x4_ready = sem("x4_ready")
        fin_ready, stored = sem("fin_ready"), sem("stored")

        x_d = A["x"][0].rearrange("(a p) d -> p a d", p=P)
        out_d = out[0].rearrange("(a p) d -> p a d", p=P)

        def by_pk(w):
            return w.rearrange("(p k) n -> p k n", k=KC)

        def by_kp(w):
            return w.rearrange("(k p) n -> p k n", p=P)

        w_in1, w_out1 = by_pk(A["w_in"][0]), by_pk(A["w_out"][0])
        wg_d = A["w_gate"][0].rearrange("g e (p k) n -> (g e) p (k n)", k=KC)
        wu_d = A["w_up"][0].rearrange("g e (p k) n -> (g e) p (k n)", k=KC)
        wd_d = A["w_down"][0].rearrange("g e (k p) n -> (g e) p k n", p=P)
        w_in2 = by_pk(A["w_in_2"][0])
        wa_d, wb_d, wo_d = by_kp(A["w_a_out_2"][0]), by_kp(A["w_b_out_2"][0]), by_kp(A["w_o_2"][0])
        w1_d, w2_d = by_pk(A["w_1_2"][0]), by_kp(A["w_2_2"][0])

        def score_banks(pair):
            at = 6 * (pair % 2)
            return PS[:, at:at + 2, 0:3 * P]

        def hT_count(name, n):
            return 4 * norms.index(name) + n + 1

        def split_count(name, n):
            return 4 * split_norms.index(name) + n + 1

        def chunked(s, n):
            return slot[s][:, 0:SLOT_FLOATS // n * n].rearrange("p (k n) -> p k n", n=n)

        late_slot = [1, 3, 2, 0]
        late = [wb_d[:, :, HALF * n:HALF * (n + 1)] for n in range(4)]
        L_A, L_O, L_F = 4, 6, 8
        late += [wa_d[:, :, BLOCK * n:BLOCK * (n + 1)] for n in range(2)]
        late += [wo_d[:, :, BLOCK * n:BLOCK * (n + 1)] for n in range(2)]
        for half in range(2):
            late += [w1_d[:, :, BLOCK * n:BLOCK * (n + 1)] for n in range(4 * half, 4 * half + 4)]
            late += [w2_d[:, 4 * n:4 * n + 4, :] for n in range(4 * half, 4 * half + 4)]

        LATE_UNITS, LATE_DVE = 12, 0
        U_A, U_O = 4, 8

        def late_unit(u):
            load = u if u < U_A else L_A + (u - U_A) // 2
            raw, rest = slot[late_slot[load % 4]], ring_rest[late_slot[load % 4]][:, :]
            if u < U_A:
                views = [v[:, 0:RC * HALF].rearrange("p (k n) -> p k n", n=HALF) for v in (raw, rest)]
                return load, views[0], wb_hi[u % 3][:, :, :], views[1], (y_ps, 2) if u == 3 else None
            if u < U_O:
                hi, free = wa_hi[u - U_A], (None, (y_ps, 4), (y_ps, 6), (y_ps, KC))[u - U_A]
            else:
                hi, free = wo_hi[u - U_O], ((y_ps, KC), None, (y_ps, KC + 6), (y_ps, 2 * KC))[u - U_O]
            return load, half_block(raw, u), hi[:, :, :], half_block(rest, u), free

        def late_rest(u):
            return (late_rest_dve, 1) if u == LATE_DVE else (late_rest_pool, u + (1 if u < LATE_DVE else 0))

        def late_arrived(n):
            return late_loaded[n % 4], 16 * (n // 4 + 1)

        def late_used(n):
            if n < L_A:
                return y_ps, 2 * (n + 1)
            if n < L_O:
                return y_ps, KC + 4 * (n - L_A + 1)
            if n < L_F:
                return o_ps, 4 * (n - L_O + 1)
            half, b = (n - L_F) // 8, (n - L_F) % 8
            return (f_ps, 16 * half + 4 * (b + 1)) if b < 4 else (w2_used, 4 * half + b - 3)

        def pre_count(n):
            return 16 * (n // RING + 1)

        def in1_used(n):
            return (vug_ps, 2 * n + 2) if n < VUG_HALVES else (qk_ps, 2 * (n - VUG_HALVES) + 2)

        def rows_done(block, tt):
            return 4 * block + 3 + tt

        def vec(v):
            return v.rearrange("(p k) -> p k", k=KC)

        block = ctx.enter_context(nc.Block())

        @block.sync
        def _(sp):
            sp.dma_start(X[:, 0, :], x_d[:, 0, :]).then_inc(x_loaded, 16)
            sp.dma_start(X[:, 1, :], x_d[:, 1, :]).then_inc(x_loaded, 16)
            def small_loads():
                half = P // 2
                sp.dma_start(wsp, A["w_spatial"][0].rearrange("h t s -> t h s")).then_inc(small_loaded, 16)
                sp.dma_start(bsp[0:HEADS], A["b_spatial"][0]).then_inc(small_loaded, 16)
                sp.dma_start(sgn_g, A["sg_norm_g"].partition_broadcast(P).rearrange("p a n -> p (a n)")).then_inc(small_loaded, 16)
                sp.dma_start(gains[0:half, G_MIX, :], vec(A["sb_out_norm_g"][0])).then_inc(small_loaded, 16)
                sp.dma_start(gains[half:P, G_MIX, :], vec(A["sg_out_norm_g"][0])).then_inc(small_loaded, 16)
                sp.dma_start(gains[:, G_MIX2, :], vec(A["g_mix_2"][0])).then_inc(small_loaded, 16)
                sp.dma_start(gains[:, G_MLP2, :], vec(A["g_mlp_2"][0])).then_inc(small_loaded, 16)
                sp.dma_start(gains[:, G_FFN, :], vec(A["ffn_norm_g"][0])).then_inc(router_loaded, 16)
                sp.dma_start(w_router[:, :, 0:GROUPS], by_pk(A["w_router_group"][0])).then_inc(router_loaded, 16)
                for g in range(GROUPS):
                    at = GROUPS + g * EXPERTS_PER_GROUP
                    sp.dma_start(w_router[:, :, at:at + EXPERTS_PER_GROUP], by_pk(A["w_router_expert"][0, g])).then_inc(router_loaded, 16)
                sp.dma_start(b_router[:, 0:GROUPS], A["b_router_group"][0].partition_broadcast(P)).then_inc(router_loaded, 16)
                sp.dma_start(b_router[:, GROUPS:], A["b_router_expert"][0].rearrange("g e -> (g e)").partition_broadcast(P)).then_inc(router_loaded, 16)
                sp.dma_start(g_first[:, :], A["final_norm_g"].partition_broadcast(P)).then_inc(router_loaded, 16)
                sp.dma_start(g_last[:, :], A["g_final_2"].partition_broadcast(P)).then_inc(router_loaded, 16)

                def rows128(v):
                    return v.rearrange("(c p) -> c p", p=P)

                for to, count, name in ((V_CAB, 8, "conv_a_b_2"), (V_LNG, 8, "ln_g_2"), (V_LNB, 8, "ln_b_2"),
                                        (V_CBB, RC, "conv_b_b_2"), (V_BRA, RC, "b_rg_a_2"), (V_BRX, RC, "b_rg_x_2"),
                                        (V_LAM, RC, "lam_2")):
                    sp.dma_start(vec_raw[to:to + count], rows128(A[name][0])).then_inc(table_loaded, 16)
                sp.dma_start(vec_raw[0:ZC], rows128(A["b_in_2"][0])).then_inc(table_loaded, 16)
                taps = A["conv_a_w_2"][0].rearrange("k (c p) -> (k c) p", p=P)
                sp.dma_start(caw_raw[:, 0, :], taps[0:P]).then_inc(table_loaded, 16)
                sp.dma_start(caw_raw[0:TAPS_A * KC - P, 1, :], taps[P:]).then_inc(table_loaded, 16)
                sp.dma_start(cbw_raw[0:TAPS_B * RC], A["conv_b_w_2"][0].rearrange("k (c p) -> (k c) p", p=P)).then_inc(table_loaded, 16)

            for n in range(PRE):
                if n >= RING:
                    small_loads()
                    sp.wait_ge(*in1_used(1))
                w, b = (w_in1, IN1_ORDER[n]) if n < IN1_BLOCKS else (w_out1, n - IN1_BLOCKS)
                sp.dma_start(chunked(n % RING, BLOCK), w[:, :, b * BLOCK:(b + 1) * BLOCK]).then_inc(loaded[n % RING], 16)

            def load_expert(w, places, signals):
                for d, to, signal in zip((wg_d, wu_d), places, signals):
                    sp.dma_start(to, d[bass.ds(w, 1)].rearrange("e p n -> p (e n)")).then_inc(signal, 16)

            def load_down(w, place, signal):
                sp.dma_start(place.rearrange("p (k n) -> p k n", n=D), wd_d[bass.ds(w, 1)].rearrange("e p k n -> p (e k) n")).then_inc(signal, 16)

            first, second = ([(slot[s], loaded[s]) for s in slots] for slots in (EVEN, ODD))
            third = [(mem[:, third_at + n * SLOT_FLOATS:third_at + (n + 1) * SLOT_FLOATS], third_loaded) for n in range(3)]

            def load_gate_up(w, where):
                load_expert(w, [p for p, _ in where[0:2]], [q for _, q in where[0:2]])

            sp.wait_ge(*in1_used(3))
            sp.wait_ge(*in1_used(5))
            load_gate_up(1, first)
            sp.wait_ge(*in1_used(7))
            load_down(1, *first[2])
            sp.wait_ge(rows["mix"], 2 * TT)
            sp.wait_ge(tables_turned, 1)
            load_gate_up(2, third)
            load_down(2, *third[2])
            sp.wait_ge(out1_ps, 4)
            load_gate_up(0, second)
            sp.wait_ge(out1_ps, 8)
            load_down(0, *second[2])
            sp.wait_ge(gu_done, 1)
            load_gate_up(3, second)
            sp.wait_ge(down_done, 1)
            load_down(3, *second[2])
            sp.wait_ge(extra_ready, 1)
            with sp.Fori(2, EXPERTS // 2) as pair:
                for i, where in enumerate((first, second)):
                    w = sp.value_load(order_i[0:1, bass.ds(2 * pair + i, 1)], min_val=0, max_val=EXPERTS - 1)
                    sp.wait_ge(gu_done, 2 * pair + (i - 1))
                    load_gate_up(w, where)
                    sp.wait_ge(down_done, 2 * pair + (i - 1))
                    load_down(w, *where[2])
            def load_z(n):
                if n >= RAW:
                    sp.wait_ge(z_ps, 2 * (n - RAW + 1))
                h = IN2_ORDER[n]
                sp.dma_start(z_raw(n).rearrange("p (k n) -> p k n", n=HALF),
                             w_in2[:, :, h * HALF:(h + 1) * HALF]).then_inc(raw_loaded[n % RAW], 16)

            sp.wait_ge(down_done, EXPERTS - 1)
            for n in range(RAW):
                load_z(n)

            def extra_weights(j):
                e = sp.value_load(extra_i[0:1, 1, bass.ds(j, 1)], min_val=0, max_val=EXPERTS - 1)
                w = sp.value_load(order_i[0:1, bass.ds(e, 1)], min_val=0, max_val=EXPERTS - 1)
                again = sp.value_load(extra_i[0:1, 4, bass.ds(j, 1)], min_val=0, max_val=1)
                with sp.If(again < 1):
                    for part in range(3):
                        sp.sem_inc(extra_loaded[part], 16)
                with sp.If(again > 0):
                    sp.wait_ge(down_done, j + EXPERTS)
                    load_expert(w, [slot[s] for s in ODD[0:2]], extra_loaded[0:2])
                    load_down(w, slot[ODD[2]], extra_loaded[2])

            n_extra = sp.value_load(extra_i[0:1, 0, 0:1], min_val=0, max_val=EXTRA_MAX)
            with sp.If(n_extra > 0):
                extra_weights(0)
            with sp.If(n_extra > 1):
                with sp.Fori(1, EXTRA_MAX) as j:
                    with sp.If(j < n_extra):
                        extra_weights(j)
            for n in range(RAW, IN2_HALVES):
                load_z(n)
            for n, src in enumerate(late):
                if n < 2:
                    sp.wait_ge(z_ps, ZC - 4)
                elif n < 4:
                    sp.wait_ge(z_ps, ZC)
                else:
                    sp.wait_ge(*late_used(n - 4))
                rows_, width = src.shape[1], src.shape[2]
                dst = slot[late_slot[n % 4]][:, 0:rows_ * width].rearrange("p (k n) -> p k n", n=width)
                sp.dma_start(dst, src).then_inc(late_loaded[n % 4], 16)
            for tt in range(TT):
                sp.wait_ge(fin_ready, tt + 1)
                sp.dma_start(out_d[:, tt, :], fin[:, tt, :]).then_inc(stored, 16)
            sp.wait_ge(stored, 16 * TT)

        @block.gpsimd
        def _(pool):
            done = [0]

            def link(ins):
                done[0] += 1
                ins.then_inc(pool_chain, 1)
                pool.wait_ge(pool_chain, done[0])

            def triangle(m, inside, outside, compare, row, col, base=0):
                link(nc.gpsimd.memset(m[:, :], inside))
                nc.gpsimd.affine_select(out=m[:, :], in_=m[:, :], compare_op=compare, fill=outside, base=base,
                                        pattern=[[col, P]], channel_multiplier=row).then_inc(consts, 1)

            nc.gpsimd.memset(eps[:, :], EPS).then_inc(consts, 1)
            triangle(ident, 0.0, 1.0, ALU.not_equal, 1, -1)
            nc.gpsimd.memset(qT, 0.0).then_inc(qz_ready, 1)
            triangle(upto, 1.0, 0.0, ALU.is_ge, -1, 1)
            triangle(before, 1.0, 0.0, ALU.is_gt, -1, 1)
            triangle(maskbias, 0.0, MASKED, ALU.is_gt, -1, 1)
            triangle(tri_neg, -1.0, 0.0, ALU.is_ge, 1, -1)
            nc.gpsimd.memset(neg_ones[:, :], -1.0).then_inc(consts, 1)
            nc.gpsimd.memset(ones[:, :], 1.0).then_inc(consts, 1)
            nc.gpsimd.memset(mean_ones[:, :], 1.0 / D).then_inc(consts, 1)
            link(nc.gpsimd.iota(iota_i[:, :], pattern=[[1, SLOTS]], base=0, channel_multiplier=0))
            nc.gpsimd.tensor_copy(iota_s[:, :], iota_i[:, :]).then_inc(consts, 1)

            for n in range(4):
                raw, rest = out1_half(n)
                if n == 0:
                    pool.wait_ge(*in1_used(IN1_HALVES - 1))
                if n == 2:
                    pool.wait_ge(av_done, PAIRS)
                if n % 2 == 0:
                    w = IN1_BLOCKS + n // 2
                    pool.wait_ge(loaded[w % RING], pre_count(w))
                link(nc.gpsimd.tensor_copy(out1_hi[n][:, :, :], raw))
                nc.gpsimd.tensor_tensor(rest, raw, out1_hi[n][:, :, :].bitcast(F32), ALU.subtract).then_inc(out1_rest_ready, 1)

            def rest_half(n):
                pool.wait_ge(z_hi_ready, n + 1)
                nc.gpsimd.tensor_tensor(z_rest(n), z_raw(n), z_hi(n).bitcast(F32), ALU.subtract).then_inc(z_rest_ready, 1)

            for n in range(2):
                rest_half(n)
            pool.wait_ge(moe_done, 1)
            link(nc.gpsimd.memset(BDA[:, :, :, :], 0.0))
            link(nc.gpsimd.memset(BDX[:, :, :, :], 0.0))
            nc.gpsimd.memset(UP[:, :, 0:PAD], 0.0).then_inc(pads_ready, 1)
            for bd, w in ((BDA, A["w_rg_a_2"]), (BDX, A["w_rg_x_2"])):
                heads = w[0].rearrange("(g h) i j -> h i g j", g=RG)
                for h in range(4):
                    r0 = h * RNN_HEAD
                    while r0 < (h + 1) * RNN_HEAD:
                        chunk = r0 // P
                        r1 = min((chunk + 1) * P, (h + 1) * RNN_HEAD)
                        c0 = h * RNN_HEAD - chunk * RNN_HEAD
                        pool.dma_start(bd[r0 - chunk * P:r1 - chunk * P, :, chunk, c0:c0 + RNN_HEAD],
                                       heads[h, r0 - h * RNN_HEAD:r1 - h * RNN_HEAD]).then_inc(bd_loaded, 16)
                        r0 = r1

            for n in range(2, IN2_HALVES):
                rest_half(n)
            for g in range(RG):
                rows_ = slice(3 * g, 3 * g + 3)
                pool.wait_ge(out_hi_ready, g + 1)
                nc.gpsimd.tensor_tensor(h_rest[:, rows_, :], RB[:, rows_, :], h_hi[:, rows_, :].bitcast(F32), ALU.subtract).then_inc(h_rest_ready, 1)
            for u in range(LATE_UNITS):
                if u == LATE_DVE:
                    continue
                _, raw, hi, rest, _ = late_unit(u)
                pool.wait_ge(late_hi_ready, u + 1)
                nc.gpsimd.tensor_tensor(rest, raw, hi.bitcast(F32), ALU.subtract).then_inc(late_rest_pool, 1)

        N_TABLE = 11
        N_BD = 12
        C_EPS, C_IDENT, N_CONST = 1, 2, 10
        N_ROUTER = 10
        SQRT_SET = "sqrt_and_others"
        N_SMALL = 7

        @block.scalar
        def _(act):
            done = [0]

            def link(ins):
                done[0] += 1
                ins.then_inc(act_chain, 1)
                act.wait_ge(act_chain, done[0])

            act.dma_start(gains[:, G_ATTN, :], vec(A["attn_norm_g"][0])).then_inc(gain_loaded, 16)

            def add_squares(rows_, col, scratch):
                link(nc.scalar.activation(scratch, rows_, ACT.Square, accum_out=ss[:, col:col + 1]))

            def rms(name, col, n, width):
                nc.scalar.activation(rstd[:, col:col + n], ss[:, col:col + n], ACT.Sqrt, scale=1.0 / width,
                                     bias=eps[:, :]).then_inc(rms_ready[name], 1)

            def row_squares(name, col):
                for tt in range(TT):
                    add_squares(X[:, tt, :], col + tt, square)
                rms(name, col, TT, D)

            def split_hT(name):
                for n in range(4):
                    tt, ks = n // 2, slice(4 * (n % 2), 4 * (n % 2) + 4)
                    act.wait_ge(hT_ready, hT_count(name, n))
                    nc.scalar.activation(HT_hi[:, tt, ks, :], HT[:, ks, tt * P:(tt + 1) * P], ACT.Copy).then_inc(hT_hi_ready, 1)

            def split_in1(n):
                act.wait_ge(loaded[n // 2], 16)
                if n >= IN1_HI:
                    act.wait_ge(*in1_used(n - IN1_HI))
                nc.scalar.activation(in1_hi[n % IN1_HI][:, :, :], in1_half(n)[0], ACT.Copy).then_inc(in1_hi_ready, 1)

            def take_qk(n):
                act.wait_ge(qk_ps, n + 1)
                ps = PS[:, n % 4, 0:T]
                if n < 4:
                    nc.scalar.activation(qT[0:64, 2 * n, :], ps[0:64], ACT.Copy, scale=HEAD_DIM ** -0.5)
                    nc.scalar.activation(qT[64:P, 2 * n + 1, :], ps[64:P], ACT.Copy, scale=HEAD_DIM ** -0.5).then_inc(qk_ready, 1)
                else:
                    nc.scalar.activation(kT[:, n - 4, :], ps, ACT.Copy).then_inc(qk_ready, 1)

            def take_gelu(block, to):
                for tt in range(TT):
                    act.wait_ge(vug_ps, rows_done(block, tt))
                    nc.scalar.activation(to[:, tt, :], PS[:, 4 + 2 * block + tt, :], ACT.Gelu_apprx_tanh).then_inc(gelu_ready, 1)

            act.preload_act_table_set(SQRT_SET)
            act.wait_ge(consts, C_EPS)
            act.wait_ge(x_loaded, 16 * TT)
            row_squares("attn", 0)
            split_in1(0)
            split_hT("attn")
            split_in1(1)
            split_in1(2)
            act.wait_ge(qz_ready, 1)
            for n in range(IN1_HALVES):
                if n == 1:
                    take_gelu(0, U)
                if n == 3:
                    take_gelu(1, VG)
                if n >= VUG_HALVES:
                    take_qk(2 * (n - VUG_HALVES))
                    take_qk(2 * (n - VUG_HALVES) + 1)
                if n + IN1_HI < IN1_HALVES:
                    split_in1(n + IN1_HI)
                if n == 5:
                    act.wait_ge(gelu_ready, 4)
                    for tt in range(TT):
                        add_squares(VG[:, tt, :], 2 + tt, square[:, 0:SB])
                    rms("vg", 2, TT, SB)
            def att_log(pair):
                act.wait_ge(score_ps, pair + 1)
                if pair >= 2:
                    act.wait_ge(att_sp, pair - 1)
                e = att_e[pair % 2]
                link(nc.scalar.activation(e, score_banks(pair), ACT.Abs))
                link(nc.scalar.activation(e, e, ACT.Exp, scale=-1.0))
                nc.scalar.activation(e, e, ACT.Ln, bias=1.0).then_inc(att_ln, 1)

            def att_weights(pair):
                act.wait_ge(att_x, pair + 1)
                nc.scalar.activation(att_a[pair % 2], att_a[pair % 2], ACT.Exp).then_inc(att_exp, 1)

            act.preload_act_table_set("natural_log_exp_and_others")
            att_log(0)
            for pair in range(PAIRS):
                if pair + 1 < PAIRS:
                    att_log(pair + 1)
                att_weights(pair)
            act.preload_act_table_set(SQRT_SET)
            for half_n, rows_, ready in ((1, so, so_ready), (0, ao, ao_ready)):
                for tt in range(TT):
                    act.wait_ge(ready, tt + 1)
                    add_squares(rows_[:, tt, :], 4 + 2 * half_n + tt, square[:, 0:SB])
            rms("mix", 4, 2 * TT, SB)
            split_hT("mix")
            act.wait_ge(tables_turned, 1)
            for dst, at in ((VEC, 0), (CAW, P), (CBW, P + TAPS_A * KC)):
                n = dst.shape[1]
                nc.scalar.activation(dst[:, :], PS[:, 0, at:at + n], ACT.Copy).then_inc(tables_ready, 1)
            act.wait_ge(tables_ready, 3)
            link(nc.scalar.activation(sp8[:, 0, :], VEC[:, V_LAM:V_LAM + RC], ACT.Abs))
            link(nc.scalar.activation(sp8[:, 0, :], sp8[:, 0, :], ACT.Exp, scale=-1.0))
            nc.scalar.activation(sp8[:, 0, :], sp8[:, 0, :], ACT.Ln, bias=1.0).then_inc(lam_ln, 1)
            act.preload_act_table_set(SQRT_SET)
            act.wait_ge(x_ready, 4)
            row_squares("ffn", 8)
            act.wait_ge(r_exp_in, 1)
            nc.scalar.activation(r_a[:, :, 0:GROUPS + 1], r_a[:, :, 0:GROUPS + 1], ACT.Exp).then_inc(r_exp, 1)

            def turn_combine(pack):
                act.wait_ge(ct_ps, pack + 1)
                act.wait_ge(comb_ps, 4 * pack + 1)
                nc.scalar.activation(CT, PS[:, B_GATHER, 0:T], ACT.Copy).then_inc(ct_ready, 1)

            def gate(e, i):
                act.wait_ge(gu_done, e + 1)
                nc.scalar.activation(silu[:, i % 2, :], PS[:, B_GATE + i % 2, 0:P], ACT.Silu).then_inc(silu_ready, 1)

            def hidden_turned(e, i):
                act.wait_ge(hidT_ps, e + 1)
                nc.scalar.activation(hidT[:, i % 2, :], PS[:, B_TURN, 0:P], ACT.Copy).then_inc(hidT_ready, 1)

            def collect(e, i):
                act.wait_ge(down_done, e + 1)
                for j in range(2):
                    ins = nc.scalar.activation(Y[SLOTS * i:SLOTS * (i + 1), D_STRIP * j:D_STRIP * (j + 1)],
                                               PS[SLOTS * j:SLOTS * (j + 1), B_DOWN + i % 2, 0:D_STRIP], ACT.Copy)
                ins.then_inc(y_act, 1)

            with act.Fori(0, PACKS) as pack:
                e = PACK * pack
                turn_combine(pack)
                gate(e, 0)
                gate(e + 1, 1)
                for i in range(PACK):
                    hidden_turned(e + i, i)
                    collect(e + i, i)
                    if i + 2 < PACK:
                        gate(e + (i + 2), i + 2)
            def split_half(n):
                act.wait_ge(raw_loaded[n % RAW], 16 * (n // RAW + 1))
                if n >= HI:
                    act.wait_ge(z_ps, 2 * (n - HI + 1))
                nc.scalar.activation(z_hi(n), z_raw(n), ACT.Copy).then_inc(z_hi_ready, 1)

            split_half(0)
            split_half(1)

            def extra_tile(j):
                turn_combine(j + PACKS)
                gate(j + EXPERTS, 0)
                hidden_turned(j + EXPERTS, 0)
                collect(j + EXPERTS, 0)

            act.wait_ge(extra_ready, 1)
            n_extra = act.value_load(extra_i[0:1, 0, 0:1], min_val=0, max_val=EXTRA_MAX)
            with act.If(n_extra > 0):
                extra_tile(0)
            with act.If(n_extra > 1):
                with act.Fori(1, EXTRA_MAX) as j:
                    with act.If(j < n_extra):
                        extra_tile(j)

            act.preload_act_table_set(SQRT_SET)
            act.wait_ge(moe_done, 1)
            row_squares("first", 10)
            for tt in range(TT):
                act.wait_ge(gained, tt + 1)
                ins = nc.scalar.activation(square, HG[:, tt, :], ACT.Square, accum_out=ss[:, 12 + tt:13 + tt])
                if tt == 0:
                    link(ins)
            ins.then_inc(gained_squares, 1)
            act.wait_ge(mix2_in, 1)
            nc.scalar.activation(rstd[:, 12:14], ss[:, 12:14], ACT.Sqrt, scale=1.0 / D, bias=eps[:, :]).then_inc(rms_ready["mix2"], 1)
            split_half(2)
            split_hT("mix2")
            split_half(3)

            def take_z(n):
                for i in range(2):
                    ch = 2 * IN2_ORDER[n] + i
                    dst = UP[:, ch, PAD:] if ch < C_GA else Z[:, ch - C_GA, :]
                    func = (ACT.Identity if ch < C_GA or C_XB <= ch < C_GB else
                            ACT.Gelu_apprx_tanh if C_GB <= ch < C_SA else ACT.Sigmoid)
                    act.wait_ge(z_ps, 2 * n + i + 1)
                    nc.scalar.activation(dst, PS[:, (2 * n + i) % Z_BANKS, 0:T], func, bias=VEC[:, ch:ch + 1]).then_inc(z_bank_free, 1)

            def lru_sigmoids():
                for g in range(RG):
                    act.wait_ge(lru_ps, g + 1)
                    at = 4 * (g % 2)
                    for k in range(3):
                        n = 3 * g + k
                        nc.scalar.activation(RB[:, n, :], PS[:, at + k // 2, (k % 2) * T:(k % 2 + 1) * T], ACT.Sigmoid,
                                             bias=VEC[:, V_BRA + n:V_BRA + n + 1])
                        ins = nc.scalar.activation(IB[g][:, k, :], PS[:, at + 2 + k // 2, (k % 2) * T:(k % 2 + 1) * T], ACT.Sigmoid,
                                                   bias=VEC[:, V_BRX + n:V_BRX + n + 1])
                    ins.then_inc(lru_gates, 1)

            def lru_exponentials():
                act.wait_ge(lam_ready, 1)
                act.wait_ge(lru_gates, RG)
                for n in range(RC):
                    nc.scalar.activation(Z[:, Z_XB + n, :], RB[:, n, :], ACT.Tanh, scale=sp8[:, 2, n:n + 1])
                for n in range(RC):
                    ins = nc.scalar.activation(AB[:, n, :], RB[:, n, :], ACT.Exp, scale=sp8[:, 3, n:n + 1])
                    if n % 3 == 2:
                        ins.then_inc(lru_exp, 1)

            def short_conv_first(n):
                act.wait_ge(z_bank_free, Z_BANKS + 2 * n + 2)
                for i in range(2):
                    c = 2 * IN2_ORDER[n] + i - C_XB
                    tap = (TAPS_B - 1) * RC + c
                    nc.scalar.activation(VB[:, c, :], Z[:, Z_XB + c, :], ACT.Identity, scale=CBW[:, tap:tap + 1],
                                         bias=VEC[:, V_CBB + c:V_CBB + c + 1]).then_inc(short_first, 1)

            def lru_roots():
                for g in range(RG):
                    act.wait_ge(lru_square, g + 1)
                    th = Z[:, Z_XB + 3 * g:Z_XB + 3 * g + 3, :]
                    nc.scalar.activation(th, th, ACT.Sqrt).then_inc(lru_root, 1)

            def split_h():
                for g in range(RG):
                    rows_ = slice(3 * g, 3 * g + 3)
                    act.wait_ge(h_ready, g + 1)
                    nc.scalar.activation(h_hi[:, rows_, :], RB[:, rows_, :], ACT.Copy).then_inc(out_hi_ready, 1)

            def split_late(u):
                load, raw, hi, _, free = late_unit(u)
                act.wait_ge(*late_arrived(load))
                if free:
                    act.wait_ge(*free)
                nc.scalar.activation(hi, raw, ACT.Copy).then_inc(late_hi_ready, 1)

            for n in range(IN2_HALVES):
                if 2 * IN2_ORDER[n] == C_SB:
                    act.wait_ge(lru_input, RG)
                take_z(n)
                if n + HI < IN2_HALVES:
                    split_half(n + HI)
                if C_XB <= 2 * IN2_ORDER[n] < C_GB:
                    short_conv_first(n)
                if n == LRU_AFTER * IN2_GROUP - 1:
                    lru_sigmoids()
                    lru_exponentials()
                if n == ACT_ROOT:
                    lru_roots()
                if n == ACT_H:
                    split_h()
                if n == IN2_HALVES - 2:
                    split_late(0)
            split_late(1)
            split_late(2)
            act.wait_ge(centred, 1)
            nc.scalar.activation(Z[:, Z_GA:Z_GA + KC, :], CU, ACT.Square).then_inc(sq_ready, 1)
            split_late(3)
            act.wait_ge(var_in, 1)
            nc.scalar.activation(inv_ln, inv_ln, ACT.Sqrt).then_inc(var_root, 1)
            split_late(U_A)
            act.wait_ge(scaled, 1)
            for half in range(2):
                ks = slice(4 * half, 4 * half + 4)
                for k in range(4 * half, 4 * half + 4):
                    nc.scalar.activation(CU[:, k, :], CU[:, k, :], ACT.Silu, bias=VEC[:, V_LNB + k:V_LNB + k + 1],
                                         scale=VEC[:, V_LNG + k:V_LNG + k + 1]).then_inc(a_ready, 1)
                act.wait_ge(a_ready, 4 * half + 4)
                nc.scalar.activation(a_hi[:, ks, :], CU[:, ks, :], ACT.Copy).then_inc(out_hi_ready, 1)
            for u in range(U_A + 1, U_O + 2):
                split_late(u)

            def split_m(n):
                act.wait_ge(m_ready, n + 1)
                pair = slice(2 * n, 2 * n + 2)
                nc.scalar.activation(m_hi[:, pair, :], Z[:, Z_SA + 2 * n:Z_SA + 2 * n + 2, :], ACT.Copy).then_inc(out_hi_ready, 1)

            split_m(0)
            split_m(1)
            split_late(U_O + 2)
            split_m(2)
            split_m(3)
            split_late(U_O + 3)
            def split_mlp(n):
                act.wait_ge(*late_arrived(L_F + n))
                if n < 3:
                    act.wait_ge(y_ps, 2 * KC)
                elif n == 3:
                    act.wait_ge(o_ps, 8)
                else:
                    act.wait_ge(*late_used(L_F + n - 4))
                nc.scalar.activation(mlp_hi[n % 4][:, :], slot[late_slot[n % 4]], ACT.Copy).then_inc(mlp_hi_ready, 1)

            act.preload_act_table_set(SQRT_SET)
            split_mlp(0)
            split_mlp(1)
            for tt in range(TT):
                act.wait_ge(x3_ready, 3 + tt)
                add_squares(X[:, tt, :], 14 + tt, UP.rearrange("p a t -> p (a t)")[:, 0:D])
            rms("mlp2", 14, TT, D)
            split_hT("mlp2")
            split_mlp(2)
            split_mlp(3)
            for half_n in range(2):
                for b in range(4):
                    at = 4 * half_n + b
                    for i in range(4):
                        act.wait_ge(f_ps, 4 * at + i + 1)
                        nc.scalar.activation(FT[:, 4 * b + i, :], PS[:, 4 + i, 0:T], ACT.Relu).then_inc(f_bank_free, 1)
                    split_mlp(8 * half_n + b + 4)
                    act.wait_ge(f_squared, at + 1)
                    nc.scalar.activation(FT_hi[:, 4 * b:4 * b + 4, :], FT[:, 4 * b:4 * b + 4, :], ACT.Copy).then_inc(f_hi_ready, 1)
                if half_n == 0:
                    for b in range(4):
                        split_mlp(8 + b)
            act.preload_act_table_set(SQRT_SET)
            for tt in range(TT):
                act.wait_ge(x4_ready, 2 * tt + 2)
                add_squares(X[:, tt, :], tt, fin[:, tt, :])
            rms("last", 0, TT, D)

        @block.vector
        def _(dve):
            done = [0]

            def link(ins):
                done[0] += 1
                ins.then_inc(dve_chain, 1)
                dve.wait_ge(dve_chain, done[0])

            def inverse_rms(name, col, n):
                dve.wait_ge(rms_ready[name], 1)
                link(nc.vector.reciprocal(rstd[:, col:col + n], rstd[:, col:col + n]))

            def permuted(tt):
                return HN[:, tt, :, :].rearrange("p k q -> p q k")

            def plain(v):
                return v.rearrange("p (q k) -> p q k", k=KC)

            def normalise(name, col):
                inverse_rms(name, col, TT)
                for tt in range(TT):
                    nc.vector.tensor_scalar(permuted(tt), plain(X[:, tt, :]), rstd[:, col + tt:col + tt + 1], None,
                                            ALU.mult).then_inc(rows[name], 1)

            def apply_gain(name, g, free=None, credits=0):
                if name == "attn":
                    dve.wait_ge(gain_loaded, 16)
                if name == "mix":
                    dve.wait_ge(small_loaded, 16 * N_SMALL)
                if name == "ffn":
                    dve.wait_ge(router_loaded, 16 * N_ROUTER)
                for n in range(4):
                    tt, half = n // 2, n % 2
                    dve.wait_ge(turned, 4 * norms.index(name) + n + 1)
                    ks = slice(4 * half, 4 * half + 4)
                    ins = nc.vector.tensor_tensor(HT[:, ks, tt * P:(tt + 1) * P], PS[:, 4 + n, :].rearrange("p (k t) -> p k t", k=4),
                                                  gains[:, g, ks].unsqueeze(2).broadcast_to((P, 4, P)), ALU.mult)
                    ins.then_inc(hT_ready, 1)

            def rest_hT(name):
                for n in range(4):
                    tt, ks = n // 2, slice(4 * (n % 2), 4 * (n % 2) + 4)
                    dve.wait_ge(hT_hi_ready, split_count(name, n))
                    at = slice(tt * P, (tt + 1) * P)
                    nc.vector.tensor_tensor(HT_rest[:, ks, at], HT[:, ks, at], HT_hi[:, tt, ks, :].bitcast(F32),
                                            ALU.subtract).then_inc(hT_rest_ready, 1)

            def rest_in1(n):
                raw, rest = in1_half(n)
                dve.wait_ge(in1_hi_ready, n + 1)
                nc.vector.tensor_tensor(rest, raw, in1_hi[n % IN1_HI][:, :, :].bitcast(F32), ALU.subtract).then_inc(in1_rest_ready, 1)

            dve.wait_ge(x_loaded, 16 * TT)
            normalise("attn", 0)
            apply_gain("attn", G_ATTN)
            rest_hT("attn")
            for n in range(IN1_HALVES):
                if n == 8:
                    for tt in range(TT):
                        dve.wait_ge(vug_ps, rows_done(2, tt))
                        nc.vector.tensor_copy(V[:, tt, :], PS[:, 4 + tt, :]).then_inc(v_ready, 1)
                rest_in1(n)
            inverse_rms("vg", 2, TT)
            dve.wait_ge(small_loaded, 16 * N_SMALL)
            for tt in range(TT):
                nc.vector.scalar_tensor_tensor(VG[:, tt, :], VG[:, tt, :], rstd[:, 2 + tt:3 + tt], sgn_g, ALU.mult,
                                               ALU.mult).then_inc(vg_ready, 1)
            dve.wait_ge(consts, N_CONST)

            def by_block(v):
                return v.rearrange("p h (b q) -> p h b q", b=3)

            def att_softplus(pair):
                dve.wait_ge(att_ln, pair + 1)
                t = att_s[pair % 2]
                link(nc.vector.scalar_tensor_tensor(t, score_banks(pair), 0.0, att_e[pair % 2], ALU.max, ALU.add))
                for h in range(2):
                    diagonal = by_block(t)[:, h, 0:3:2, :]
                    ins = nc.vector.tensor_tensor(diagonal, diagonal, before[:, :].unsqueeze(1).broadcast_to((P, 2, P)), ALU.mult)
                ins.then_inc(att_sp, 1)

            def att_masked(pair):
                dve.wait_ge(att_ps, pair + 1)
                if pair >= 2:
                    dve.wait_ge(av_done, pair - 1)
                a, ps = by_block(att_a[pair % 2]), by_block(score_banks(pair))
                nc.vector.tensor_scalar(a[:, :, 1, :], ps[:, :, 1, :], 0.0, None, ALU.min)
                for h in range(2):
                    ins = nc.vector.scalar_tensor_tensor(a[:, h, 0:3:2, :], ps[:, h, 0:3:2, :], 0.0,
                                                         maskbias[:, :].unsqueeze(1).broadcast_to((P, 2, P)), ALU.min, ALU.add)
                ins.then_inc(att_x, 1)

            def spatial_weights():
                for n in range(2):
                    dve.wait_ge(wsp_turned, n + 1)
                    nc.vector.tensor_tensor(wspT[:, 4 * n:4 * n + 4, :], PS[:, 4 + n, :].rearrange("p (k t) -> p k t", k=4),
                                            upto[:, :].unsqueeze(1).broadcast_to((P, 4, P)), ALU.mult).then_inc(wspT_ready, 1)
                dve.wait_ge(wsp_turned, 3)
                nc.vector.tensor_copy(bspT, PS[:, 4, 0:HEADS]).then_inc(wspT_ready, 1)

            def gating(tt):
                dve.wait_ge(sgu_ps, tt + 1)
                link(nc.vector.tensor_tensor(so[:, tt, :].rearrange("p (h d) -> p h d", h=HEADS),
                                             PS[:, 4 + tt, :].rearrange("p (h d) -> p h d", h=HEADS),
                                             bspT.unsqueeze(2).broadcast_to((P, HEADS, HEAD_DIM)), ALU.add))
                nc.vector.tensor_tensor(so[:, tt, :], so[:, tt, :], U[:, tt, :], ALU.mult).then_inc(so_ready, 1)

            att_softplus(0)
            spatial_weights()
            att_softplus(1)
            att_masked(0)
            att_masked(1)
            att_softplus(2)
            gating(0)
            att_masked(2)
            att_softplus(3)
            gating(1)
            att_masked(3)
            dve.wait_ge(av_done, PAIRS)
            for tt in range(TT):
                nc.vector.tensor_copy(ao[:, tt, :], PS[:, 2 + tt, :]).then_inc(ao_ready, 1)
            inverse_rms("mix", 4, 2 * TT)
            for tt in range(TT):
                for half_n, src in enumerate((ao, so)):
                    nc.vector.tensor_scalar(permuted(tt)[:, 64 * half_n:64 * half_n + 64, :], plain(src[:, tt, :]),
                                            rstd[:, 4 + 2 * half_n + tt:5 + 2 * half_n + tt], None, ALU.mult).then_inc(rows["mix"], 1)
            apply_gain("mix", G_MIX)
            rest_hT("mix")
            dve.wait_ge(tables_ready, 3)
            lam = VEC[:, V_LAM:V_LAM + RC]
            link(nc.vector.tensor_scalar(sp8[:, 1, :], lam, -1.0, 0.0, ALU.mult, ALU.max))
            dve.wait_ge(lam_ln, 1)
            link(nc.vector.tensor_tensor(sp8[:, 1, :], sp8[:, 1, :], sp8[:, 0, :], ALU.add))
            nc.vector.tensor_scalar(sp8[:, 2, :], sp8[:, 1, :], LRU_C, None, ALU.mult)
            nc.vector.tensor_scalar(sp8[:, 3, :], sp8[:, 1, :], -LRU_C, None, ALU.mult).then_inc(lam_ready, 1)
            for n in range(4):
                dve.wait_ge(out1_ps, rows_done(n // 2, n % 2))
                half = slice((n // 2) * BLOCK, (n // 2 + 1) * BLOCK)
                nc.vector.tensor_tensor(X[:, n % 2, half], X[:, n % 2, half], PS[:, n, :], ALU.add).then_inc(x_ready, 1)
            dve.wait_ge(x_ready, 4)
            normalise("ffn", 8)
            apply_gain("ffn", G_FFN)

            dve.wait_ge(router_loaded, 16 * N_ROUTER)
            dve.wait_ge(logits_ps, 1)
            link(nc.vector.tensor_tensor(logit, PS[:, 0, 0:TT * 36].rearrange("p (a n) -> p a n", a=TT),
                                         b_router[:, :].unsqueeze(1).broadcast_to((P, TT, GROUPS + EXPERTS)), ALU.add))
            g_log = logit[:, :, 0:GROUPS]
            e_log = logit[:, :, GROUPS:].rearrange("p a (g e) -> p a g e", g=GROUPS)

            def over(v, n):
                return v.broadcast_to((P, TT, n))

            def first_max(values, n, top, onehot, tmp, places):
                link(nc.vector.tensor_reduce(top, values, AX_X, ALU.max))
                link(nc.vector.tensor_tensor(tmp, values, over(top, n), ALU.is_lt))
                link(nc.vector.scalar_tensor_tensor(tmp, tmp, 64.0, places, ALU.mult, ALU.add))
                link(nc.vector.tensor_reduce(place, tmp, AX_X, ALU.min))
                link(nc.vector.tensor_tensor(onehot, places, over(place, n), ALU.is_equal))

            places4 = iota_s[:, 0:GROUPS].unsqueeze(1).broadcast_to((P, TT, GROUPS))
            places8 = iota_s[:, 0:EXPERTS_PER_GROUP].unsqueeze(1).broadcast_to((P, TT, EXPERTS_PER_GROUP))
            g_hot, g_top, tmp4 = r_c[:, :, 0:4], r_c[:, :, 4:5], r_c[:, :, 8:12]
            top1, top2, place = r_c[:, :, 5:6], r_c[:, :, 6:7], r_c[:, :, 7:8]
            hot1, hot2, tmp8, e_sel, e_rest = (r_c[:, :, 16 + 8 * k:24 + 8 * k] for k in range(5))
            first_max(g_log, GROUPS, g_top, g_hot, tmp4, places4)
            link(nc.vector.tensor_tensor(r_b.rearrange("p a (g e) -> p a g e", g=GROUPS)[:, 0], e_log[:, 0],
                                         g_hot[:, 0].unsqueeze(2).broadcast_to((P, GROUPS, EXPERTS_PER_GROUP)), ALU.mult))
            link(nc.vector.tensor_tensor(r_b.rearrange("p a (g e) -> p a g e", g=GROUPS)[:, 1], e_log[:, 1],
                                         g_hot[:, 1].unsqueeze(2).broadcast_to((P, GROUPS, EXPERTS_PER_GROUP)), ALU.mult))
            link(nc.vector.tensor_reduce(e_sel, r_b.rearrange("p a (g e) -> p a e g", g=GROUPS), AX_X, ALU.add))
            first_max(e_sel, EXPERTS_PER_GROUP, top1, hot1, tmp8, places8)
            link(nc.vector.scalar_tensor_tensor(e_rest, hot1, -3e38, e_sel, ALU.mult, ALU.add))
            first_max(e_rest, EXPERTS_PER_GROUP, top2, hot2, tmp8, places8)
            link(nc.vector.tensor_tensor(r_a[:, :, 0:GROUPS], g_log, over(g_top, GROUPS), ALU.subtract))
            nc.vector.tensor_tensor(r_a[:, :, GROUPS:GROUPS + 1], top2, top1, ALU.subtract).then_inc(r_exp_in, 1)
            link(nc.vector.tensor_tensor(tmp8, hot1, hot2, ALU.add))
            for tt in range(TT):
                nc.vector.tensor_tensor(routed[:, tt, :].rearrange("p (g e) -> p g e", g=GROUPS),
                                        g_hot[:, tt].unsqueeze(2).broadcast_to((P, GROUPS, EXPERTS_PER_GROUP)),
                                        tmp8[:, tt].unsqueeze(1).broadcast_to((P, GROUPS, EXPERTS_PER_GROUP)), ALU.mult).then_inc(routed_ready, 1)
            dve.wait_ge(r_exp, 1)
            w1c, w2c = r_a[:, :, 8:9], r_a[:, :, 9:10]
            link(nc.vector.tensor_reduce(r_a[:, :, 6:7], r_a[:, :, 0:GROUPS], AX_X, ALU.add))
            link(nc.vector.tensor_scalar(r_a[:, :, 7:8], r_a[:, :, GROUPS:GROUPS + 1], 1.0, None, ALU.add))
            link(nc.vector.tensor_tensor(r_a[:, :, 6:7], r_a[:, :, 6:7], r_a[:, :, 7:8], ALU.mult))
            link(nc.vector.reciprocal(w1c, r_a[:, :, 6:7]))
            link(nc.vector.tensor_tensor(w2c, w1c, r_a[:, :, GROUPS:GROUPS + 1], ALU.mult))
            link(nc.vector.tensor_tensor(hot1, hot1, over(w1c, EXPERTS_PER_GROUP), ALU.mult))
            link(nc.vector.tensor_tensor(hot2, hot2, over(w2c, EXPERTS_PER_GROUP), ALU.mult))
            link(nc.vector.tensor_tensor(tmp8, hot1, hot2, ALU.add))
            for tt in range(TT):
                link(nc.vector.tensor_tensor(combine[:, tt, :].rearrange("p (g e) -> p g e", g=GROUPS),
                                             g_hot[:, tt].unsqueeze(2).broadcast_to((P, GROUPS, EXPERTS_PER_GROUP)),
                                             tmp8[:, tt].unsqueeze(1).broadcast_to((P, GROUPS, EXPERTS_PER_GROUP)), ALU.mult))
            dve.wait_ge(rank_ps, 1)
            ranks = PS[:, 1, 0:TT * EXPERTS].rearrange("p (a e) -> p a e", a=TT)
            link(nc.vector.scalar_tensor_tensor(rank, ranks, 1.0, routed, ALU.add, ALU.mult))
            link(nc.vector.tensor_scalar(rank, rank, -1.0, None, ALU.add))

            def select(first, e0, n_experts, w):
                rk, cb = rank[:, :, e0], combine[:, :, e0]
                for tt in range(TT):
                    one = sel[:, tt, 0:n_experts * SLOTS].rearrange("p (e s) -> p e s", e=n_experts)
                    two = selw[:, tt, 0:n_experts * SLOTS].rearrange("p (e s) -> p e s", e=n_experts)
                    link(nc.vector.tensor_tensor(one, rk[:, tt].unsqueeze(2).broadcast_to((P, n_experts, SLOTS)),
                                                 first.unsqueeze(1).broadcast_to((P, n_experts, SLOTS)), ALU.is_equal))
                    ins = nc.vector.tensor_tensor(two, one, cb[:, tt].unsqueeze(2).broadcast_to((P, n_experts, SLOTS)), ALU.mult)
                return ins

            select(iota_s[:, :], slice(0, PACK), PACK, None).then_inc(sel_ready, 1)

            def take_gathered(pack, slots=P):
                for r in range(2):
                    dve.wait_ge(gath_ps, 2 * pack + (r + 1))
                    ks = slice(4 * r, 4 * r + 4)
                    nc.vector.tensor_tensor(XG[:, ks, 0:slots], PS[:, B_GATHER, :].rearrange("p (k s) -> p k s", k=4)[:, :, 0:slots],
                                            gains[:, G_FFN, ks].unsqueeze(2).broadcast_to((P, 4, slots)), ALU.mult).then_inc(xg_ready, 1)

            take_gathered(0)
            dve.sem_inc(comb_free, 2)
            def hidden(e, i):
                dve.wait_ge(silu_ready, e + 1)
                nc.vector.tensor_tensor(hid[:, i % 2, :], silu[:, i % 2, :], PS[:, B_GATE + i % 2, P:2 * P], ALU.mult).then_inc(hid_ready, 1)

            def collect(e, i):
                dve.wait_ge(down_done, e + 1)
                for j in range(2, 4):
                    ins = nc.vector.tensor_copy(Y[SLOTS * i:SLOTS * (i + 1), D_STRIP * j:D_STRIP * (j + 1)],
                                                PS[SLOTS * j:SLOTS * (j + 1), B_DOWN + i % 2, 0:D_STRIP])
                ins.then_inc(y_dve, 1)

            def add_pack(pack):
                for n in range(4):
                    half, tt = slice((n // 2) * BLOCK, (n // 2 + 1) * BLOCK), n % 2
                    dve.wait_ge(comb_ps, 4 * pack + (n + 2))
                    nc.vector.tensor_tensor(X[:, tt, half], X[:, tt, half], PS[:, B_COMB + n % 2, :], ALU.add).then_inc(comb_free, 1)

            def select_loop(base, first, e0, n_experts):
                rk, cb = rank[:, :, e0], combine[:, :, e0]
                for tt in range(TT):
                    one = sel[:, tt, 0:n_experts * SLOTS].rearrange("p (e s) -> p e s", e=n_experts)
                    nc.vector.tensor_tensor(one, rk[:, tt].unsqueeze(2).broadcast_to((P, n_experts, SLOTS)),
                                            first.unsqueeze(1).broadcast_to((P, n_experts, SLOTS)), ALU.is_equal).then_inc(sel_made, 1)
                dve.wait_ge(sel_made, base + TT)
                for tt in range(TT):
                    one = sel[:, tt, 0:n_experts * SLOTS].rearrange("p (e s) -> p e s", e=n_experts)
                    two = selw[:, tt, 0:n_experts * SLOTS].rearrange("p (e s) -> p e s", e=n_experts)
                    ins = nc.vector.tensor_tensor(two, one, cb[:, tt].unsqueeze(2).broadcast_to((P, n_experts, SLOTS)), ALU.mult)
                ins.then_inc(sel_ready, 1)

            def plan_extra_tiles():
                dve.wait_ge(count_ps, 1)
                link(nc.vector.tensor_copy(extra_f[:, 0, :], PS[0:1, B_COMB, 0:EXPERTS]))
                place_row, over_row, last_row, order_row = iota_s[0:1, :], extra_f[:, 4, :], extra_f[:, 5, 0:1], extra_f[:, 6, :]
                link(nc.vector.tensor_scalar(over_row, extra_f[:, 0, :], float(SLOTS), None, ALU.is_gt))
                link(nc.vector.tensor_tensor(over_row, over_row, place_row, ALU.mult))
                link(nc.vector.tensor_reduce(last_row, over_row, AX_X, ALU.max))
                spare = extra_f[:, 5, 1:2]
                link(nc.vector.tensor_scalar(spare, last_row, float(PACK), float(EXPERTS), ALU.is_lt, ALU.mult))
                link(nc.vector.tensor_tensor(last_row, last_row, spare, ALU.add))
                link(nc.vector.tensor_scalar(last_row, last_row, float(EXPERTS - 1), None, ALU.min))
                hot_row, to_last = extra_f[:, 7, :], over_row
                link(nc.vector.tensor_scalar(hot_row, place_row, last_row, None, ALU.is_equal))
                link(nc.vector.tensor_scalar(to_last, place_row, -1.0, float(EXPERTS - 1), ALU.mult, ALU.add))
                link(nc.vector.tensor_tensor(to_last, to_last, hot_row, ALU.mult))
                link(nc.vector.tensor_tensor(order_row, place_row, to_last, ALU.add))
                link(nc.vector.tensor_copy(order_row[:, EXPERTS - 1:EXPERTS], last_row))
                nc.vector.tensor_copy(order_i[:, 0:EXPERTS], order_row)
                link(nc.vector.tensor_copy(order_i[:, EXPERTS:EXPERTS + 1], last_row))
                e_last = dve.value_load(order_i[0:1, EXPERTS:EXPERTS + 1], min_val=PACK, max_val=EXPERTS - 1)
                for n, v in enumerate((rank, combine)):
                    nc.vector.tensor_copy(swap[:, 2 * n], v[:, :, bass.ds(e_last, 1)])
                    nc.vector.tensor_copy(swap[:, 2 * n + 1], v[:, :, EXPERTS - 1:EXPERTS])
                nc.vector.tensor_copy(extra_f[:, 5, 2:3], extra_f[:, 0, bass.ds(e_last, 1)])
                nc.vector.tensor_copy(extra_f[:, 5, 3:4], extra_f[:, 0, EXPERTS - 1:EXPERTS]).then_inc(swapped, 1)
                dve.wait_ge(swapped, 1)
                for n, v in enumerate((rank, combine)):
                    nc.vector.tensor_copy(v[:, :, bass.ds(e_last, 1)], swap[:, 2 * n + 1]).then_inc(swapped, 1)
                nc.vector.tensor_copy(extra_f[:, 0, bass.ds(e_last, 1)], extra_f[:, 5, 3:4]).then_inc(swapped, 1)
                dve.wait_ge(swapped, 4)
                for n, v in enumerate((rank, combine)):
                    nc.vector.tensor_copy(v[:, :, EXPERTS - 1:EXPERTS], swap[:, 2 * n])
                link(nc.vector.tensor_copy(extra_f[:, 0, EXPERTS - 1:EXPERTS], extra_f[:, 5, 2:3]))
                link(nc.vector.tensor_scalar(extra_f[:, 1, :], extra_f[:, 0, :], float(SLOTS), None, ALU.is_gt))
                for k in range(2, T // SLOTS):
                    link(nc.vector.scalar_tensor_tensor(extra_f[:, 1, :], extra_f[:, 0, :], float(SLOTS * k), extra_f[:, 1, :], ALU.is_gt, ALU.add))
                link(nc.vector.memset(extra_f[:, 2, :], 1.0))
                link(nc.vector.tensor_tensor_scan(extra_f[:, 3, :], extra_f[:, 2, :], extra_f[:, 1, :], 0.0, ALU.mult, ALU.add))
                sums = extra_f[:, 3, :]
                tiles = extra_f[:, 5, 8:24]
                link(nc.vector.tensor_scalar(tiles, iota_s[0:1, 0:16], -1.0, sums[:, EXPERTS - 1:EXPERTS], ALU.mult, ALU.add))
                link(nc.vector.tensor_scalar(tiles, tiles, -1.0, None, ALU.add))
                link(nc.vector.tensor_tensor(extra_cmp[:, :, :], sums.unsqueeze(1).broadcast_to((1, 16, EXPERTS)),
                                             tiles.unsqueeze(2).broadcast_to((1, 16, EXPERTS)), ALU.is_le))
                link(nc.vector.tensor_reduce(extra_row[:, 1, :], extra_cmp[:, :, :], AX_X, ALU.add))
                link(nc.vector.tensor_tensor(extra_cmp[:, :, :], extra_cmp[:, :, :], sums.unsqueeze(1).broadcast_to((1, 16, EXPERTS)), ALU.mult))
                link(nc.vector.tensor_reduce(extra_row[:, 2, :], extra_cmp[:, :, :], AX_X, ALU.max))
                link(nc.vector.tensor_tensor(extra_row[:, 2, :], tiles, extra_row[:, 2, :], ALU.subtract))
                link(nc.vector.tensor_scalar(extra_row[:, 2, :], extra_row[:, 2, :], 1.0, float(SLOTS), ALU.add, ALU.mult))
                link(nc.vector.tensor_scalar(extra_row[:, 0, :], tiles, 0.0, sums[:, EXPERTS - 1:EXPERTS], ALU.mult, ALU.add))
                is_third, is_last = extra_f[:, 2, 0:16], extra_f[:, 2, 16:32]
                link(nc.vector.tensor_scalar(is_third, extra_row[:, 1, :], 2.0, None, ALU.is_equal))
                link(nc.vector.tensor_scalar(is_last, extra_row[:, 1, :], float(EXPERTS - 1), None, ALU.is_equal))
                link(nc.vector.tensor_copy(extra_row[:, 3, :], is_third))
                link(nc.vector.tensor_tensor(is_last, is_last, is_third, ALU.add))
                link(nc.vector.tensor_scalar(extra_row[:, 4, :], is_last, -1.0, 1.0, ALU.mult, ALU.add))
                nc.vector.tensor_copy(extra_i[:, :, :], extra_row[:, :, :]).then_inc(extra_ready, 1)

            def take_first_ranks():
                dve.wait_ge(first_ps, 1)
                nc.vector.tensor_copy(first_rank[:, :], PS[:, B_COMB + 1, 0:16]).then_inc(first_ready, 1)
                dve.wait_ge(first_ready, 1)

            def expert_pack(pack):
                e = PACK * pack
                hidden(e, 0)
                if isinstance(pack, int):
                    plan_extra_tiles()
                dve.wait_ge(gath_ps, 2 * pack + 2)
                dve.wait_ge(ct_ps, pack + 1)
                select_loop(TT * pack, iota_s[:, :], bass.ds(e + PACK, PACK), PACK)
                hidden(e + 1, 1)
                collect(e, 0)
                hidden(e + 2, 2)
                collect(e + 1, 1)
                hidden(e + 3, 3)
                collect(e + 2, 2)
                take_gathered(pack + 1)
                collect(e + 3, 3)
                if isinstance(pack, int):
                    take_first_ranks()
                add_pack(pack)

            expert_pack(0)
            with dve.Fori(1, PACKS - 1) as pack:
                expert_pack(pack)
            n_extra = dve.value_load(extra_i[0:1, 0, 0:1], min_val=0, max_val=EXTRA_MAX)

            def extra_select(j):
                e = dve.value_load(extra_i[0:1, 1, bass.ds(j, 1)], min_val=0, max_val=EXPERTS - 1)
                dve.wait_ge(gath_ps, 2 * j + 2 * PACKS)
                dve.wait_ge(ct_ps, j + PACKS)
                nc.vector.tensor_scalar(rank_iota[:, :], iota_s[:, :], first_rank[:, bass.ds(j, 1)], None, ALU.add).then_inc(slot_ranks, 1)
                dve.wait_ge(slot_ranks, j + 1)
                select_loop(TT * j + TT * (PACKS - 1), rank_iota[:, :], bass.ds(e, 1), 1)

            def extra_outputs(j):
                hidden(j + EXPERTS, 0)
                collect(j + EXPERTS, 0)
                add_pack(j + PACKS)

            dve.wait_ge(gath_ps, 2 * PACKS)
            dve.wait_ge(ct_ps, PACKS)
            link(nc.vector.memset(sel, 0.0))
            link(nc.vector.memset(selw, 0.0))
            for i in range(PACK):
                hidden(EXPERTS - PACK + i, i)
                if i == 2:
                    with dve.If(n_extra > 0):
                        take_gathered(PACKS, SLOTS)
                collect(EXPERTS - PACK + i, i)
                if i == 1:
                    with dve.If(n_extra > 0):
                        extra_select(0)
            add_pack(PACKS - 1)
            with dve.If(n_extra > 0):
                extra_outputs(0)
            with dve.If(n_extra > 1):
                with dve.Fori(1, EXTRA_MAX) as j:
                    with dve.If(j < n_extra):
                        extra_select(j)
                        take_gathered(j + PACKS, SLOTS)
                        extra_outputs(j)
            dve.wait_ge(comb_free, 4 * n_extra + (4 * PACKS + 2))
            dve.sem_inc(moe_done, 1)

            for tt in range(TT):
                nc.vector.tensor_tensor(HG[:, tt, :], X[:, tt, :], g_first[:, :], ALU.mult).then_inc(gained, 1)
            inverse_rms("first", 10, TT)
            r1, r2 = rstd[:, 10:12], rstd[:, 12:14]
            dve.wait_ge(gained_squares, 1)
            link(nc.vector.tensor_tensor(ss[:, 12:14], ss[:, 12:14], r1, ALU.mult))
            nc.vector.tensor_tensor(ss[:, 12:14], ss[:, 12:14], r1, ALU.mult).then_inc(mix2_in, 1)
            inverse_rms("mix2", 12, TT)
            link(nc.vector.tensor_tensor(r2, r2, r1, ALU.mult))
            for tt in range(TT):
                nc.vector.tensor_scalar(permuted(tt), plain(HG[:, tt, :]), rstd[:, 12 + tt:13 + tt], None, ALU.mult).then_inc(rows["mix2"], 1)
            for tt in range(TT):
                nc.vector.tensor_scalar(X[:, tt, :], HG[:, tt, :], rstd[:, 10 + tt:11 + tt], None, ALU.mult).then_inc(x2_ready, 1)
            apply_gain("mix2", G_MIX2)

            dve.sem_inc(z_bank_free, Z_BANKS)
            rest_hT("mix2")

            def conv_a(pair):
                if pair == 0:
                    dve.wait_ge(pads_ready, 1)
                dve.wait_ge(z_bank_free, Z_BANKS + 2 * (IN2_ORDER.index(pair) + 1))
                chs = slice(2 * pair, 2 * pair + 2)
                link(nc.vector.tensor_tensor(UP[:, chs, PAD:], UP[:, chs, PAD:], Z[:, Z_GA + 2 * pair:Z_GA + 2 * pair + 2, :], ALU.mult))
                for ch in range(2 * pair, 2 * pair + 2):
                    nc.vector.tensor_scalar(CU[:, ch, :], UP[:, ch, 0:T], CAW[:, ch:ch + 1], VEC[:, V_CAB + ch:V_CAB + ch + 1],
                                            ALU.mult, ALU.add).then_inc(tap_step[ch % 2], 1)
                with dve.Fori(0, PAD // TAP_ROUND) as r:
                    for j in range(TAP_ROUND):
                        for ch in range(2 * pair, 2 * pair + 2):
                            dve.wait_ge(tap_step[ch % 2], TAP_ROUND * r + (TAPS_A * pair + j + 1))
                            src = UP[:, ch, bass.ds(TAP_ROUND * r + (j + 1), T)]
                            nc.vector.scalar_tensor_tensor(CU[:, ch, :], src, CAW[:, bass.ds(TAP_ROUND * KC * r + ((j + 1) * KC + ch), 1)],
                                                           CU[:, ch, :], ALU.mult, ALU.add).then_inc(tap_step[ch % 2], 1)

            conv_a(0)
            for pair in range(RC // 2):
                dve.wait_ge(short_first, 2 * pair + 2)
                for k in range(1, TAPS_B):
                    for i in range(2):
                        n = 2 * pair + i
                        tap = (TAPS_B - 1 - k) * RC + n
                        if k > 1:
                            dve.wait_ge(short_step[i], (TAPS_B - 1) * pair + k - 1)
                        nc.vector.scalar_tensor_tensor(VB[:, n, k:T], Z[:, Z_XB + n, 0:T - k], CBW[:, tap:tap + 1], VB[:, n, k:T],
                                                       ALU.mult, ALU.add).then_inc(short_step[i], 1)
            for i in range(2):
                dve.wait_ge(short_step[i], (TAPS_B - 1) * RC // 2)
            dve.sem_inc(v2_ready, 1)
            conv_a(1)
            conv_a(2)
            for g in range(RG):
                rows_ = slice(3 * g, 3 * g + 3)
                th = Z[:, Z_XB + 3 * g:Z_XB + 3 * g + 3, :]
                dve.wait_ge(lru_gates, g + 1)
                nc.vector.tensor_tensor(VB[:, rows_, :], VB[:, rows_, :], IB[g], ALU.mult).then_inc(lru_input, 1)
                dve.wait_ge(lru_exp, g + 1)
                link(nc.vector.tensor_tensor(RB[:, rows_, :], AB[:, rows_, :], AB[:, rows_, :], ALU.mult))
                nc.vector.scalar_tensor_tensor(th, RB[:, rows_, :], 1.0, th, ALU.add, ALU.mult).then_inc(lru_square, 1)
            for g in range(RG):
                rows_ = slice(3 * g, 3 * g + 3)
                th = Z[:, Z_XB + 3 * g:Z_XB + 3 * g + 3, :]
                dve.wait_ge(lru_root, g + 1)
                link(nc.vector.memset(th[:, :, 0:1], 1.0))
                dve.wait_ge(lru_input, g + 1)
                link(nc.vector.tensor_tensor(VB[:, rows_, :], VB[:, rows_, :], th, ALU.mult))
                for n in range(3 * g, 3 * g + 3):
                    ins = nc.vector.tensor_tensor_scan(RB[:, n, :], AB[:, n, :], VB[:, n, :], 0.0, ALU.mult, ALU.add)
                link(ins)
                if g == 0:
                    dve.wait_ge(z_bank_free, Z_BANKS + 2 * (IN2_ORDER.index((C_GB + RC) // 2 - 1) + 1))
                nc.vector.tensor_tensor(RB[:, rows_, :], RB[:, rows_, :], Z[:, Z_GB + 3 * g:Z_GB + 3 * g + 3, :], ALU.mult).then_inc(h_ready, 1)
            conv_a(3)
            for i in range(2):
                dve.wait_ge(tap_step[i], TAPS_A * KC // 2)
            dve.sem_inc(conv_a_ready, 1)
            _, raw, hi, rest, _ = late_unit(LATE_DVE)
            dve.wait_ge(late_hi_ready, LATE_DVE + 1)
            nc.vector.tensor_tensor(rest, raw, hi.bitcast(F32), ALU.subtract).then_inc(late_rest_dve, 1)
            dve.wait_ge(mean_ps, 1)
            nc.vector.tensor_tensor(CU, CU, PS[:, 4, 0:T].unsqueeze(1).broadcast_to((P, KC, T)), ALU.subtract).then_inc(centred, 1)
            dve.wait_ge(var_ps, 1)
            nc.vector.tensor_scalar(inv_ln, PS[:, 5, 0:T], EPS, None, ALU.add).then_inc(var_in, 1)
            dve.wait_ge(var_root, 1)
            link(nc.vector.reciprocal(inv_ln, inv_ln))
            nc.vector.tensor_tensor(CU, CU, inv_ln.unsqueeze(1).broadcast_to((P, KC, T)), ALU.mult).then_inc(scaled, 1)
            for half in range(2):
                ks = slice(4 * half, 4 * half + 4)
                dve.wait_ge(out_hi_ready, RG + half + 1)
                nc.vector.tensor_tensor(a_rest[:, ks, :], CU[:, ks, :], a_hi[:, ks, :].bitcast(F32), ALU.subtract).then_inc(out_rest_ready, 1)
            dve.wait_ge(z_bank_free, Z_BANKS + ZC)

            def bank_pair(n):
                return PS[:, n, :].rearrange("p (c t) -> p c t", c=2)

            def rest_m(n):
                dve.wait_ge(out_hi_ready, RG + 2 + n + 1)
                pair = slice(2 * n, 2 * n + 2)
                nc.vector.tensor_tensor(m_rest[:, pair, :], Z[:, Z_SA + 2 * n:Z_SA + 2 * n + 2, :], m_hi[:, pair, :].bitcast(F32),
                                        ALU.subtract).then_inc(out_rest_ready, 1)

            for n in range(KC // 2):
                dve.wait_ge(y_ps, 2 * n + 2)
                zb = Z[:, Z_SB + 2 * n:Z_SB + 2 * n + 2, :]
                link(nc.vector.tensor_tensor(zb, zb, bank_pair(n), ALU.mult))
            for n in range(KC // 2):
                dve.wait_ge(y_ps, KC + 2 * n + 2)
                za = Z[:, Z_SA + 2 * n:Z_SA + 2 * n + 2, :]
                link(nc.vector.tensor_tensor(za, za, bank_pair(4 + n), ALU.mult))
                nc.vector.tensor_tensor(za, za, Z[:, Z_SB + 2 * n:Z_SB + 2 * n + 2, :], ALU.add).then_inc(m_ready, 1)
                if n >= 1:
                    rest_m(n - 1)
            rest_m(KC // 2 - 1)

            def rest_mlp(n):
                dve.wait_ge(mlp_hi_ready, n + 1)
                nc.vector.tensor_tensor(ring_rest[late_slot[n % 4]][:, :], slot[late_slot[n % 4]], mlp_hi[n % 4][:, :].bitcast(F32),
                                        ALU.subtract).then_inc(mlp_rest_ready, 1)

            rest_mlp(0)
            rest_mlp(1)
            for n in range(4):
                dve.wait_ge(o_ps, rows_done(n // 2, n % 2))
                half = slice((n // 2) * BLOCK, (n // 2 + 1) * BLOCK)
                nc.vector.tensor_tensor(X[:, n % 2, half], X[:, n % 2, half], PS[:, n, :], ALU.add).then_inc(x3_ready, 1)
            dve.wait_ge(x3_ready, 4)
            normalise("mlp2", 14)
            apply_gain("mlp2", G_MLP2)
            dve.wait_ge(hT_ready, hT_count("mlp2", 3))
            dve.sem_inc(f_bank_free, 4)
            rest_hT("mlp2")
            rest_mlp(2)
            rest_mlp(3)
            for half_n in range(2):
                for b in range(4):
                    at = 4 * half_n + b
                    dve.wait_ge(f_bank_free, 4 * at + 8)
                    f4 = FT[:, 4 * b:4 * b + 4, :]
                    nc.vector.tensor_tensor(f4, f4, f4, ALU.mult).then_inc(f_squared, 1)
                    rest_mlp(8 * half_n + b + 4)
                    dve.wait_ge(f_hi_ready, at + 1)
                    nc.vector.tensor_tensor(FT_rest[:, 4 * b:4 * b + 4, :], f4, FT_hi[:, 4 * b:4 * b + 4, :].bitcast(F32),
                                            ALU.subtract).then_inc(f_ready, 1)
                if half_n == 0:
                    for b in range(4):
                        rest_mlp(8 + b)
            for n in range(4):
                dve.wait_ge(w2_used, MLP_W2)
                half = slice((n % 2) * BLOCK, (n % 2 + 1) * BLOCK)
                nc.vector.tensor_copy(X[:, n // 2, half], PS[:, 2 * (n % 2) + n // 2, :]).then_inc(x4_ready, 1)
            inverse_rms("last", 0, TT)
            for tt in range(TT):
                nc.vector.scalar_tensor_tensor(fin[:, tt, :], X[:, tt, :], rstd[:, tt:tt + 1], g_last[:, :], ALU.mult, ALU.mult).then_inc(fin_ready, 1)

        @block.tensor
        def _(pe):
            def turn_rows(name):
                for n in range(4):
                    tt, half = n // 2, n % 2
                    if n % 2 == 0:
                        pe.wait_ge(rows[name], (tt + 1) * (2 if name == "mix" else 1))
                    for k in range(4):
                        ins = nc.tensor.transpose(PS[:, 4 + n, k * P:(k + 1) * P], HN[:, tt, 4 * half + k, :], ident[:, :])
                    ins.then_inc(turned, 1)

            def three_passes(dst, terms, start, stop):
                for n, (s_hi, s_rest, m_hi, m_rest) in enumerate(terms):
                    nc.tensor.matmul(dst, s_hi, m_hi, start=start and n == 0, stop=False, skip_group_check=True)
                    nc.tensor.matmul(dst, s_hi, m_rest, start=False, stop=False, skip_group_check=True)
                    ins = nc.tensor.matmul(dst, s_rest, m_hi, start=False, stop=stop and n == len(terms) - 1, skip_group_check=True)
                return ins

            def by_token_tile(v):
                return v.rearrange("p (a t) -> p a t", a=TT)

            def times_hT(dst, hi, rest, cols):
                return three_passes(by_token_tile(dst), [(hi[:, k, cols], rest[:, k, cols], HT_hi[:, :, k, :], by_token_tile(HT_rest[:, k, :]))
                                                         for k in range(KC)], True, True)

            def rows_times(tt, hi, rest):
                at = slice(tt * P, (tt + 1) * P)
                return [(HT_hi[:, tt, k, :], HT_rest[:, k, at], hi[:, k, :], rest[:, k, :]) for k in range(KC)]

            pe.wait_ge(consts, C_IDENT)
            turn_rows("attn")
            pe.wait_ge(hT_rest_ready, split_count("attn", 3))
            for n in range(VUG_HALVES):
                pe.wait_ge(in1_rest_ready, n + 1)
                for tt in range(TT):
                    if n == 4:
                        pe.wait_ge(gelu_ready, tt + 1)
                    three_passes(PS[:, 4 + (n // 2 * 2 + tt) % 4, (n % 2) * HALF:(n % 2 + 1) * HALF],
                                 rows_times(tt, in1_hi[n % IN1_HI][:, :, :], in1_half(n)[1]), True, True).then_inc(vug_ps, 1)
            for n in range(8):
                half = VUG_HALVES + n // 2
                pe.wait_ge(in1_rest_ready, half + 1)
                if n >= 4:
                    pe.wait_ge(qk_ready, n - 3)
                times_hT(PS[:, n % 4, 0:T], in1_hi[half % IN1_HI][:, :, :], in1_half(half)[1],
                         slice((n % 2) * P, (n % 2 + 1) * P)).then_inc(qk_ps, 1)

            def scores(pair):
                if pair >= 2:
                    pe.wait_ge(att_x, pair - 1)
                for h in range(2):
                    k, q, ps = kT[:, pair, :], qT[:, 2 * pair + h, :], score_banks(pair)[:, h, :]
                    nc.tensor.matmul(ps[:, 0:T], k[:, 0:P], q, start=True, stop=False, skip_group_check=True)
                    ins = nc.tensor.matmul(ps[:, T:T + P], k[:, P:T], q[:, P:T], start=False, stop=False, skip_group_check=True)
                ins.then_inc(score_ps, 1)

            def later_keys(pair):
                pe.wait_ge(att_sp, pair + 1)
                for h in range(2):
                    t, ps = att_s[pair % 2][:, h, :], score_banks(pair)[:, h, :]
                    nc.tensor.matmul(ps[:, 0:T], tri_neg[:, :], t[:, 0:T], start=False, stop=False, skip_group_check=True)
                    nc.tensor.matmul(ps[:, P:T], neg_ones[:, :], t[:, T:T + P], start=False, stop=False, skip_group_check=True)
                    ins = nc.tensor.matmul(ps[:, T:T + P], tri_neg[:, :], t[:, T:T + P], start=False, stop=True, skip_group_check=True)
                ins.then_inc(att_ps, 1)

            def weighted_values(pair):
                pe.wait_ge(att_exp, pair + 1)
                for h in range(2):
                    a, cols = att_a[pair % 2][:, h, :], slice((2 * pair + h) * HEAD_DIM, (2 * pair + h + 1) * HEAD_DIM)
                    nc.tensor.matmul(PS[:, 2, cols], a[:, 0:P], V[:, 0, cols], start=True, stop=True)
                    nc.tensor.matmul(PS[:, 3, cols], a[:, P:T], V[:, 0, cols], start=True, stop=False)
                    ins = nc.tensor.matmul(PS[:, 3, cols], a[:, T:T + P], V[:, 1, cols], start=False, stop=True)
                ins.then_inc(av_done, 1)

            def spatial_weights():
                pe.wait_ge(small_loaded, 16 * N_SMALL)
                for n in range(2):
                    for k in range(4):
                        ins = nc.tensor.transpose(PS[:, 4 + n, k * P:(k + 1) * P], wsp[:, 4 * n + k, :], ident[:, :])
                    ins.then_inc(wsp_turned, 1)
                pe.wait_ge(wspT_ready, 1)
                nc.tensor.transpose(PS[:, 4, 0:HEADS], bsp[0:HEADS], ident[0:HEADS, 0:HEADS]).then_inc(wsp_turned, 1)

            def spatial_mixing(tt):
                pe.wait_ge(wspT_ready, 3)
                pe.wait_ge(vg_ready, tt + 1)
                for h in range(HEADS):
                    cols = slice(h * HEAD_DIM, (h + 1) * HEAD_DIM)
                    ins = nc.tensor.matmul(PS[:, 4 + tt, cols], wspT[:, h, :], VG[:, tt, cols], start=True, stop=True)
                ins.then_inc(sgu_ps, 1)

            pe.wait_ge(consts, N_CONST)
            pe.wait_ge(qk_ready, 8)
            pe.wait_ge(v_ready, TT)
            pe.wait_ge(gelu_ready, 4)
            scores(0)
            scores(1)
            spatial_weights()
            later_keys(0)
            spatial_mixing(0)
            for pair in range(1, PAIRS):
                later_keys(pair)
                if pair + 1 < PAIRS:
                    scores(pair + 1)
                if pair == 1:
                    spatial_mixing(1)
                weighted_values(pair - 1)
            weighted_values(PAIRS - 1)
            pe.wait_ge(table_loaded, 16 * N_TABLE)
            at = 0
            for raw, n in ((vec_raw, P), (caw_raw[:, 0, :], P), (caw_raw[:, 1, :], TAPS_A * KC - P), (cbw_raw, TAPS_B * RC)):
                ins = nc.tensor.transpose(PS[:, 0, at:at + n], raw[0:n], ident[0:n, 0:n])
                at += n
            ins.then_inc(tables_turned, 1)
            turn_rows("mix")
            pe.wait_ge(hT_rest_ready, split_count("mix", 3))
            pe.wait_ge(tables_ready, 3)
            for n in range(4):
                pe.wait_ge(out1_rest_ready, n + 1)
                for tt in range(TT):
                    three_passes(PS[:, n // 2 * 2 + tt, (n % 2) * HALF:(n % 2 + 1) * HALF],
                                 rows_times(tt, out1_hi[n][:, :, :], out1_half(n)[1]), True, True).then_inc(out1_ps, 1)
            turn_rows("ffn")
            pe.wait_ge(hT_ready, hT_count("ffn", 3))
            pe.wait_ge(router_loaded, 16 * N_ROUTER)
            for tt in range(TT):
                at = tt * (GROUPS + EXPERTS)
                for k in range(KC):
                    ins = nc.tensor.matmul(PS[:, 0, at:at + GROUPS + EXPERTS], HT[:, k, tt * P:(tt + 1) * P], w_router[:, k, :],
                                           start=k == 0, stop=k == KC - 1)
            ins.then_inc(logits_ps, 1)
            pe.wait_ge(routed_ready, TT)
            nc.tensor.matmul(PS[:, 1, 0:EXPERTS], before[:, :], routed[:, 0, :], start=True, stop=True)
            nc.tensor.matmul(PS[:, 1, EXPERTS:2 * EXPERTS], ones[:, :], routed[:, 0, :], start=True, stop=False)
            nc.tensor.matmul(PS[:, 1, EXPERTS:2 * EXPERTS], before[:, :], routed[:, 1, :], start=False, stop=True).then_inc(rank_ps, 1)
            nc.tensor.matmul(PS[0:1, B_COMB, 0:EXPERTS], ones[:, 0:1], routed[:, 0, :], start=True, stop=False)
            nc.tensor.matmul(PS[0:1, B_COMB, 0:EXPERTS], ones[:, 0:1], routed[:, 1, :], start=False, stop=True).then_inc(count_ps, 1)

            def gather(pack):
                pe.wait_ge(sel_ready, pack + 1)
                pe.wait_ge(ct_ready, pack)
                for r in range(2):
                    pe.wait_ge(xg_ready, 2 * pack + r)
                    for k in range(4):
                        for tt in range(TT):
                            ins = nc.tensor.matmul(PS[:, B_GATHER, k * P:(k + 1) * P], HN[:, tt, 4 * r + k, :], sel[:, tt, :],
                                                   start=tt == 0, stop=tt == TT - 1)
                    ins.then_inc(gath_ps, 1)
                pe.wait_ge(xg_ready, 2 * pack + 2)
                for tt in range(TT):
                    ins = nc.tensor.transpose(PS[:, B_GATHER, tt * P:(tt + 1) * P], selw[:, tt, :], ident[:, :])
                ins.then_inc(ct_ps, 1)

            def gate_up(at, i):
                w = mem[:, at:at + 2 * SLOT_FLOATS].rearrange("p (w k n) -> p w k n", w=2, k=KC)
                for k in range(KC):
                    for j in range(STRIPS):
                        ins = nc.tensor.matmul(PS[SLOTS * j:SLOTS * (j + 1), B_GATE + i % 2, 0:2 * F_STRIP].rearrange("p (w n) -> p w n", w=2),
                                               XG[:, k, SLOTS * i:SLOTS * (i + 1)], w[:, :, k, F_STRIP * j:F_STRIP * (j + 1)],
                                               start=k == 0, stop=k == KC - 1, tile_position=(0, SLOTS * j))
                ins.then_inc(gu_done, 1)

            def turn_hidden(e, i):
                pe.wait_ge(hid_ready, e + 1)
                nc.tensor.transpose(PS[:, B_TURN, 0:P], hid[:, i % 2, :], ident[:, :]).then_inc(hidT_ps, 1)

            def down(e, at, i):
                pe.wait_ge(hidT_ready, e + 1)
                w = mem[:, at:at + SLOT_FLOATS].rearrange("p (k n) -> p k n", n=D)
                for k in range(STRIPS):
                    for j in range(STRIPS):
                        ins = nc.tensor.matmul(PS[SLOTS * j:SLOTS * (j + 1), B_DOWN + i % 2, 0:D_STRIP],
                                               hidT[:, i % 2, SLOTS * k:SLOTS * (k + 1)], w[:, k, D_STRIP * j:D_STRIP * (j + 1)],
                                               start=k == 0, stop=k == STRIPS - 1, tile_position=(0, SLOTS * j))
                ins.then_inc(down_done, 1)

            def combine_pack(pack, y_count):
                pe.wait_ge(y_act, y_count)
                pe.wait_ge(y_dve, y_count)
                pe.wait_ge(ct_ready, pack + 1)
                for n in range(4):
                    half, tt = n // 2, n % 2
                    pe.wait_ge(comb_free, 4 * pack + (n + 1))
                    nc.tensor.matmul(PS[:, B_COMB + n % 2, :], CT[:, tt * P:(tt + 1) * P], Y[:, half * BLOCK:(half + 1) * BLOCK],
                                     start=True, stop=True).then_inc(comb_ps, 1)

            def place(pack, i, part):
                if isinstance(pack, int) and pack == 0 and i < 3:
                    if i == 2:
                        return third_at + part * SLOT_FLOATS, (third_loaded, 16 * 3)
                    s = (ODD, EVEN)[i][part]
                    return s * SLOT_FLOATS, (loaded[s], 32 + 16 * (s == 0))
                s = (EVEN, ODD)[i % 2][part]
                return s * SLOT_FLOATS, (loaded[s], 32 * pack + 16 * ((i + 1) // 2 + 1 + (s == 0)))

            def expert_gate_up(pack, i):
                if i == 0:
                    pe.wait_ge(xg_ready, 2 * pack + 2)
                for part in range(2):
                    pe.wait_ge(*place(pack, i, part)[1])
                gate_up(place(pack, i, 0)[0], i)

            def expert_down(pack, i):
                turn_hidden(PACK * pack + i, i)
                at, come = place(pack, i, 2)
                pe.wait_ge(*come)
                down(PACK * pack + i, at, i)

            def residual_first():
                for n in range(4):
                    half, tt = n // 2, n % 2
                    nc.tensor.matmul(PS[:, n, :], ident[:, :], X[:, tt, half * BLOCK:(half + 1) * BLOCK], start=True, stop=False,
                                     skip_group_check=True)

            gather(0)
            pe.sem_inc(comb_ps, 1)

            def expert_pack(pack):
                expert_gate_up(pack, 0)
                for i in range(PACK):
                    if i + 1 < PACK:
                        expert_gate_up(pack, i + 1)
                    else:
                        gather(pack + 1)
                    expert_down(pack, i)
                if isinstance(pack, int):
                    first_ranks()
                combine_pack(pack, PACK * pack + PACK)

            def first_ranks():
                pe.wait_ge(extra_ready, 1)
                nc.tensor.matmul(PS[:, B_COMB + 1, 0:16], ones[0:1, :], extra_row[0:1, 2, :], start=True, stop=True).then_inc(first_ps, 1)
                pe.wait_ge(first_ready, 1)

            expert_pack(0)
            with pe.Fori(1, PACKS - 1) as pack:
                expert_pack(pack)
            pe.wait_ge(extra_ready, 1)
            n_extra = pe.value_load(extra_i[0:1, 0, 0:1], min_val=0, max_val=EXTRA_MAX)

            def in_third(j):
                return pe.value_load(extra_i[0:1, 3, bass.ds(j, 1)], min_val=0, max_val=1)

            def extra_gate_up(j):
                third = in_third(j)
                for part in range(2):
                    pe.wait_ge(extra_loaded[part], 16 * j + 16)
                pe.wait_ge(xg_ready, 2 * j + (2 * PACKS + 2))
                with pe.If(third > 0):
                    gate_up(third_at, 0)
                with pe.If(third < 1):
                    gate_up(ODD[0] * SLOT_FLOATS, 0)

            def extra_down(j):
                third = in_third(j)
                turn_hidden(j + EXPERTS, 0)
                pe.wait_ge(extra_loaded[2], 16 * j + 16)
                with pe.If(third > 0):
                    down(j + EXPERTS, third_at + 2 * SLOT_FLOATS, 0)
                with pe.If(third < 1):
                    down(j + EXPERTS, ODD[2] * SLOT_FLOATS, 0)
                combine_pack(j + PACKS, j + (EXPERTS + 1))

            expert_gate_up(PACKS - 1, 0)
            for i in range(PACK):
                if i == 2:
                    with pe.If(n_extra > 0):
                        gather(PACKS)
                if i + 1 < PACK:
                    expert_gate_up(PACKS - 1, i + 1)
                expert_down(PACKS - 1, i)
            with pe.If(n_extra > 0):
                extra_gate_up(0)
            combine_pack(PACKS - 1, EXPERTS)
            with pe.If(n_extra > 0):
                extra_down(0)
            with pe.If(n_extra > 1):
                with pe.Fori(1, EXTRA_MAX) as j:
                    with pe.If(j < n_extra):
                        gather(j + PACKS)
                        extra_gate_up(j)
                        extra_down(j)

            turn_rows("mix2")
            pe.wait_ge(hT_rest_ready, split_count("mix2", 3))

            def z_round(r, after_lru):
                for h in range(IN2_GROUP):
                    if h == IN2_GROUP // 2 and after_lru:
                        pe.wait_ge(lru_gates, RG)
                    pe.wait_ge(z_rest_ready, IN2_GROUP * r + (h + 1))
                    hi, rest = (v.rearrange("p (k n) -> p k n", n=HALF) for v in (z_hi(h), z_rest(h)))
                    for i in range(2):
                        pe.wait_ge(z_bank_free, 2 * IN2_GROUP * r + (2 * h + i + 1))
                        times_hT(PS[:, (2 * h + i) % Z_BANKS, 0:T], hi, rest, slice(i * P, (i + 1) * P)).then_inc(z_ps, 1)

            with pe.Fori(0, LRU_AFTER) as r:
                z_round(r, False)
            pe.wait_ge(bd_loaded, 16 * N_BD)
            pe.wait_ge(v2_ready, 1)
            for g in range(RG):
                if g < 2:
                    pe.wait_ge(z_bank_free, Z_BANKS * LRU_AFTER + 4 * g + 4)
                if g >= 2:
                    pe.wait_ge(lru_gates, g - 1)
                for bd, bank in ((BDA, 4 * (g % 2)), (BDX, 4 * (g % 2) + 2)):
                    for o in range(3):
                        dst = PS[:, bank + o // 2, (o % 2) * T:(o % 2 + 1) * T]
                        pieces = [(o, 32 * o, 0, P)]
                        pieces += [[(1, 0, 96, 32)], [(0, P, 0, 64), (2, 0, 64, 64)], [(1, 160, 0, 32)]][o]
                        for n, (r, c0, p0, m) in enumerate(pieces):
                            ins = nc.tensor.matmul(dst[p0:p0 + m], bd[:, g, r, c0:c0 + m], VB[:, 3 * g + r, :], start=n == 0,
                                                   stop=n == len(pieces) - 1, skip_group_check=True)
                ins.then_inc(lru_ps, 1)
            pe.wait_ge(lru_gates, RG - 1)
            with pe.Fori(LRU_AFTER, IN2_HALVES // IN2_GROUP) as r:
                z_round(r, True)
            def means():
                pe.wait_ge(conv_a_ready, 1)
                for k in range(KC):
                    ins = nc.tensor.matmul(PS[:, 4, 0:T], mean_ones[:, :], CU[:, k, :], start=k == 0, stop=k == KC - 1)
                ins.then_inc(mean_ps, 1)

            def variances():
                pe.wait_ge(sq_ready, 1)
                for k in range(KC):
                    ins = nc.tensor.matmul(PS[:, 5, 0:T], mean_ones[:, :], Z[:, Z_GA + k, :], start=k == 0, stop=k == KC - 1)
                ins.then_inc(var_ps, 1)

            pe.wait_ge(z_bank_free, Z_BANKS + ZC)
            means()
            for n in range(KC):
                if n == 0:
                    pe.wait_ge(h_rest_ready, RG)
                if n % 2 == 0:
                    pe.wait_ge(*late_rest(n // 2))
                _, _, hi, rest, _ = late_unit(n // 2)
                cols = slice((n % 2) * P, (n % 2 + 1) * P)
                ins = three_passes(PS[:, n // 2, (n % 2) * T:(n % 2 + 1) * T],
                                   [(hi[:, k, cols], rest[:, k, cols], h_hi[:, k, :], h_rest[:, k, :]) for k in range(RC)], True, True)
                ins.then_inc(y_ps, 1)
                if n == PE_VAR:
                    variances()
            for n in range(KC):
                if n % 2 == 0:
                    pe.wait_ge(*late_rest(U_A + n // 2))
                _, _, hi, rest, _ = late_unit(U_A + n // 2)
                cols = slice((n % 2) * P, (n % 2 + 1) * P)
                for k in range(KC):
                    if n == 0 and k % 4 == 0:
                        pe.wait_ge(out_rest_ready, k // 4 + 1)
                    ins = three_passes(PS[:, 4 + n // 2, (n % 2) * T:(n % 2 + 1) * T],
                                       [(hi[:, k, cols], rest[:, k, cols], a_hi[:, k, :], a_rest[:, k, :])], k == 0, k == KC - 1)
                ins.then_inc(y_ps, 1)
            for n in range(4):
                pe.wait_ge(*late_rest(U_O + n))
                _, _, hi, rest, _ = late_unit(U_O + n)
                for tt in range(TT):
                    at = slice(tt * P, (tt + 1) * P)
                    for k in range(KC):
                        if n == 0 and tt == 0 and k % 2 == 0:
                            pe.wait_ge(out_rest_ready, 2 + k // 2 + 1)
                        ins = three_passes(PS[:, n // 2 * 2 + tt, (n % 2) * HALF:(n % 2 + 1) * HALF],
                                           [(m_hi[:, k, at], m_rest[:, k, at], hi[:, k, :], rest[:, k, :])], k == 0, k == KC - 1)
                    ins.then_inc(o_ps, 1)
            turn_rows("mlp2")
            residual_first()
            pe.wait_ge(hT_rest_ready, split_count("mlp2", 3))
            with pe.Fori(0, 2) as half:
                for b in range(4):
                    pe.wait_ge(mlp_rest_ready, 8 * half + (b + 1))
                    hi, rest = (v.rearrange("p (k n) -> p k n", n=BLOCK) for v in (mlp_hi[b][:, :], ring_rest[late_slot[b]][:, :]))
                    for i in range(4):
                        pe.wait_ge(f_bank_free, 16 * half + (4 * b + i + 1))
                        times_hT(PS[:, 4 + i, 0:T], hi, rest, slice(i * P, (i + 1) * P)).then_inc(f_ps, 1)
                for b in range(4):
                    pe.wait_ge(mlp_rest_ready, 8 * half + (b + 5))
                    pe.wait_ge(f_ready, 4 * half + (b + 1))
                    hi, rest = (v.rearrange("p (k n) -> p k n", n=D) for v in (mlp_hi[b][:, :], ring_rest[late_slot[b]][:, :]))
                    for k in range(4):
                        for n in range(4):
                            h, at = slice((n // 2) * BLOCK, (n // 2 + 1) * BLOCK), slice((n % 2) * P, (n % 2 + 1) * P)
                            ins = three_passes(PS[:, n, :], [(FT_hi[:, 4 * b + k, at], FT_rest[:, 4 * b + k, at], hi[:, k, h], rest[:, k, h])],
                                               False, False)
                    ins.then_inc(w2_used, 1)


_INS = [
    "x", "attn_norm_g", "w_in", "sg_norm_g", "w_spatial", "b_spatial", "sb_out_norm_g", "sg_out_norm_g", "w_out",
    "ffn_norm_g", "w_router_group", "b_router_group", "w_router_expert", "b_router_expert", "w_gate", "w_up",
    "w_down", "final_norm_g", "g_mix_2", "w_in_2", "b_in_2", "conv_a_w_2", "conv_a_b_2", "ln_g_2", "ln_b_2",
    "w_a_out_2", "conv_b_w_2", "conv_b_b_2", "w_rg_a_2", "b_rg_a_2", "w_rg_x_2", "b_rg_x_2", "lam_2", "w_b_out_2",
    "w_o_2", "g_mlp_2", "w_1_2", "w_2_2", "g_final_2",
]


def kernel(**inputs):
    import numpy as _np
    import concourse.bacc as _bacc
    from concourse import mybir as _mybir
    from concourse.bass_utils import run_bass_kernel_spmd as _run

    nc = _bacc.Bacc("TRN2", target_bir_lowering=False, num_devices=1)
    arrays, args = {}, {}
    for name in _INS:
        a = _np.ascontiguousarray(inputs[name])
        arrays[f"in_{name}"] = a
        args[name] = nc.dram_tensor(f"in_{name}", a.shape, _mybir.dt.from_np(a.dtype), kind="ExternalInput").ap()
    out = nc.dram_tensor("out", (1, T, D), _mybir.dt.float32, kind="ExternalOutput").ap()
    build(nc, args, out)
    r = _run(nc, [arrays], core_ids=[0])
    return r.results[0]["out"]
```
